# Optimizing a Trainium2 kernel written in Bass

```python
import jax, jax.numpy as jnp
from jax import lax
import numpy as np
import math

D_MODEL = 1024
BATCH = 1
SEQ = 1024
DEPTH = 1

N_META = 16
HGRN_HEAD_V = 128
HGRN_WIDTH = D_MODEL // 2
HGRN_HEADS = HGRN_WIDTH // HGRN_HEAD_V
HGRN_EXPAND = 128
HGRN_KDIM = HGRN_HEADS * HGRN_EXPAND
CHUNK = 64
POOL_WINDOWS = (2, 4, 8, 16)
POOL_GROUPS = len(POOL_WINDOWS)
POOL_WIDTH = D_MODEL // 2
POOL_GROUP_DIM = POOL_WIDTH // POOL_GROUPS
D_FF = 2816
CONV_WIDTH = 3
EPS = 1e-6
LOG_FLOOR = 1e-30
SPLITS = (HGRN_KDIM, HGRN_KDIM, HGRN_WIDTH, HGRN_WIDTH, POOL_WIDTH, D_MODEL, D_MODEL)
IN_COLS = sum(SPLITS)


def rmsnorm(x, gain):
    xf = x.astype(jnp.float32)
    y = xf * lax.rsqrt(jnp.mean(xf * xf, axis=-1, keepdims=True) + EPS)
    return (y * gain.astype(jnp.float32)).astype(x.dtype)

def _hgrn2_chunk_step(state, xs):
    q, k, v, lf = xs
    c = q.shape[2]
    b = jnp.cumsum(lf, axis=2)
    o_inter = jnp.einsum('bhtk,bhkv->bhtv', q * jnp.exp(b), state)
    diff = b[:, :, :, None, :] - b[:, :, None, :, :]
    causal = (jnp.arange(c)[:, None] >= jnp.arange(c)[None, :])[None, None, :, :, None]
    decay = jnp.where(causal, jnp.exp(jnp.where(causal, diff, 0.0)), 0.0)
    scores = jnp.einsum('bhtk,bhtsk,bhsk->bhts', q, decay, k)
    o_intra = jnp.einsum('bhts,bhsv->bhtv', scores, v)
    b_last = b[:, :, -1, :]
    k_dec = k * jnp.exp(b_last[:, :, None, :] - b)
    new_state = jnp.exp(b_last)[..., None] * state + jnp.einsum('bhsk,bhsv->bhkv', k_dec, v)
    return new_state, o_inter + o_intra

def hgrn2(q, f_logit, i, g, lb, out_gain):
    bsz, L, _ = q.shape
    lb = lb.astype(jnp.float32)
    fl = f_logit.astype(jnp.float32)
    f = lb + (1.0 - lb) * jax.nn.sigmoid(fl)
    log_f = jnp.log(jnp.maximum(f, LOG_FLOOR))
    k = (1.0 - lb) * jax.nn.sigmoid(-fl)
    pad = CHUNK - N_META
    def prep(t, d):
        t = jnp.pad(t.astype(jnp.float32), ((0, 0), (pad, 0), (0, 0)))
        n = t.shape[1] // CHUNK
        return t.reshape(bsz, n, CHUNK, HGRN_HEADS, d).transpose(1, 0, 3, 2, 4)
    xs = (prep(q, HGRN_EXPAND), prep(k, HGRN_EXPAND), prep(i, HGRN_HEAD_V), prep(log_f, HGRN_EXPAND))
    state0 = jnp.zeros((bsz, HGRN_HEADS, HGRN_EXPAND, HGRN_HEAD_V), jnp.float32)
    _, o = lax.scan(_hgrn2_chunk_step, state0, xs)
    o = o.transpose(1, 0, 3, 2, 4).reshape(bsz, -1, HGRN_HEADS, HGRN_HEAD_V)[:, pad:]
    o = o * lax.rsqrt(jnp.mean(o * o, axis=-1, keepdims=True) + EPS)
    o = o.reshape(bsz, L, HGRN_WIDTH) * out_gain.astype(jnp.float32)
    return o * jax.nn.sigmoid(g.astype(jnp.float32))

def multiscale_pool(v, proj, scale):
    bsz, L, _ = v.shape
    vg = v.astype(jnp.float32).reshape(bsz, L, POOL_GROUPS, POOL_GROUP_DIM)
    cs0 = jnp.pad(jnp.cumsum(vg, axis=1), ((0, 0), (1, 0), (0, 0), (0, 0)))
    t1 = jnp.arange(1, L + 1)
    outs = []
    for gi, w in enumerate(POOL_WINDOWS):
        hi = cs0[:, 1:, gi]
        lo = jnp.pad(cs0[:, :L + 1 - w, gi], ((0, 0), (w - 1, 0), (0, 0)))
        cnt = jnp.minimum(t1, w).astype(jnp.float32)[None, :, None]
        outs.append((hi - lo) / cnt - vg[:, :, gi])
    pooled = jnp.stack(outs, axis=2)
    y = jnp.einsum('blgc,gcd->blgd', pooled, proj.astype(jnp.float32))
    return y.reshape(bsz, L, POOL_WIDTH) * scale.astype(jnp.float32)

def causal_dwconv(x, w, b):
    L = x.shape[1]
    xp = jnp.pad(x, ((0, 0), (CONV_WIDTH - 1, 0), (0, 0)))
    y = b
    for j in range(CONV_WIDTH):
        y = y + xp[:, j:j + L] * w[j]
    return y

def first_inputs(seed: int = 0) -> dict:
    key = jax.random.key(seed)
    ks = jax.random.split(key, 24)
    nrm = lambda k, shape, s: jax.random.normal(k, shape, jnp.float32) * s
    gain = lambda k, shape: 1.0 + nrm(k, shape, 0.05)
    return {
        "x": nrm(ks[0], (BATCH, SEQ, D_MODEL), 1.0),
        "meta_tokens": nrm(ks[1], (N_META, D_MODEL), 1.0),
        "mix_norm_pre": gain(ks[2], (DEPTH, D_MODEL)),
        "mix_norm_post": gain(ks[3], (DEPTH, D_MODEL)),
        "w_in": nrm(ks[4], (DEPTH, D_MODEL, IN_COLS), D_MODEL ** -0.5),
        "hgrn_lower_bounds": nrm(ks[5], (DEPTH, HGRN_KDIM), 0.5),
        "hgrn_out_norm": gain(ks[6], (DEPTH, HGRN_WIDTH)),
        "w_branch_hgrn": nrm(ks[7], (DEPTH, HGRN_WIDTH, D_MODEL), HGRN_WIDTH ** -0.5),
        "pool_proj": nrm(ks[8], (DEPTH, POOL_GROUPS, POOL_GROUP_DIM, POOL_GROUP_DIM), POOL_GROUP_DIM ** -0.5),
        "pool_scale": gain(ks[9], (DEPTH, POOL_WIDTH)),
        "w_branch_pool": nrm(ks[10], (DEPTH, POOL_WIDTH, D_MODEL), POOL_WIDTH ** -0.5),
        "w_out": nrm(ks[11], (DEPTH, D_MODEL, D_MODEL), D_MODEL ** -0.5),
        "ffn_norm_pre": gain(ks[12], (DEPTH, D_MODEL)),
        "ffn_norm_post": gain(ks[13], (DEPTH, D_MODEL)),
        "ffn_w_gate": nrm(ks[14], (DEPTH, D_MODEL, D_FF), D_MODEL ** -0.5),
        "ffn_w_up": nrm(ks[15], (DEPTH, D_MODEL, D_FF), D_MODEL ** -0.5),
        "ffn_conv_w": nrm(ks[16], (DEPTH, CONV_WIDTH, D_FF), CONV_WIDTH ** -0.5),
        "ffn_conv_b": nrm(ks[17], (DEPTH, D_FF), 0.02),
        "ffn_w_down": nrm(ks[18], (DEPTH, D_FF, D_MODEL), D_FF ** -0.5),
    }

def first_block(x, meta_tokens, mix_norm_pre, mix_norm_post, w_in, hgrn_lower_bounds, hgrn_out_norm,
              w_branch_hgrn, pool_proj, pool_scale, w_branch_pool, w_out, ffn_norm_pre, ffn_norm_post,
              ffn_w_gate, ffn_w_up, ffn_conv_w, ffn_conv_b, ffn_w_down):
    bsz = x.shape[0]
    meta = jnp.broadcast_to(meta_tokens[None].astype(x.dtype), (bsz, N_META, D_MODEL))
    h = jnp.concatenate([meta, x], axis=1)
    gam = jax.nn.softmax(hgrn_lower_bounds.astype(jnp.float32), axis=0)
    lbs = jnp.clip(jnp.cumsum(gam, axis=0) - gam[0], 0.0, 1.0)
    cuts = list(np.cumsum(SPLITS)[:-1])
    for l in range(DEPTH):
        u = rmsnorm(h, mix_norm_pre[l])
        proj = u @ w_in[l]
        q, f_logit, i_in, g_out, v_pool, gate_a, gate_b = jnp.split(proj, cuts, axis=-1)
        a = hgrn2(q, f_logit, i_in, g_out, lbs[l], hgrn_out_norm[l])
        p = multiscale_pool(v_pool, pool_proj[l], pool_scale[l])
        z = (jax.nn.sigmoid(gate_a.astype(jnp.float32)) * (a @ w_branch_hgrn[l])
             + jax.nn.sigmoid(gate_b.astype(jnp.float32)) * (p @ w_branch_pool[l]))
        h = h + rmsnorm(z @ w_out[l], mix_norm_post[l])
        u = rmsnorm(h, ffn_norm_pre[l])
        gt = causal_dwconv(u @ ffn_w_gate[l], ffn_conv_w[l], ffn_conv_b[l])
        y = (jax.nn.gelu(gt, approximate=True) * (u @ ffn_w_up[l])) @ ffn_w_down[l]
        h = h + rmsnorm(y, ffn_norm_post[l])
    return h[:, N_META:]


ATT_HEADS = 8
ATT_KV_HEADS = 2
ATT_HEAD_DIM = 64
ATT_GROUP = ATT_HEADS // ATT_KV_HEADS
WINDOW = 128
BLOCK = 128
ML_HEADS = 4
ML_HEAD_DIM = 128
ML_CHUNK = 64
CONV_WIDTH_2 = 4
MEM_LEN = 256
X_HEADS = 4
X_HEAD_DIM = 128
N_GROUPS = 4
EXPERTS_PER_GROUP = 8
N_EXPERTS = N_GROUPS * EXPERTS_PER_GROUP
TOP_K = 2
D_EXPERT = 512
MOE_BLOCK = 128

ATT_Q = ATT_HEADS * ATT_HEAD_DIM
ATT_KV = ATT_KV_HEADS * ATT_HEAD_DIM
ML_W = ML_HEADS * ML_HEAD_DIM
MIX_WIDTH = ATT_Q + ML_W
IN_SPLITS = [ATT_Q, ATT_KV, ATT_KV, 2 * ML_W, ML_W, ML_W, 2 * ML_HEADS]
IN_COLS_2 = sum(IN_SPLITS)
IN_OFFSETS = [int(v) for v in np.cumsum(IN_SPLITS)[:-1]]


def rms_norm(x, g):
    xf = x.astype(jnp.float32)
    y = xf * lax.rsqrt(jnp.mean(xf * xf, axis=-1, keepdims=True) + EPS)
    return (y * g.astype(jnp.float32)).astype(x.dtype)

def alibi_slopes(n):
    return jnp.exp2(-8.0 * jnp.arange(1, n + 1, dtype=jnp.float32) / n)

def causal_depthwise_conv(x, w, b):
    c = x.shape[-1]
    y = lax.conv_general_dilated(x, w[:, None, :], window_strides=(1,),
                                 padding=[(CONV_WIDTH_2 - 1, 0)],
                                 dimension_numbers=('NWC', 'WIO', 'NWC'),
                                 feature_group_count=c)
    return y + b

def sliding_window_gqa(q, k, v, sinks):
    bsz, s = q.shape[0], q.shape[1]
    nb = s // BLOCK
    qb = q.reshape(bsz, nb, BLOCK, ATT_KV_HEADS, ATT_GROUP, ATT_HEAD_DIM)

    def with_prev(t):
        t = t.reshape(bsz, nb, BLOCK, ATT_KV_HEADS, ATT_HEAD_DIM)
        prev = jnp.pad(t[:, :-1], ((0, 0), (1, 0), (0, 0), (0, 0), (0, 0)))
        return jnp.concatenate([prev, t], axis=2)

    kk, vv = with_prev(k), with_prev(v)
    scores = jnp.einsum('bnqkgd,bnskd->bkgnqs', qb, kk).astype(jnp.float32)
    scores = scores * (1.0 / math.sqrt(ATT_HEAD_DIM))
    dist = (jnp.arange(BLOCK)[:, None] + BLOCK) - jnp.arange(2 * BLOCK)[None, :]
    in_band = (dist >= 0) & (dist < WINDOW)
    pad_key = (jnp.arange(nb)[:, None, None] == 0) & (jnp.arange(2 * BLOCK)[None, None, :] < BLOCK)
    valid = in_band[None] & ~pad_key
    slopes = alibi_slopes(ATT_HEADS).reshape(ATT_KV_HEADS, ATT_GROUP)[:, :, None, None, None]
    logits = scores - slopes * dist.astype(jnp.float32)
    logits = jnp.where(valid, logits, -jnp.inf)
    sink = sinks.astype(jnp.float32).reshape(ATT_KV_HEADS, ATT_GROUP)[:, :, None, None, None]
    mx = jnp.maximum(logits.max(axis=-1, keepdims=True), sink)
    e = jnp.exp(logits - mx)
    p = e / (e.sum(axis=-1, keepdims=True) + jnp.exp(sink - mx))
    out = jnp.einsum('bkgnqs,bnskd->bnqkgd', p.astype(v.dtype), vv)
    return out.reshape(bsz, s, ATT_Q)

def mlstm_chunk_step(carry, inp):
    c_st, n_st, m_st = carry
    q, k, v, ig, lf = inp
    L = q.shape[2]
    b = jnp.cumsum(lf, axis=-1)
    causal = jnp.tril(jnp.ones((L, L), dtype=bool))
    log_d = jnp.where(causal, b[..., :, None] - b[..., None, :] + ig[..., None, :], -jnp.inf)
    m_inter = b + m_st[..., None]
    m_t = jnp.maximum(m_inter, log_d.max(axis=-1))
    s = jnp.einsum('bhtd,bhsd->bhts', q, k) * jnp.exp(log_d - m_t[..., None])
    a_inter = jnp.exp(m_inter - m_t)
    num = jnp.einsum('bhts,bhsd->bhtd', s, v) + a_inter[..., None] * jnp.einsum('bhtk,bhkv->bhtv', q, c_st)
    den = s.sum(axis=-1) + a_inter * jnp.einsum('bhtk,bhk->bht', q, n_st)
    h = num / jnp.maximum(jnp.abs(den), jnp.exp(-m_t))[..., None]
    b_last = b[..., -1]
    log_w = b_last[..., None] - b + ig
    m_new = jnp.maximum(b_last + m_st, log_w.max(axis=-1))
    w = jnp.exp(log_w - m_new[..., None])
    decay = jnp.exp(b_last + m_st - m_new)
    c_new = decay[..., None, None] * c_st + jnp.einsum('bhsk,bhsv->bhkv', k * w[..., None], v)
    n_new = decay[..., None] * n_st + jnp.einsum('bhs,bhsk->bhk', w, k)
    return (c_new, n_new, m_new), h

def mlstm(q, k, v, i_pre, f_pre):
    bsz, s, nh, dh = q.shape
    nc = s // ML_CHUNK
    f32 = jnp.float32
    def chunks(t):
        return t.astype(f32).reshape(bsz, nc, ML_CHUNK, nh, dh).transpose(1, 0, 3, 2, 4)
    def gchunks(t):
        return t.reshape(bsz, nc, ML_CHUNK, nh).transpose(1, 0, 3, 2)
    qc = chunks(q)
    kc = chunks(k) * (1.0 / math.sqrt(dh))
    vc = chunks(v)
    igc = gchunks(i_pre.astype(f32))
    lfc = gchunks(jax.nn.log_sigmoid(f_pre.astype(f32)))
    init = (jnp.zeros((bsz, nh, dh, dh), f32), jnp.zeros((bsz, nh, dh), f32), jnp.zeros((bsz, nh), f32))
    _, hs = lax.scan(mlstm_chunk_step, init, (qc, kc, vc, igc, lfc))
    return hs.transpose(1, 0, 3, 2, 4).reshape(bsz, s, nh, dh)

def memory_cross_attention(xn, memn, w_cq, w_ckv, w_co):
    bsz, s, _ = xn.shape
    q = (xn @ w_cq).reshape(bsz, s, X_HEADS, X_HEAD_DIM)
    kv = (memn @ w_ckv).reshape(bsz, memn.shape[1], 2, X_HEADS, X_HEAD_DIM)
    k, v = kv[:, :, 0], kv[:, :, 1]
    sc = jnp.einsum('bshd,bmhd->bhsm', q, k).astype(jnp.float32) * (1.0 / math.sqrt(X_HEAD_DIM))
    p = jax.nn.softmax(sc, axis=-1)
    o = jnp.einsum('bhsm,bmhd->bshd', p.astype(v.dtype), v).reshape(bsz, s, X_HEADS * X_HEAD_DIM)
    return o @ w_co

def hierarchical_moe(xn, w_rg, b_rg, w_re, b_re, w_g, w_u, w_d):
    bsz, s, d = xn.shape
    t = bsz * s
    xt = xn.reshape(t, d)
    g_logits = (xt @ w_rg).astype(jnp.float32) + b_rg.astype(jnp.float32)
    g_prob = jax.nn.softmax(g_logits, axis=-1)
    g_sel = jnp.argmax(g_logits, axis=-1)
    g_w = jnp.take_along_axis(g_prob, g_sel[:, None], axis=-1)
    e_logits = ((xt @ w_re).astype(jnp.float32) + b_re.astype(jnp.float32)).reshape(t, N_GROUPS, EXPERTS_PER_GROUP)
    e_in = jnp.take_along_axis(e_logits, g_sel[:, None, None], axis=1)[:, 0]
    top_v, top_i = lax.top_k(e_in, TOP_K)
    top_p = jax.nn.softmax(top_v, axis=-1) * g_w
    expert_idx = (g_sel[:, None] * EXPERTS_PER_GROUP + top_i).reshape(-1)
    gates = top_p.reshape(-1)
    n_assign = t * TOP_K
    token_idx = jnp.arange(n_assign) // TOP_K
    order = jnp.argsort(expert_idx)
    sorted_e = expert_idx[order]
    counts = jnp.bincount(expert_idx, length=N_EXPERTS)
    padded = (counts + MOE_BLOCK - 1) // MOE_BLOCK * MOE_BLOCK
    pad_end = jnp.cumsum(padded)
    pad_start = pad_end - padded
    start = jnp.cumsum(counts) - counts
    dest = pad_start[sorted_e] + (jnp.arange(n_assign) - start[sorted_e])
    n_blocks = -(-n_assign // MOE_BLOCK) + N_EXPERTS
    x_pad = jnp.zeros((n_blocks * MOE_BLOCK, d), xt.dtype).at[dest].set(xt[token_idx[order]])
    block_e = jnp.minimum(jnp.searchsorted(pad_end, jnp.arange(n_blocks) * MOE_BLOCK, side='right'), N_EXPERTS - 1)

    def expert_block(args):
        xb, e = args
        hb = jax.nn.silu(xb @ w_g[e]) * (xb @ w_u[e])
        return hb @ w_d[e]

    y_pad = lax.map(expert_block, (x_pad.reshape(n_blocks, MOE_BLOCK, d), block_e)).reshape(-1, d)
    y = y_pad[dest] * gates[order][:, None].astype(y_pad.dtype)
    out = jnp.zeros((t, d), xt.dtype).at[token_idx[order]].add(y)
    return out.reshape(bsz, s, d)

def second_inputs(seed: int = 0) -> dict:
    key = jax.random.key(seed)
    ks = iter(jax.random.split(key, 40))
    f32 = jnp.float32

    def nrm(shape, scale):
        return jax.random.normal(next(ks), shape, f32) * scale

    def gain(shape):
        return 1.0 + nrm(shape, 0.02)

    L = DEPTH
    x = nrm((BATCH, SEQ, D_MODEL), 1.0)
    mem = nrm((BATCH, MEM_LEN, D_MODEL), 1.0)
    b_i = nrm((L, ML_HEADS), 0.1)
    b_f = jnp.linspace(3.0, 6.0, ML_HEADS, dtype=f32)[None, :] + nrm((L, ML_HEADS), 0.01)
    return {
        'x': x,
        'mem': mem,
        'norm_mix': gain((L, D_MODEL)),
        'w_in': nrm((L, D_MODEL, IN_COLS_2), D_MODEL ** -0.5),
        'b_gates': jnp.concatenate([b_i, b_f], axis=-1),
        'conv_w': nrm((L, CONV_WIDTH_2, 2 * ML_W), CONV_WIDTH_2 ** -0.5),
        'conv_b': nrm((L, 2 * ML_W), 0.01),
        'att_sinks': nrm((L, ATT_HEADS), 0.5),
        'norm_att_out': gain((L, ATT_Q)),
        'norm_ml_out': gain((L, ML_W)),
        'w_out': nrm((L, MIX_WIDTH, D_MODEL), MIX_WIDTH ** -0.5),
        'norm_cross': gain((L, D_MODEL)),
        'norm_mem': gain((L, D_MODEL)),
        'w_cq': nrm((L, D_MODEL, X_HEADS * X_HEAD_DIM), D_MODEL ** -0.5),
        'w_ckv': nrm((L, D_MODEL, 2 * X_HEADS * X_HEAD_DIM), D_MODEL ** -0.5),
        'w_co': nrm((L, X_HEADS * X_HEAD_DIM, D_MODEL), (X_HEADS * X_HEAD_DIM) ** -0.5),
        'norm_ffn': gain((L, D_MODEL)),
        'w_router_group': nrm((L, D_MODEL, N_GROUPS), D_MODEL ** -0.5),
        'b_router_group': nrm((L, N_GROUPS), 0.01),
        'w_router_expert': nrm((L, D_MODEL, N_EXPERTS), D_MODEL ** -0.5),
        'b_router_expert': nrm((L, N_EXPERTS), 0.01),
        'w_e_gate': nrm((L, N_EXPERTS, D_MODEL, D_EXPERT), D_MODEL ** -0.5),
        'w_e_up': nrm((L, N_EXPERTS, D_MODEL, D_EXPERT), D_MODEL ** -0.5),
        'w_e_down': nrm((L, N_EXPERTS, D_EXPERT, D_MODEL), D_EXPERT ** -0.5),
        'norm_final': gain((D_MODEL,)),
    }

def second_block(x, mem, norm_mix, w_in, b_gates, conv_w, conv_b, att_sinks, norm_att_out,
              norm_ml_out, w_out, norm_cross, norm_mem, w_cq, w_ckv, w_co, norm_ffn,
              w_router_group, b_router_group, w_router_expert, b_router_expert,
              w_e_gate, w_e_up, w_e_down, norm_final):
    bsz, s, _ = x.shape
    for l in range(DEPTH):
        h = rms_norm(x, norm_mix[l])
        proj = h @ w_in[l]
        q_a, k_a, v_a, qk_m, v_m, o_m, g_m = jnp.split(proj, IN_OFFSETS, axis=-1)
        att = sliding_window_gqa(q_a.reshape(bsz, s, ATT_HEADS, ATT_HEAD_DIM),
                                 k_a.reshape(bsz, s, ATT_KV_HEADS, ATT_HEAD_DIM),
                                 v_a.reshape(bsz, s, ATT_KV_HEADS, ATT_HEAD_DIM),
                                 att_sinks[l])
        att = rms_norm(att, norm_att_out[l])
        qk_m = jax.nn.silu(causal_depthwise_conv(qk_m, conv_w[l], conv_b[l]))
        q_m, k_m = jnp.split(qk_m, 2, axis=-1)
        g_m = g_m + b_gates[l]
        i_pre, f_pre = g_m[..., :ML_HEADS], g_m[..., ML_HEADS:]
        hm = mlstm(q_m.reshape(bsz, s, ML_HEADS, ML_HEAD_DIM),
                   k_m.reshape(bsz, s, ML_HEADS, ML_HEAD_DIM),
                   v_m.reshape(bsz, s, ML_HEADS, ML_HEAD_DIM), i_pre, f_pre)
        hm = jax.nn.sigmoid(o_m.astype(jnp.float32)).reshape(bsz, s, ML_HEADS, ML_HEAD_DIM) * hm
        hm = rms_norm(hm.astype(x.dtype), norm_ml_out[l].reshape(ML_HEADS, ML_HEAD_DIM)).reshape(bsz, s, ML_W)
        x = x + jnp.concatenate([att, hm], axis=-1) @ w_out[l]
        x = x + memory_cross_attention(rms_norm(x, norm_cross[l]), rms_norm(mem, norm_mem[l]),
                                       w_cq[l], w_ckv[l], w_co[l])
        x = x + hierarchical_moe(rms_norm(x, norm_ffn[l]), w_router_group[l], b_router_group[l],
                                 w_router_expert[l], b_router_expert[l],
                                 w_e_gate[l], w_e_up[l], w_e_down[l])
    return rms_norm(x, norm_final)


def setup_inputs(seed=0):
    out = dict(first_inputs(seed))
    for name, value in second_inputs(seed + 1).items():
        if name != "x":
            out[name + "_2"] = value
    return out


def reference(
    x, meta_tokens, mix_norm_pre, mix_norm_post, w_in, hgrn_lower_bounds, hgrn_out_norm,
    w_branch_hgrn, pool_proj, pool_scale, w_branch_pool, w_out, ffn_norm_pre, ffn_norm_post,
    ffn_w_gate, ffn_w_up, ffn_conv_w, ffn_conv_b, ffn_w_down, mem_2, norm_mix_2, w_in_2,
    b_gates_2, conv_w_2, conv_b_2, att_sinks_2, norm_att_out_2, norm_ml_out_2, w_out_2,
    norm_cross_2, norm_mem_2, w_cq_2, w_ckv_2, w_co_2, norm_ffn_2, w_router_group_2,
    b_router_group_2, w_router_expert_2, b_router_expert_2, w_e_gate_2, w_e_up_2, w_e_down_2,
    norm_final_2,
):
    x = first_block(
        x, meta_tokens, mix_norm_pre, mix_norm_post, w_in, hgrn_lower_bounds, hgrn_out_norm,
        w_branch_hgrn, pool_proj, pool_scale, w_branch_pool, w_out, ffn_norm_pre, ffn_norm_post,
        ffn_w_gate, ffn_w_up, ffn_conv_w, ffn_conv_b, ffn_w_down,
    )
    return second_block(
        x, mem_2, norm_mix_2, w_in_2, b_gates_2, conv_w_2, conv_b_2, att_sinks_2,
        norm_att_out_2, norm_ml_out_2, w_out_2, norm_cross_2, norm_mem_2, w_cq_2, w_ckv_2,
        w_co_2, norm_ffn_2, w_router_group_2, b_router_group_2, w_router_expert_2,
        b_router_expert_2, w_e_gate_2, w_e_up_2, w_e_down_2, norm_final_2,
    )


_drawn_inputs = setup_inputs


def setup_inputs(seed=0):
    import zlib

    import numpy as np

    out = dict(_drawn_inputs(seed))
    spreads = {}
    factors = {'ffn_conv_b': 3.187,
     'conv_b_2': 7.349,
     'att_sinks_2': 3.051,
     'norm_att_out_2': 5.505,
     'norm_ml_out_2': 5.01,
     'norm_cross_2': 8.0,
     'norm_mem_2': 8.0,
     'norm_ffn_2': 4.099,
     'b_router_group_2': 5.819,
     'b_router_expert_2': 6.589,
     'norm_final_2': 2.815}
    for name, (base, spread) in spreads.items():
        noise = np.random.default_rng([zlib.crc32(name.encode()), seed]).standard_normal(out[name].shape)
        drawn = base * np.exp(spread * noise) if base else spread * noise
        out[name] = __import__('jax').numpy.asarray(drawn.astype(out[name].dtype))
    for name, factor in factors.items():
        out[name] = (out[name] * factor).astype(out[name].dtype)
    return out
```

```python
from contextlib import ExitStack

import concourse.bass as bass
from concourse import mybir

F32 = mybir.dt.float32
F32R = mybir.dt.float32r
I32 = mybir.dt.int32
U32 = mybir.dt.uint32
ALU = mybir.AluOpType
ACT = mybir.ActivationFunctionType
AX = mybir.AxisListType
ds = bass.ds

P = 128
D = 1024
KD = D // P
SEQ = 1024
META = 16
HEAD = P - META
WIDE = SEQ + P
CHUNKS = WIDE // P
HALF = 4
TAPS = 3
LIVE = SEQ + TAPS - 1
FIRST = WIDE - LIVE
DFF = 2816
KF = DFF // P
EPS = 1e-6
LEVELS = 7
BANK = 512
REAL = ((HEAD, 352), (464, 344), (808, 344))
FULL = ((0, 384), (384, 384), (768, 384))
LIVES = ((0, 342), (342, 342), (684, 342))
SEQS = ((0, 512), (512, 512))

NEG = -1e30
LN2 = 0.6931471805599453

QH, DH = 8, 64
WIN = 128
NB = SEQ // P
ML_H = 4
MEM = 256
NE, NG, EPG = 32, 4, 8
DE = 512
KE = DE // P
MAXB = 2 * SEQ // P + NE
PAIRS = 63
ROUTER = NG + NE


def sems(ctx, nc, stage, names):
    return [nc.alloc_semaphore(name=f"{stage}_{n}") for n in names.split()]


def free(n):
    return n + 1


def ready(n):
    return n + 3


def buffer(ctx, nc, name, shape, dt=F32, side="left"):
    return ctx.enter_context(nc.sbuf_tensor(name, shape, dt, side=side))


VECS = (("mix_pre", "mix_norm_pre", 8), ("mix_post", "mix_norm_post", 8), ("ffn_pre", "ffn_norm_pre", 8),
        ("ffn_post", "ffn_norm_post", 8), ("lb", "hgrn_lower_bounds", 4), ("out_norm", "hgrn_out_norm", 4),
        ("pool_scale", "pool_scale", 4), ("conv_w", "ffn_conv_w", 66),
        ("conv_b", "ffn_conv_b", 22), ("norm_mix2", "norm_mix_2", 8), ("conv_w2", "conv_w_2", 32),
        ("conv_b2", "conv_b_2", 8), ("norm_ml", "norm_ml_out_2", 4), ("norm_cross", "norm_cross_2", 8),
        ("norm_mem", "norm_mem_2", 8), ("norm_ffn2", "norm_ffn_2", 8), ("norm_att", "norm_att_out_2", 4))


def vec_columns():
    at, out = 0, {}
    for name, _, n in VECS:
        if at < P < at + n:
            at = P
        out[name] = at
        at += n
    assert at <= 2 * P
    return out


VEC = vec_columns()


def stage_constants(nc, ctx, A, K, bank):
    rows_in, rows_zero, made, turned, kept = sems(ctx, nc, "c", "rows_in rows_zero made turned kept")
    ident, ones, vec, level, causal, sums_d = (K[n] for n in ("ident", "ones", "vec", "level", "causal", "reset"))
    lower = K["lower"]
    with ExitStack() as inner:
        rows = buffer(inner, nc, "vec_rows", [P, 2, P])
        block = inner.enter_context(nc.Block())

        @block.sync
        def _(sp):
            sp.wait_ge(rows_zero, 1)
            for name, source, n in VECS:
                a = A[source]
                v = a.rearrange("o (k p) -> (o k) p", p=P) if len(a.shape) == 2 else a.rearrange("o t (k p) -> (o t k) p", p=P)
                c = VEC[name]
                sp.dma_start(rows[c % P:c % P + n, c // P, :], v).then_inc(rows_in, 16)
            sp.wait_ge(rows_in, 16 * len(VECS))

        @block.gpsimd
        def _(pool):
            pool.memset(rows[:, :, :], 0.0).then_inc(rows_zero, 1)
            pool.memset(ones[:, :], 1.0).then_inc(made, 1)
            pool.memset(ident[:, :], 0.0).then_inc(made, 1)
            pool.memset(sums_d[:, :], 1.0).then_inc(made, 1)
            pool.memset(causal[:, :], 0.0).then_inc(made, 1)
            pool.memset(lower[:, :], 1.0).then_inc(made, 1)
            pool.wait_ge(made, 5)
            pool.affine_select(ident[:, :], ident[:, :], [[-1, P]], ALU.not_equal, 1.0, base=0, channel_multiplier=1).then_inc(made, 1)
            v = sums_d[:, :].rearrange("p (c t) -> p c t", t=P)
            pool.affine_select(v, v, [[0, HALF], [1, P]], ALU.not_equal, 0.0, base=0, channel_multiplier=0).then_inc(made, 1)
            pool.affine_select(causal[:, :], causal[:, :], [[1, P]], ALU.is_ge, NEG, base=0, channel_multiplier=-1).then_inc(made, 1)
            pool.affine_select(lower[:, :], lower[:, :], [[1, P]], ALU.is_gt, 0.0, base=0, channel_multiplier=-1).then_inc(made, 1)
            pool.wait_ge(made, 9)
            n = 9
            for l in range(LEVELS + 1):
                m = level[:, l, :]
                pool.memset(m, 1).then_inc(made, 1)
                n += 1
                pool.wait_ge(made, n)
                if l == LEVELS:
                    pool.affine_select(m, m, [[1, P]], ALU.is_equal, 0.0, base=0, channel_multiplier=-1).then_inc(made, 1)
                    n += 1
                    continue
                h = 1 << l
                blocks = P // (2 * h)
                v = m.rearrange("p (b u t) -> p b u t", u=2, t=h)
                for steps, base, sign in (([[0, blocks], [1, 2], [0, h]], -1, 0),
                                          ([[-2 * h, blocks], [0, 2], [0, h]], 0, 1),
                                          ([[2 * h, blocks], [0, 2], [0, h]], h - 1, -1)):
                    pool.affine_select(v, v, steps, ALU.is_ge, 0.0, base=base, channel_multiplier=sign).then_inc(made, 1)
                    n += 1
                    pool.wait_ge(made, n)

        @block.tensor
        def _(pe):
            pe.wait_ge(rows_in, 16 * len(VECS))
            pe.wait_ge(made, 6)
            for j in range(2):
                pe.transpose(bank[0][:, j * P:(j + 1) * P], rows[:, j, :], ident[:, :]).then_inc(turned, 1)

        @block.vector
        def _(dve):
            dve.memset(K["eps"][:, :], EPS)
            dve.wait_ge(turned, 2)
            dve.tensor_copy(vec[:, :], bank[0][:, 0:2 * P]).then_inc(kept, 1)


def product(pe, out, w, x, c, n):
    (wh, wl), (xh, xl) = w, x
    tiles = wh.shape[1]
    for t in range(tiles):
        pe.matmul(out, wh[:, t, :], xh[:, t, c:c + n], start=t == 0, stop=False)
        pe.matmul(out, wh[:, t, :], xl[:, t, c:c + n], start=False, stop=False)
        m = pe.matmul(out, wl[:, t, :], xh[:, t, c:c + n], start=False, stop=t == tiles - 1)
    return m


def squares(act, x, cols, sq, sq_made, sq_used):
    for k in range(KD):
        act.wait_ge(sq_used, free(k))
        act.activation(sq[:, k % 2, 0:cols], x[:, k, 0:cols], ACT.Square).then_inc(sq_made, 1)


def sum_squares(pe, splits, sq, banks, ones, sq_made, sq_used):
    pe.sem_inc(sq_used, 2)
    for k in range(KD):
        pe.wait_ge(sq_made, k + 1)
        for j, (c, n) in enumerate(splits):
            m = pe.matmul(banks[j][:, 0:n], ones[:, :], sq[:, k % 2, c:c + n], start=k == 0, stop=k == KD - 1)
        m.then_inc(sq_used, 1)


def inverse_root(act, sums, out, eps, log_made, made, n=1, at=0, width=D):
    for j, (s, o) in enumerate(zip(sums, out)):
        act.activation(o, s, ACT.Ln, bias=eps, scale=1.0 / width).then_inc(log_made, 1)
    for j, o in enumerate(out):
        act.wait_ge(log_made, at + j + 1)
        act.activation(o, o, ACT.Exp, scale=-0.5).then_inc(made, 1)


def stage_load(nc, ctx, A, K, bank, h0, u, h0_dram):
    meta_in, x_in0, x_in1, low_turned, high_turned, meta_turned, low_kept, high_kept, sq_made, sq_used, logs, rstd_made, zeroed, stored = sems(
        ctx, nc, "l", "meta_in x_in0 x_in1 low_turned high_turned meta_turned low_kept high_kept sq_made sq_used logs rstd_made zeroed stored")
    x_in = (x_in0, x_in1)
    ident, ones, vec, eps = K["ident"], K["ones"], K["vec"], K["eps"]
    x = A["x"]
    with ExitStack() as inner:
        xs = buffer(inner, nc, "x_rows", [P, 2, D])
        mt = buffer(inner, nc, "meta_rows", [META, D])
        sq = buffer(inner, nc, "l_sq", [P, 2, WIDE])
        rstd = buffer(inner, nc, "l_rstd", [P, WIDE])
        block = inner.enter_context(nc.Block())

        @block.sync
        def _(sp):
            sp.dma_start(mt[:, :], A["meta_tokens"]).then_inc(meta_in, 16)
            with sp.Fori(0, NB // 2) as i:
                for s in range(2):
                    sp.wait_ge(high_turned, free(2 * i + s))
                    sp.dma_start(xs[:, s, :], x[0, ds((2 * i + s) * P, P), :]).then_inc(x_in[s], 16)
            sp.wait_ge(low_kept, ready(NB - 1))
            sp.wait_ge(high_kept, ready(NB - 1))
            sp.wait_ge(zeroed, 2)
            sp.dma_start(h0_dram, h0[:, :, :]).then_inc(stored, 16)
            sp.wait_ge(stored, 16)

        @block.tensor
        def _(pe):
            pe.sem_inc(high_turned, 2)
            pe.wait_ge(meta_in, 16)
            for k in range(KD):
                m = pe.transpose(bank[4][:, k * META:(k + 1) * META], mt[:, k * P:(k + 1) * P], ident[0:META, 0:META])
            m.then_inc(meta_turned, 1)
            with pe.Fori(0, NB // 2) as i:
                for s in range(2):
                    pe.wait_ge(x_in[s], 16 * i + 16)
                    pe.wait_ge(low_kept, free(2 * i + s))
                    for k in range(4):
                        m = pe.transpose(bank[2 * s][:, k * P:(k + 1) * P], xs[:, s, k * P:(k + 1) * P], ident[:, :])
                    m.then_inc(low_turned, 1)
                    pe.wait_ge(high_kept, free(2 * i + s))
                    for k in range(4):
                        m = pe.transpose(bank[2 * s + 1][:, k * P:(k + 1) * P], xs[:, s, (k + 4) * P:(k + 5) * P], ident[:, :])
                    m.then_inc(high_turned, 1)
            sum_squares(pe, FULL, sq, bank[5:8], ones, sq_made, sq_used)

        @block.vector
        def _(dve):
            dve.sem_inc(low_kept, 2)
            dve.memset(h0[:, :, 0:HEAD], 0.0).then_inc(zeroed, 1)
            dve.wait_ge(meta_turned, 1)
            dve.tensor_copy(h0[:, :, HEAD:P], bank[4][:, 0:KD * META].rearrange("p (k t) -> p k t", t=META)).then_inc(zeroed, 1)
            with dve.Fori(0, NB // 2) as i:
                for s in range(2):
                    dve.wait_ge(low_turned, 2 * i + s + 1)
                    dve.tensor_copy(h0[:, 0:4, ds((2 * i + s) * P + P, P)],
                                    bank[2 * s][:, :].rearrange("p (k t) -> p k t", t=P)).then_inc(low_kept, 1)
            dve.wait_ge(rstd_made, len(FULL))
            dve.wait_ge(high_kept, ready(NB - 1))
            for k in range(KD):
                dve.scalar_tensor_tensor(u[:, k, :], h0[:, k, :], vec[:, VEC["mix_pre"] + k:VEC["mix_pre"] + k + 1],
                                         rstd[:, :], ALU.mult, ALU.mult)

        @block.scalar
        def _(act):
            act.sem_inc(high_kept, 2)
            with act.Fori(0, NB // 2) as i:
                for s in range(2):
                    act.wait_ge(high_turned, ready(2 * i + s))
                    act.copy(h0[:, 4:8, ds((2 * i + s) * P + P, P)],
                             bank[2 * s + 1][:, :].rearrange("p (k t) -> p k t", t=P)).then_inc(high_kept, 1)
            act.wait_ge(low_kept, ready(NB - 1))
            act.wait_ge(high_kept, ready(NB - 1))
            act.wait_ge(zeroed, 2)
            squares(act, h0, WIDE, sq, sq_made, sq_used)
            act.wait_ge(sq_used, ready(KD - 1))
            inverse_root(act, [bank[5 + j][:, 0:n] for j, (c, n) in enumerate(FULL)],
                         [rstd[:, c:c + n] for c, n in FULL], eps[:, 0:1], logs, rstd_made)


def stage_hgrn_in(nc, ctx, A, K, bank, u, q, k, lf, v):
    w0, w1, wv0, wv1, mm, taken, vmm, vkept, lb_made, sig, logged, small, fixed = sems(
        ctx, nc, "p", "w0 w1 wv0 wv1 mm taken vmm vkept lb_made sig logged small fixed")
    w_in = (w0, w1)
    vec = K["vec"]
    w = A["w_in"][0].rearrange("(k p) n -> p k n", p=P)
    lbc = VEC["lb"]
    with ExitStack() as inner:
        ring = buffer(inner, nc, "p_ring", [P, 2, KD, P])
        wv = buffer(inner, nc, "p_wv", [P, KD, 4 * P])
        lb = buffer(inner, nc, "lb", [P, 4, 4])
        f = buffer(inner, nc, "f_tile", [P, WIDE])
        tiny = buffer(inner, nc, "f_tiny", [P, WIDE])
        block = inner.enter_context(nc.Block())

        @block.sync
        def _(sp):
            with sp.Fori(0, HALF) as i:
                for s in range(2):
                    sp.wait_ge(mm, free(2 * i + s))
                    sp.dma_start(ring[:, s, :, :], w[:, :, ds((2 * i + s) * P, P)]).then_inc(w_in[s], 16)
            sp.dma_start(wv[:, :, :], w[:, :, 8 * P:12 * P]).then_inc(wv0, 16)

        @block.tensor
        def _(pe):
            pe.sem_inc(mm, 2)
            with pe.Fori(0, HALF) as i:
                for s in range(2):
                    pe.wait_ge(w_in[s], 16 * i + 16)
                    pe.wait_ge(taken, free(2 * i + s))
                    for j, (c, n) in enumerate(REAL):
                        for t in range(KD):
                            m = pe.matmul(bank[3 * s + j][:, 0:n], ring[:, s, t, :], u[:, t, c:c + n], start=t == 0, stop=t == KD - 1)
                    m.then_inc(mm, 1)
            pe.wait_ge(wv0, 16)
            for c in range(CHUNKS):
                pe.wait_ge(vkept, free(c))
                for t in range(KD):
                    m = pe.matmul(bank[6 + c % 2][:, :], u[:, t, c * P:(c + 1) * P], wv[:, t, :], start=t == 0, stop=t == KD - 1)
                m.then_inc(vmm, 1)

        @block.scalar
        def _(act):
            act.wait_ge(lb_made, 1)
            act.activation(lb[:, 0, :], lb[:, 1, :], ACT.Exp).then_inc(lb_made, 1)
            act.sem_inc(taken, 2)
            with act.Fori(0, HALF // 2) as i:
                for s in range(2):
                    act.wait_ge(mm, ready(2 * i + s))
                    for j, (c, n) in enumerate(REAL):
                        a = act.copy(q[:, ds(2 * i + s, 1), c:c + n], bank[3 * s + j][:, 0:n])
                    a.then_inc(taken, 1)
            for t in range(HALF):
                s = t % 2
                act.wait_ge(mm, ready(HALF + t))
                act.wait_ge(small, t + 1)
                for j, (c, n) in enumerate(REAL):
                    act.activation(f[:, c:c + n], bank[3 * s + j][:, 0:n], ACT.Sigmoid)
                    a = act.activation(k[:, t, c:c + n], bank[3 * s + j][:, 0:n], ACT.Sigmoid, scale=-1.0)
                a.then_inc(taken, 1)
                act.wait_ge(fixed, t + 1)
                act.activation(lf[:, t, HEAD:], f[:, HEAD:], ACT.Ln).then_inc(logged, 1)

        @block.vector
        def _(dve):
            n = 0

            def then(ins):
                nonlocal n
                n += 1
                ins.then_inc(logged_own, 1)
                dve.wait_ge(logged_own, n)
            logged_own = sig
            then(dve.memset(q[:, :, 0:HEAD], 0.0))
            dve.memset(k[:, :, 0:HEAD], 0.0)
            dve.memset(lf[:, :, 0:HEAD], 0.0)
            dve.tensor_tensor(lb[:, 1, :], vec[:, lbc:lbc + 4], vec[:, lbc:lbc + 4], ALU.subtract).then_inc(lb_made, 1)
            dve.wait_ge(lb_made, 2)
            then(dve.reciprocal(lb[:, 1, :], lb[:, 0, :]))
            then(dve.tensor_tensor(lb[:, 0, :], lb[:, 0, :], lb[:, 1, :], ALU.mult))
            then(dve.tensor_tensor(lb[:, 2, :], lb[:, 0, :], lb[:, 0, :], ALU.subtract))
            then(dve.tensor_scalar(lb[:, 2, :], lb[:, 2, :], 0.0, 1.0, ALU.max, ALU.min))
            then(dve.tensor_scalar(lb[:, 3, :], lb[:, 2, :], -1.0, 1.0, ALU.mult, ALU.add))
            dve.sem_inc(small, 1)
            for t in range(HALF):
                dve.wait_ge(taken, ready(HALF + t))
                then(dve.tensor_scalar(f[:, HEAD:], f[:, HEAD:], lb[:, 3, t:t + 1], lb[:, 2, t:t + 1], ALU.mult, ALU.add))
                then(dve.tensor_scalar(f[:, HEAD:], f[:, HEAD:], 1e-30, None, ALU.max))
                then(dve.tensor_scalar(tiny[:, HEAD:], f[:, HEAD:], 2.0 ** -60, None, ALU.is_lt))
                then(dve.tensor_scalar(tiny[:, HEAD:], tiny[:, HEAD:], 2.0 ** 64 - 1.0, 1.0, ALU.mult, ALU.add))
                dve.tensor_tensor(f[:, HEAD:], f[:, HEAD:], tiny[:, HEAD:], ALU.mult).then_inc(fixed, 1)
                dve.wait_ge(fixed, t + 1)
                then(dve.tensor_scalar(tiny[:, HEAD:], tiny[:, HEAD:], 2.0, -64 * LN2, ALU.is_ge, ALU.mult))
                dve.wait_ge(logged, t + 1)
                then(dve.tensor_tensor(lf[:, t, HEAD:], lf[:, t, HEAD:], tiny[:, HEAD:], ALU.add))
                then(dve.tensor_scalar(k[:, t, HEAD:], k[:, t, HEAD:], lb[:, 3, t:t + 1], None, ALU.mult))
                dve.sem_inc(small, 1)
            dve.sem_inc(vkept, 2)
            for c in range(CHUNKS):
                dve.wait_ge(vmm, c + 1)
                dve.tensor_copy(v[:, c, :], bank[6 + c % 2][:, :]).then_inc(vkept, 1)


def constants(ctx, nc):
    return {"ident": buffer(ctx, nc, "ident", [P, P]), "ones": buffer(ctx, nc, "ones", [P, P]),
            "vec": buffer(ctx, nc, "vec", [P, 2 * P]), "level": buffer(ctx, nc, "level", [P, LEVELS + 1, P], I32),
            "causal": buffer(ctx, nc, "causal", [P, P]), "reset": buffer(ctx, nc, "reset", [P, BANK]),
            "lower": buffer(ctx, nc, "lower", [P, P]), "eps": buffer(ctx, nc, "eps", [P, 1])}


def stage_hgrn(nc, ctx, A, K, bank, q, k, lf, v, o, spare):
    staged, summed, subbed, exped, scaled, scored, picked, turned, kd_kept, added, state_made, o_mm, o_kept, cleared, waited = sems(
        ctx, nc, "h", "staged summed subbed exped scaled scored picked turned kd_kept added state_made o_mm o_kept cleared waited")
    ident, level, reset = K["ident"], K["level"], K["reset"]
    NX = LEVELS + 2
    LAST = CHUNKS - 1
    with ExitStack() as inner:
        lfc = buffer(inner, nc, "lf_chunk", [P, 2, BANK])
        kc = buffer(inner, nc, "k_chunk", [P, 2, BANK])
        vc = buffer(inner, nc, "v_chunk", [P, 2, BANK])
        b = buffer(inner, nc, "b_chunk", [P, BANK])
        x = buffer(inner, nc, "scaled_chunk", [P, 2, NX, BANK])
        kdt = buffer(inner, nc, "kd_tok", [P, BANK])
        qe, sc, st = (spare[:, j * 2 * BANK:(j + 1) * 2 * BANK].rearrange("p (s n) -> p s n", s=2) for j in range(3))
        block = inner.enter_context(nc.Block())

        def heads(ap):
            return ap.rearrange("p (h t) -> p h t", t=P)

        def halves(ap, l):
            w = ap.rearrange("p (n u t) -> p n u t", u=2, t=1 << l)
            return w[:, :, 0, :], w[:, :, 1, :]

        @block.gpsimd
        def _(pool):
            def stage(c, s):
                pool.wait_ge(o_mm, free(c))
                pool.tensor_copy(heads(lfc[:, s, :]), lf[:, :, ds(c * P, P)]).then_inc(staged, 1)
                pool.tensor_copy(heads(kc[:, s, :]), k[:, :, ds(c * P, P)]).then_inc(staged, 1)
                pool.tensor_copy(vc[:, s, :], v[:, ds(c, 1), :].rearrange("p a n -> p (a n)")).then_inc(staged, 1)
            with pool.Fori(0, LAST // 2) as i:
                for s in range(2):
                    stage(2 * i + s, s)
            stage(LAST, LAST % 2)

        @block.vector
        def _(dve):
            dve.memset(sc[:, :, :], 0.0).then_inc(cleared, 1)
            dve.memset(st[:, 0, :], 0.0).then_inc(state_made, 1)
            dve.sem_inc(picked, 4)

            def differences(c, s):
                dve.wait_ge(staged, 3 * c + 3)
                dve.tensor_tensor_scan(b[:, :], reset[:, :], lfc[:, s, :], 0.0, ALU.mult, ALU.add).then_inc(summed, 1)
                dve.wait_ge(summed, c + 1)
                for l in range(LEVELS):
                    left, right = halves(b[:, :], l)
                    x_left, x_right = halves(x[:, s, l, :], l)
                    middle = left[:, :, (1 << l) - 1:1 << l].to_broadcast(list(left.shape))
                    dve.tensor_tensor(x_left, middle, left, ALU.subtract)
                    dve.tensor_tensor(x_right, right, middle, ALU.subtract)
                last = heads(b[:, :])[:, :, P - 1:P].to_broadcast([P, HALF, P])
                dve.tensor_tensor(heads(x[:, s, LEVELS + 1, :]), last, heads(b[:, :]), ALU.subtract)
                dve.tensor_copy(x[:, s, LEVELS, :], b[:, :]).then_inc(subbed, 1)

            def scale(c, s):
                qc = q[:, :, ds(c * P, P)]
                for l in range(LEVELS):
                    if l % 3 == 0:
                        dve.wait_ge(exped, 3 * c + l // 3 + 1)
                    x_left, x_right = halves(x[:, s, l, :], l)
                    k_left, _ = halves(kc[:, s, :], l)
                    dve.tensor_tensor(x_left, x_left, k_left, ALU.mult)
                    w = qc.rearrange("p h (n u t) -> p h n u t", u=2, t=1 << l)[:, :, :, 1, :]
                    y = x[:, s, l, :].rearrange("p (h n u t) -> p h n u t", h=HALF, u=2, t=1 << l)[:, :, :, 1, :]
                    dve.tensor_tensor(y, y, w, ALU.mult).then_inc(scaled, 1)
                dve.tensor_tensor(heads(qe[:, s, :]), heads(x[:, s, LEVELS, :]), qc, ALU.mult).then_inc(scaled, 1)
                dve.tensor_tensor(x[:, s, LEVELS + 1, :], x[:, s, LEVELS + 1, :], kc[:, s, :], ALU.mult).then_inc(scaled, 1)

            def pick(c, s):
                for l in range(LEVELS + 1):
                    dve.wait_ge(scored, 8 * c + l + 1)
                    dve.wait_ge(picked, 8 * c + l + 4)
                    dve.sem_inc(waited, 1)
                    dve.wait_ge(cleared, 1)
                    mask = level[:, l:l + 1, :].to_broadcast([P, HALF, P])
                    dve.copy_predicated(heads(sc[:, s, :]), mask, heads(bank[l % 4][:, :])).then_inc(picked, 1)
                dve.wait_ge(added, c + 1)
                for h in range(HALF):
                    m = dve.scalar_tensor_tensor(st[:, 1 - s, h * P:(h + 1) * P], st[:, s, h * P:(h + 1) * P],
                                                 x[:, s, LEVELS, (h + 1) * P - 1:(h + 1) * P],
                                                 bank[6][:, h * P:(h + 1) * P], ALU.mult, ALU.add)
                m.then_inc(state_made, 1)
            differences(0, 0)
            with dve.Fori(0, LAST // 2) as i:
                for s in range(2):
                    scale(2 * i + s, s)
                    differences(2 * i + s + 1, 1 - s)
                    pick(2 * i + s, s)
            scale(LAST, LAST % 2)
            pick(LAST, LAST % 2)

        @block.scalar
        def _(act):
            act.sem_inc(kd_kept, 1)
            act.sem_inc(o_kept, 1)

            def exponentials(c, s):
                act.wait_ge(subbed, c + 1)
                for g in range(3):
                    y = x[:, s, 3 * g:3 * g + 3, :]
                    act.activation(y, y, ACT.Exp).then_inc(exped, 1)

            def evacuate(c):
                act.wait_ge(turned, c + 1)
                act.copy(kdt[:, :], bank[4][:, :]).then_inc(kd_kept, 1)
                act.wait_ge(o_mm, ready(c))
                act.copy(o[:, :, ds(c * P, P)], heads(bank[5][:, :])).then_inc(o_kept, 1)
            exponentials(0, 0)
            with act.Fori(0, LAST // 2) as i:
                for s in range(2):
                    exponentials(2 * i + s + 1, 1 - s)
                    evacuate(2 * i + s)
            evacuate(LAST)

        @block.tensor
        def _(pe):
            pe.sem_inc(o_mm, 2)

            def chunk(c, s):
                for l in range(LEVELS + 1):
                    pe.wait_ge(scaled, 9 * c + min(l, LEVELS - 1) + 1)
                    pe.wait_ge(picked, 8 * c + l + 1)
                    for h in range(HALF):
                        col = slice(h * P, (h + 1) * P)
                        if l < LEVELS:
                            m = pe.matmul(bank[l % 4][:, col], x[:, s, l, col], x[:, s, l, col], start=True, stop=True)
                        else:
                            m = pe.matmul(bank[l % 4][:, col], kc[:, s, col], q[:, ds(h, 1), ds(c * P, P)], start=True, stop=True)
                    m.then_inc(scored, 1)
                pe.wait_ge(scaled, 9 * c + 9)
                pe.wait_ge(kd_kept, c + 1)
                for h in range(HALF):
                    m = pe.transpose(bank[4][:, h * P:(h + 1) * P], x[:, s, LEVELS + 1, h * P:(h + 1) * P], ident[:, :])
                m.then_inc(turned, 1)
                pe.wait_ge(state_made, c + 1)
                pe.wait_ge(kd_kept, c + 2)
                for h in range(HALF):
                    col = slice(h * P, (h + 1) * P)
                    m = pe.matmul(bank[6][:, col], kdt[:, col], vc[:, s, col], start=True, stop=True)
                m.then_inc(added, 1)
                pe.wait_ge(picked, 8 * c + 12)
                pe.wait_ge(o_kept, c + 1)
                for h in range(HALF):
                    col = slice(h * P, (h + 1) * P)
                    pe.matmul(bank[5][:, col], vc[:, s, col], sc[:, s, col], start=True, stop=False)
                    m = pe.matmul(bank[5][:, col], st[:, s, col], qe[:, s, col], start=False, stop=True)
                m.then_inc(o_mm, 1)
            with pe.Fori(0, LAST // 2) as i:
                for s in range(2):
                    chunk(2 * i + s, s)
            chunk(LAST, LAST % 2)


def stage_branches(nc, ctx, A, K, bank, u, o, p):
    (sq_made, sums, logs, rstd_made, normed, w0, w1, mm, g_taken, gated, v_taken, chain, pooled, proj_in, ymm, y_taken) = sems(
        ctx, nc, "b", "sq_made sums logs rstd_made normed w0 w1 mm g_taken gated v_taken chain pooled proj_in ymm y_taken")
    w_in = (w0, w1)
    ones, vec, eps = K["ones"], K["vec"], K["eps"]
    w = A["w_in"][0].rearrange("(k p) n -> p k n", p=P)
    G0, V0 = 3 * HALF, 4 * HALF
    with ExitStack() as inner:
        ring = buffer(inner, nc, "b_ring", [P, 2, KD, P])
        proj = buffer(inner, nc, "pool_proj", [P, HALF, P])
        sq = buffer(inner, nc, "b_sq", [P, LIVE])
        rstd = buffer(inner, nc, "b_rstd", [P, LIVE])
        sig = buffer(inner, nc, "b_sig", [P, 2, LIVE])
        v = buffer(inner, nc, "pool_v", [P, HALF, WIDE])
        s0 = buffer(inner, nc, "pool_sum0", [P, HALF, WIDE])
        s1 = buffer(inner, nc, "pool_sum1", [P, HALF, WIDE])
        block = inner.enter_context(nc.Block())

        @block.sync
        def _(sp):
            sp.dma_start(proj[:, :, :], A["pool_proj"][0].rearrange("g c d -> c g d")).then_inc(proj_in, 16)
            with sp.Fori(0, HALF) as i:
                for s in range(2):
                    sp.wait_ge(mm, free(2 * i + s))
                    sp.dma_start(ring[:, s, :, :], w[:, :, ds((2 * i + s + G0) * P, P)]).then_inc(w_in[s], 16)

        @block.tensor
        def _(pe):
            pe.sem_inc(mm, 2)
            for h in range(HALF):
                pe.wait_ge(sq_made, h + 1)
                if h:
                    pe.wait_ge(rstd_made, 3 * h)
                for j, (c, n) in enumerate(LIVES):
                    m = pe.matmul(bank[5 + j][:, 0:n], ones[:, :], sq[:, c:c + n], start=True, stop=True)
                m.then_inc(sums, 1)
            pe.wait_ge(rstd_made, 12)
            with pe.Fori(0, HALF // 2) as i:
                for s in range(2):
                    pe.wait_ge(w_in[s], 16 * i + 16)
                    pe.wait_ge(g_taken, free(2 * i + s))
                    for j, (c, n) in enumerate(LIVES):
                        for t in range(KD):
                            m = pe.matmul(bank[3 * s + j][:, 0:n], ring[:, s, t, :], u[:, t, FIRST + c:FIRST + c + n], start=t == 0, stop=t == KD - 1)
                    m.then_inc(mm, 1)
            with pe.Fori(0, HALF // 2) as i:
                for s in range(2):
                    pe.wait_ge(w_in[s], 16 * i + 48)
                    pe.wait_ge(g_taken, ready(HALF - 1))
                    pe.wait_ge(v_taken, free(2 * i + s))
                    for j, (c, n) in enumerate(REAL):
                        for t in range(KD):
                            m = pe.matmul(bank[3 * s + j][:, 0:n], ring[:, s, t, :], u[:, t, c:c + n], start=t == 0, stop=t == KD - 1)
                    m.then_inc(mm, 1)
            pe.wait_ge(proj_in, 16)
            pe.wait_ge(v_taken, ready(HALF - 1))
            for g in range(HALF):
                pe.wait_ge(pooled, g + 1)
                pe.wait_ge(y_taken, free(g))
                for j, (c, n) in enumerate(LIVES):
                    m = pe.matmul(bank[3 * (g % 2) + j][:, 0:n], proj[:, g, :], s0[:, g, FIRST + c:FIRST + c + n], start=True, stop=True)
                m.then_inc(ymm, 1)

        @block.scalar
        def _(act):
            act.sem_inc(g_taken, 2)
            act.sem_inc(v_taken, 2)
            act.sem_inc(y_taken, 2)
            for h in range(HALF):
                if h:
                    act.wait_ge(sums, h)
                act.activation(sq[:, :], o[:, h, FIRST:], ACT.Square).then_inc(sq_made, 1)
                act.wait_ge(sums, h + 1)
                if h:
                    act.wait_ge(normed, h)
                inverse_root(act, [bank[5 + j][:, 0:n] for j, (c, n) in enumerate(LIVES)],
                             [rstd[:, c:c + n] for c, n in LIVES], eps[:, 0:1], logs, rstd_made, at=3 * h, width=P)
            for t in range(HALF):
                s = t % 2
                act.wait_ge(mm, ready(t))
                if t >= 2:
                    act.wait_ge(gated, t - 1)
                for j, (c, n) in enumerate(LIVES):
                    a = act.activation(sig[:, s, c:c + n], bank[3 * s + j][:, 0:n], ACT.Sigmoid)
                a.then_inc(g_taken, 1)
            for t in range(HALF):
                act.wait_ge(mm, ready(HALF + t))
                for j, (c, n) in enumerate(REAL):
                    a = act.copy(v[:, t, c:c + n], bank[3 * (t % 2) + j][:, 0:n])
                a.then_inc(v_taken, 1)
            for g in range(HALF):
                act.wait_ge(ymm, g + 1)
                for j, (c, n) in enumerate(LIVES):
                    a = act.mul(p[:, g, c:c + n], bank[3 * (g % 2) + j][:, 0:n], vec[:, VEC["pool_scale"] + g:VEC["pool_scale"] + g + 1])
                a.then_inc(y_taken, 1)

        @block.vector
        def _(dve):
            n = 0

            def then(ins):
                nonlocal n
                n += 1
                ins.then_inc(chain, 1)
                dve.wait_ge(chain, n)
            dve.memset(v[:, :, 0:HEAD], 0.0)
            for h in range(HALF):
                dve.wait_ge(rstd_made, 3 * h + 3)
                dve.scalar_tensor_tensor(o[:, h, FIRST:], o[:, h, FIRST:], vec[:, VEC["out_norm"] + h:VEC["out_norm"] + h + 1],
                                         rstd[:, :], ALU.mult, ALU.mult).then_inc(normed, 1)
            for t in range(HALF):
                dve.wait_ge(g_taken, ready(t))
                dve.wait_ge(normed, t + 1)
                dve.tensor_tensor(o[:, t, FIRST:], o[:, t, FIRST:], sig[:, t % 2, :], ALU.mult).then_inc(gated, 1)
            for g in range(HALF):
                dve.wait_ge(v_taken, ready(g))
                src = v
                for e in range(g + 1):
                    dst = (s0, s1)[(g - e) % 2]
                    back = 1 << e
                    lo = P - 16 + back
                    then(dve.tensor_tensor(dst[:, g, lo:], src[:, g, lo:], src[:, g, lo - back:WIDE - back], ALU.add))
                    if e < g:
                        then(dve.tensor_copy(dst[:, g, HEAD:lo], src[:, g, HEAD:lo]))
                    src = dst
                size = 2 << g
                if size > FIRST - HEAD + 1:
                    short = FIRST - HEAD + 1
                    then(dve.scalar_tensor_tensor(s0[:, g, FIRST:FIRST + 1], s0[:, g, FIRST:FIRST + 1], 1.0 / short, v[:, g, FIRST:FIRST + 1], ALU.mult, ALU.subtract))
                    dve.scalar_tensor_tensor(s0[:, g, FIRST + 1:], s0[:, g, FIRST + 1:], 1.0 / size, v[:, g, FIRST + 1:], ALU.mult, ALU.subtract).then_inc(pooled, 1)
                else:
                    dve.scalar_tensor_tensor(s0[:, g, FIRST:], s0[:, g, FIRST:], 1.0 / size, v[:, g, FIRST:], ALU.mult, ALU.subtract).then_inc(pooled, 1)


def stage_mix(nc, ctx, A, K, bank, u, o, p, z):
    w0, w1, mm, sig_made, summed, product, added = sems(ctx, nc, "z", "w0 w1 mm sig_made summed product added")
    w_in = (w0, w1)
    w = A["w_in"][0].rearrange("(k p) n -> p k n", p=P)
    wh = A["w_branch_hgrn"][0].rearrange("(k p) n -> p k n", p=P)
    wp = A["w_branch_pool"][0].rearrange("(k p) n -> p k n", p=P)
    GA, GB = 5 * HALF, 7 * HALF
    with ExitStack() as inner:
        ring = buffer(inner, nc, "z_ring", [P, 2, 3 * KD, P])
        sig = buffer(inner, nc, "z_sig", [P, 2, 2, 342])
        block = inner.enter_context(nc.Block())

        @block.sync
        def _(sp):
            with sp.Fori(0, KD // 2) as i:
                for s in range(2):
                    sp.wait_ge(mm, 6 * i + 3 * s + 3)
                    n = 2 * i + s
                    sp.dma_start(ring[:, s, 0:8, :], w[:, :, ds((n + GA) * P, P)]).then_inc(w_in[s], 16)
                    sp.dma_start(ring[:, s, 8:16, :], w[:, :, ds((n + GB) * P, P)]).then_inc(w_in[s], 16)
                    sp.dma_start(ring[:, s, 16:20, :], wh[:, :, ds(n * P, P)]).then_inc(w_in[s], 16)
                    sp.dma_start(ring[:, s, 20:24, :], wp[:, :, ds(n * P, P)]).then_inc(w_in[s], 16)

        @block.tensor
        def _(pe):
            pe.sem_inc(mm, 6)
            with pe.Fori(0, KD // 2) as i:
                for s in range(2):
                    pe.wait_ge(w_in[s], 64 * i + 64)
                    for j, (c, n) in enumerate(LIVES):
                        e = 3 * s + j
                        b = bank[4 * (e % 2):4 * (e % 2) + 4]
                        pe.wait_ge(product, 6 * i + e + 1)
                        for t in range(KD):
                            pe.matmul(b[0][:, 0:n], ring[:, s, t, :], u[:, t, FIRST + c:FIRST + c + n], start=t == 0, stop=t == KD - 1)
                        for t in range(KD):
                            pe.matmul(b[1][:, 0:n], ring[:, s, 8 + t, :], u[:, t, FIRST + c:FIRST + c + n], start=t == 0, stop=t == KD - 1)
                        for t in range(HALF):
                            pe.matmul(b[2][:, 0:n], ring[:, s, 16 + t, :], o[:, t, FIRST + c:FIRST + c + n], start=t == 0, stop=t == HALF - 1)
                        for t in range(HALF):
                            m = pe.matmul(b[3][:, 0:n], ring[:, s, 20 + t, :], p[:, t, c:c + n], start=t == 0, stop=t == HALF - 1)
                        m.then_inc(mm, 1)

        @block.scalar
        def _(act):
            with act.Fori(0, KD // 2) as i:
                for e in range(6):
                    n = LIVES[e % 3][1]
                    act.wait_ge(mm, 6 * i + e + 7)
                    act.wait_ge(added, 6 * i + e + 1)
                    act.activation(sig[:, e % 2, 0, 0:n], bank[4 * (e % 2)][:, 0:n], ACT.Sigmoid)
                    act.activation(sig[:, e % 2, 1, 0:n], bank[4 * (e % 2) + 1][:, 0:n], ACT.Sigmoid).then_inc(sig_made, 1)

        @block.vector
        def _(dve):
            dve.sem_inc(product, 2)
            with dve.Fori(0, KD // 2) as i:
                for e in range(6):
                    n = LIVES[e % 3][1]
                    dve.wait_ge(sig_made, 6 * i + e + 1)
                    for g in range(2):
                        m = dve.tensor_tensor(sig[:, e % 2, g, 0:n], sig[:, e % 2, g, 0:n], bank[4 * (e % 2) + 2 + g][:, 0:n], ALU.mult)
                    m.then_inc(product, 1)

        @block.gpsimd
        def _(pool):
            pool.sem_inc(added, 2)
            with pool.Fori(0, KD // 2) as i:
                for e in range(6):
                    c, n = LIVES[e % 3]
                    pool.wait_ge(product, 6 * i + e + 3)
                    pool.tensor_tensor(z[:, ds(2 * i + e // 3, 1), c:c + n], sig[:, e % 2, 0, 0:n], sig[:, e % 2, 1, 0:n], ALU.add).then_inc(added, 1)


def stage_project(nc, ctx, A, K, bank, name, weights, tiles_in, x, y, h, gain, splits, h_load, h_store, u, u_gain):
    (w0, w1, mm, kept, squared, added, sums, logs, rstd_made, scaled, h_in, h_made, sq_made, sq_used, logs2, rstd2, u_made, u_hi, u_lo, stored) = sems(
        ctx, nc, name, "w0 w1 mm kept squared added sums logs rstd_made scaled h_in h_made sq_made sq_used logs2 rstd2 u_made u_hi u_lo stored")
    w_in = (w0, w1)
    ones, vec, eps = K["ones"], K["vec"], K["eps"]
    w = weights.rearrange("(k p) n -> p k n", p=P)
    cols = splits[-1][0] + splits[-1][1]
    ns = len(splits)
    with ExitStack() as inner:
        ring = buffer(inner, nc, name + "_ring", [P, 2, tiles_in, P])
        sq = buffer(inner, nc, name + "_sq", [P, 2, cols])
        acc = buffer(inner, nc, name + "_acc", [P, cols])
        rstd = buffer(inner, nc, name + "_rstd", [P, cols])
        block = inner.enter_context(nc.Block())

        @block.sync
        def _(sp):
            sp.dma_start(h[:, :, :], h_load).then_inc(h_in, 16)
            with sp.Fori(0, KD // 2) as i:
                for s in range(2):
                    sp.wait_ge(mm, free(2 * i + s))
                    sp.dma_start(ring[:, s, :, :], w[:, :, ds((2 * i + s) * P, P)]).then_inc(w_in[s], 16)
            sp.wait_ge(h_made, KD)
            sp.dma_start(h_store, h[:, :, :]).then_inc(stored, 16)
            sp.wait_ge(stored, 16)

        @block.tensor
        def _(pe):
            pe.sem_inc(mm, 2)
            with pe.Fori(0, KD // 2) as i:
                for s in range(2):
                    pe.wait_ge(w_in[s], 16 * i + 16)
                    pe.wait_ge(kept, free(2 * i + s))
                    for j, (c, n) in enumerate(splits):
                        for t in range(tiles_in):
                            m = pe.matmul(bank[ns * s + j][:, 0:n], ring[:, s, t, :], x[:, t, c:c + n], start=t == 0, stop=t == tiles_in - 1)
                    m.then_inc(mm, 1)
            pe.wait_ge(added, ready(KD - 1))
            pe.wait_ge(kept, ready(KD - 1))
            for j, (c, n) in enumerate(splits):
                m = pe.matmul(bank[j][:, 0:n], ones[:, :], acc[:, c:c + n], start=True, stop=True)
            m.then_inc(sums, 1)
            pe.sem_inc(sq_used, 2)
            for k in range(KD):
                pe.wait_ge(sq_made, k + 1)
                for j, (c, n) in enumerate(splits):
                    m = pe.matmul(bank[ns + j][:, 0:n], ones[:, :], sq[:, k % 2, c:c + n], start=k == 0, stop=k == KD - 1)
                m.then_inc(sq_used, 1)

        @block.vector
        def _(dve):
            dve.sem_inc(kept, 2)
            with dve.Fori(0, KD // 2) as i:
                for s in range(2):
                    dve.wait_ge(mm, ready(2 * i + s))
                    for j, (c, n) in enumerate(splits):
                        m = dve.tensor_copy(y[:, ds(2 * i + s, 1), c:c + n], bank[ns * s + j][:, 0:n])
                    m.then_inc(kept, 1)
            dve.wait_ge(h_in, 16)
            dve.wait_ge(rstd_made, ns)
            for k in range(KD):
                dve.scalar_tensor_tensor(y[:, k, 0:cols], y[:, k, 0:cols], vec[:, VEC[gain] + k:VEC[gain] + k + 1], rstd[:, :],
                                         ALU.mult, ALU.mult).then_inc(scaled, 1)
                dve.wait_ge(scaled, k + 1)
                dve.tensor_tensor(h[:, k, :], h[:, k, :], y[:, k, 0:cols], ALU.add).then_inc(h_made, 1)
            dve.wait_ge(rstd2, ns)
            dve.wait_ge(h_made, KD)

            def low(k):
                dve.wait_ge(u_hi, k + 1)
                dve.tensor_tensor(u[1][:, k, 0:cols], y[:, k, 0:cols], u[0][:, k, 0:cols], ALU.subtract)
            for k in range(KD):
                dve.scalar_tensor_tensor(y[:, k, 0:cols], h[:, k, :], vec[:, VEC[u_gain] + k:VEC[u_gain] + k + 1], acc[:, :],
                                         ALU.mult, ALU.mult).then_inc(u_made, 1)
                if k % 2 and k > 1:
                    low(k - 2)
            low(KD - 1)

        @block.scalar
        def _(act):
            act.sem_inc(squared, 2)
            with act.Fori(0, KD // 2) as i:
                for s in range(2):
                    act.wait_ge(kept, ready(2 * i + s))
                    act.wait_ge(added, free(2 * i + s))
                    act.activation(sq[:, s, :], y[:, ds(2 * i + s, 1), 0:cols], ACT.Square).then_inc(squared, 1)
            act.wait_ge(sums, 1)
            inverse_root(act, [bank[j][:, 0:n] for j, (c, n) in enumerate(splits)], [rstd[:, c:c + n] for c, n in splits],
                         eps[:, 0:1], logs, rstd_made)
            for k in range(KD):
                act.wait_ge(h_made, k + 1)
                act.wait_ge(sq_used, free(k))
                act.activation(sq[:, k % 2, :], h[:, k, :], ACT.Square).then_inc(sq_made, 1)
            act.wait_ge(sq_used, ready(KD - 1))
            inverse_root(act, [bank[ns + j][:, 0:n] for j, (c, n) in enumerate(splits)], [acc[:, c:c + n] for c, n in splits],
                         eps[:, 0:1], logs2, rstd2)
            for k in range(KD):
                act.wait_ge(u_made, k + 1)
                act.copy(u[0][:, k, 0:cols], y[:, k, 0:cols]).then_inc(u_hi, 1)

        @block.gpsimd
        def _(pool):
            pool.sem_inc(added, 2)
            pool.wait_ge(squared, ready(0))
            pool.tensor_copy(acc[:, :], sq[:, 0, :]).then_inc(added, 1)
            for k in range(1, KD):
                pool.wait_ge(squared, ready(k))
                pool.wait_ge(added, ready(k - 1))
                pool.tensor_tensor(acc[:, :], acc[:, :], sq[:, k % 2, :], ALU.add).then_inc(added, 1)
            for k in range(0, KD, 2):
                pool.wait_ge(u_hi, k + 1)
                pool.tensor_tensor(u[1][:, k, 0:cols], y[:, k, 0:cols], u[0][:, k, 0:cols], ALU.subtract)


def stage_ffn(nc, ctx, A, K, bank, u, inner_):
    wg_in, wu_in, hi_g, hi_u, lo_g, lo_u, gmm, umm, g_kept, conv1, conv2, conv3, gelu_made, inner_made = sems(
        ctx, nc, "f", "wg_in wu_in hi_g hi_u lo_g lo_u gmm umm g_kept conv1 conv2 conv3 gelu_made inner_made")
    w_in, hi_made, lo_made = (wg_in, wu_in), (hi_g, hi_u), (lo_g, lo_u)
    vec = K["vec"]
    sources = [A[n][0].rearrange("(k p) n -> p k n", p=P) for n in ("ffn_w_gate", "ffn_w_up")]
    cw, cb = VEC["conv_w"], VEC["conv_b"]
    with ExitStack() as inner:
        raw = buffer(inner, nc, "f_raw", [P, 2, KD, P])
        wh = buffer(inner, nc, "f_w_hi", [P, 2, KD, P], F32R)
        wl = buffer(inner, nc, "f_w_lo", [P, 2, KD, P], F32R)
        g = buffer(inner, nc, "f_gate", [P, LIVE])
        block = inner.enter_context(nc.Block())

        @block.sync
        def _(sp):
            with sp.Fori(0, KF) as n:
                for e in range(2):
                    sp.wait_ge(lo_made[e], n + 1)
                    sp.dma_start(raw[:, e, :, :], sources[e][:, :, ds(n * P, P)]).then_inc(w_in[e], 16)

        @block.gpsimd
        def _(pool):
            pool.sem_inc(lo_g, 1)
            pool.sem_inc(lo_u, 1)
            with pool.Fori(0, KF) as n:
                for e in range(2):
                    pool.wait_ge(hi_made[e], n + 1)
                    pool.tensor_tensor(wl[:, e, :, :], raw[:, e, :, :], wh[:, e, :, :], ALU.subtract).then_inc(lo_made[e], 1)

        @block.tensor
        def _(pe):
            pe.sem_inc(umm, 2)
            with pe.Fori(0, KF // 2) as i:
                for s in range(2):
                    n = 2 * i + s
                    pe.wait_ge(lo_g, n + 2)
                    pe.wait_ge(g_kept, n + 1)
                    for j, (c, w) in enumerate(LIVES):
                        m = product(pe, bank[j][:, 0:w], (wh[:, 0], wl[:, 0]), u, c, w)
                    m.then_inc(gmm, 1)
                    pe.wait_ge(lo_u, n + 2)
                    pe.wait_ge(inner_made, free(n))
                    for j, (c, w) in enumerate(SEQS):
                        m = product(pe, bank[3 + 2 * s + j][:, 0:w], (wh[:, 1], wl[:, 1]), u, TAPS - 1 + c, w)
                    m.then_inc(umm, 1)

        @block.scalar
        def _(act):
            act.sem_inc(g_kept, 1)

            def high(e, n):
                act.wait_ge(w_in[e], 16 * n + 16)
                act.copy(wh[:, e, :, :], raw[:, e, :, :]).then_inc(hi_made[e], 1)

            def step(n, more):
                act.wait_ge(gmm, n + 1)
                act.wait_ge(conv3, n + 1)
                for j, (c, w) in enumerate(LIVES):
                    a = act.copy(g[:, c:c + w], bank[j][:, 0:w])
                a.then_inc(g_kept, 1)
                if more:
                    high(0, n + 1)
                act.wait_ge(conv3, n + 2)
                tile = inner_[:, ds(n, 1), :]
                act.activation(tile, tile, ACT.Gelu_apprx_tanh).then_inc(gelu_made, 1)
                if more:
                    act.wait_ge(umm, ready(n))
                    high(1, n + 1)
            high(0, 0)
            high(1, 0)
            with act.Fori(0, KF - 1) as n:
                step(n, True)
            step(KF - 1, False)

        @block.vector
        def _(dve):
            dve.sem_inc(inner_made, 2)
            dve.sem_inc(conv3, 1)
            taps = vec[:, cw:cw + TAPS * KF].rearrange("p (j k) -> p j k", j=TAPS)
            with dve.Fori(0, KF // 2) as i:
                for s in range(2):
                    n = 2 * i + s
                    tile = inner_[:, ds(n, 1), :].rearrange("p a t -> p (a t)")
                    dve.wait_ge(g_kept, n + 2)
                    dve.tensor_scalar(tile, g[:, 0:SEQ], taps[:, 0, ds(n, 1)], vec[:, ds(n + cb, 1)], ALU.mult, ALU.add).then_inc(conv1, 1)
                    dve.wait_ge(conv1, n + 1)
                    dve.scalar_tensor_tensor(tile, g[:, 1:SEQ + 1], taps[:, 1, ds(n, 1)], tile, ALU.mult, ALU.add).then_inc(conv2, 1)
                    dve.wait_ge(conv2, n + 1)
                    dve.scalar_tensor_tensor(tile, g[:, 2:SEQ + 2], taps[:, 2, ds(n, 1)], tile, ALU.mult, ALU.add).then_inc(conv3, 1)
                    dve.wait_ge(gelu_made, n + 1)
                    dve.wait_ge(umm, ready(n))
                    for j, (c, w) in enumerate(SEQS):
                        part = inner_[:, ds(n, 1), c:c + w].rearrange("p a t -> p (a t)")
                        m = dve.tensor_tensor(part, part, bank[3 + 2 * s + j][:, 0:w], ALU.mult)
                    m.then_inc(inner_made, 1)


def stage_down(nc, ctx, A, K, bank, hidden, y, h, h_load, u):
    (w0, w1, hi_made, lo_made, used, mm, kept, squared, added, sums, logs, rstd_made, scaled, h_made, sq_made, sq_used, logs2, rstd2, h_in) = sems(
        ctx, nc, "d", "w0 w1 hi_made lo_made used mm kept squared added sums logs rstd_made scaled h_made sq_made sq_used logs2 rstd2 h_in")
    w_in = (w0, w1)
    ones, vec, eps = K["ones"], K["vec"], K["eps"]
    w = A["ffn_w_down"][0]
    PAIRS_K = KF // 2
    with ExitStack() as inner:
        raw = buffer(inner, nc, "d_raw", [P, 2, D])
        wh = buffer(inner, nc, "d_w_hi", [P, 2, D], F32R)
        wl = buffer(inner, nc, "d_w_lo", [P, 2, D], F32R)
        xh = buffer(inner, nc, "d_x_hi", [P, 2, BANK], F32R)
        xl = buffer(inner, nc, "d_x_lo", [P, 2, BANK], F32R)
        sq = buffer(inner, nc, "d_sq", [P, 2, SEQ])
        acc = buffer(inner, nc, "d_acc", [P, SEQ])
        rstd = raw[:, 0, :]
        sqs = sq[:, :, :].rearrange("p s (a n) -> p (s a) n", n=BANK)
        block = inner.enter_context(nc.Block())

        @block.sync
        def _(sp):
            sp.dma_start(h[:, :, :], h_load).then_inc(h_in, 16)
            for half in range(2):
                with sp.Fori(0, PAIRS_K) as i:
                    for s in range(2):
                        sp.wait_ge(lo_made, free(KF * half + 2 * i + s))
                        sp.dma_start(raw[:, s, :], w[ds((2 * i + s) * P, P), :]).then_inc(w_in[s], 16)

        @block.tensor
        def _(pe):
            pe.sem_inc(used, 2)

            def step(half, k, s, first=False, last=False):
                pe.wait_ge(lo_made, ready(KF * half + k))
                for j in range(KD):
                    if first and half:
                        pe.wait_ge(kept, j + 1)
                    col = slice(j * P, (j + 1) * P)
                    pe.matmul(bank[j][:, :], wh[:, s, col], xh[:, s, :], start=first, stop=False)
                    pe.matmul(bank[j][:, :], wh[:, s, col], xl[:, s, :], start=False, stop=False)
                    m = pe.matmul(bank[j][:, :], wl[:, s, col], xh[:, s, :], start=False, stop=last)
                    if last:
                        m.then_inc(mm, 1)
                if last:
                    pe.wait_ge(mm, KD * (half + 1))
                    pe.sem_inc(used, 1)
                else:
                    m.then_inc(used, 1)
            for half in range(2):
                step(half, 0, 0, first=True)
                step(half, 1, 1)
                with pe.Fori(1, PAIRS_K - 1) as i:
                    for s in range(2):
                        step(half, 2 * i + s, s)
                step(half, KF - 2, 0)
                step(half, KF - 1, 1, last=True)
            for half in range(2):
                pe.wait_ge(added, KD * (half + 1))
                pe.wait_ge(kept, 2 * KD)
                pe.matmul(bank[half][:, :], ones[:, :], acc[:, half * BANK:(half + 1) * BANK], start=True, stop=True).then_inc(sums, 1)
            pe.sem_inc(sq_used, 2)
            for k in range(KD):
                pe.wait_ge(sq_made, k + 1)
                for j, (c, n) in enumerate(SEQS):
                    m = pe.matmul(bank[2 + j][:, 0:n], ones[:, :], sq[:, k % 2, c:c + n], start=k == 0, stop=k == KD - 1)
                m.then_inc(sq_used, 1)

        @block.vector
        def _(dve):
            dve.sem_inc(lo_made, 2)

            def low(half, k, s):
                dve.wait_ge(hi_made, KF * half + k + 1)
                part = hidden[:, ds(k, 1), half * BANK:(half + 1) * BANK].rearrange("p a t -> p (a t)")
                dve.tensor_tensor(wl[:, s, :], raw[:, s, :], wh[:, s, :], ALU.subtract)
                dve.tensor_tensor(xl[:, s, :], part, xh[:, s, :], ALU.subtract).then_inc(lo_made, 1)

            def keep(half):
                for j in range(KD):
                    dve.wait_ge(mm, KD * half + j + 1)
                    dve.tensor_copy(y[:, j, half * BANK:(half + 1) * BANK], bank[j][:, :]).then_inc(kept, 1)
            with dve.Fori(0, PAIRS_K) as i:
                for s in range(2):
                    low(0, 2 * i + s, s)
            low(1, 0, 0)
            keep(0)
            low(1, 1, 1)
            with dve.Fori(1, PAIRS_K) as i:
                for s in range(2):
                    low(1, 2 * i + s, s)
            keep(1)
            dve.wait_ge(h_in, 16)
            dve.wait_ge(rstd_made, 2)
            dve.wait_ge(kept, 2 * KD)
            for k in range(KD):
                dve.scalar_tensor_tensor(y[:, k, :], y[:, k, :], vec[:, VEC["ffn_post"] + k:VEC["ffn_post"] + k + 1], rstd[:, :],
                                         ALU.mult, ALU.mult).then_inc(scaled, 1)
                dve.wait_ge(scaled, k + 1)
                dve.tensor_tensor(h[:, k, :], h[:, k, :], y[:, k, :], ALU.add).then_inc(h_made, 1)
            dve.wait_ge(rstd2, 2)
            dve.wait_ge(h_made, KD)
            for k in range(KD):
                dve.scalar_tensor_tensor(u[:, k, :], h[:, k, :], vec[:, VEC["norm_mix2"] + k:VEC["norm_mix2"] + k + 1], acc[:, :],
                                         ALU.mult, ALU.mult)

        @block.scalar
        def _(act):
            def high(half, k, s, n_in):
                act.wait_ge(w_in[s], 16 * n_in)
                act.wait_ge(used, free(KF * half + k))
                act.copy(wh[:, s, :], raw[:, s, :])
                part = hidden[:, ds(k, 1), half * BANK:(half + 1) * BANK].rearrange("p a t -> p (a t)")
                act.copy(xh[:, s, :], part).then_inc(hi_made, 1)

            def square(half):
                for j in range(KD):
                    n = KD * half + j
                    act.wait_ge(kept, n + 1)
                    if n >= 4:
                        act.wait_ge(added, n - 3)
                    act.activation(sqs[:, n % 4, :], y[:, j, half * BANK:(half + 1) * BANK], ACT.Square).then_inc(squared, 1)
            with act.Fori(0, PAIRS_K) as i:
                for s in range(2):
                    high(0, 2 * i + s, s, i + 1)
            high(1, 0, 0, PAIRS_K + 1)
            high(1, 1, 1, PAIRS_K + 1)
            square(0)
            with act.Fori(1, PAIRS_K) as i:
                for s in range(2):
                    high(1, 2 * i + s, s, i + PAIRS_K + 1)
            square(1)
            act.wait_ge(sums, 2)
            inverse_root(act, [bank[j][:, :] for j in range(2)], [rstd[:, c:c + n] for c, n in SEQS], eps[:, 0:1], logs, rstd_made)
            for k in range(KD):
                act.wait_ge(h_made, k + 1)
                act.wait_ge(sq_used, free(k))
                act.activation(sq[:, k % 2, :], h[:, k, :], ACT.Square).then_inc(sq_made, 1)
            act.wait_ge(sq_used, ready(KD - 1))
            inverse_root(act, [bank[2 + j][:, :] for j in range(2)], [acc[:, c:c + n] for c, n in SEQS], eps[:, 0:1], logs2, rstd2)

        @block.gpsimd
        def _(pool):
            for half in range(2):
                part = acc[:, half * BANK:(half + 1) * BANK]
                for j in range(KD):
                    n = KD * half + j
                    pool.wait_ge(squared, n + 1)
                    if j == 0:
                        pool.tensor_copy(part, sqs[:, n % 4, :]).then_inc(added, 1)
                    else:
                        pool.wait_ge(added, n)
                        pool.tensor_tensor(part, part, sqs[:, n % 4, :], ALU.add).then_inc(added, 1)


AHEAD = 3


def stage_in2(nc, ctx, A, K, bank, u, qa, ka, va, qk, vm, og, gi, gf):
    w0, w1, wv_in, wg_in, mm, taken, conv_used, conv, vmm, vkept, gmm, gates, cleared = sems(
        ctx, nc, "i", "w0 w1 wv_in wg_in mm taken conv_used conv vmm vkept gmm gates cleared")
    w_in = (w0, w1)
    vec = K["vec"]
    w = A["w_in_2"][0].rearrange("(k p) n -> p k n", p=P)
    QT, CT, OT = 4, 8, 4
    C0, V0, O0, G0 = 768, 1792, 2304, 2816
    cw, cb = VEC["conv_w2"], VEC["conv_b2"]
    with ExitStack() as inner:
        ring = buffer(inner, nc, "i_ring", [P, 2, KD, P])
        wv = buffer(inner, nc, "i_wv", [P, KD, 5 * P])
        wg = buffer(inner, nc, "i_wg", [P, KD, 2 * ML_H])
        gb = buffer(inner, nc, "i_gate_bias", [ML_H, 2])
        g = buffer(inner, nc, "i_conv_in", [P, 2, AHEAD + SEQ])
        block = inner.enter_context(nc.Block())

        @block.sync
        def _(sp):
            with sp.Fori(0, QT // 2) as i:
                for s in range(2):
                    sp.wait_ge(mm, free(2 * i + s))
                    for e in range(2):
                        sp.dma_start(ring[:, s, :, e * DH:(e + 1) * DH], w[:, :, ds((2 * i + s + QT * e) * DH, DH)]).then_inc(w_in[s], 16)
            with sp.Fori(0, CT // 2) as i:
                for s in range(2):
                    sp.wait_ge(mm, free(2 * i + s + QT))
                    sp.dma_start(ring[:, s, :, :], w[:, :, ds((2 * i + s) * P + C0, P)]).then_inc(w_in[s], 16)
            with sp.Fori(0, OT // 2) as i:
                for s in range(2):
                    sp.wait_ge(mm, free(2 * i + s + QT + CT))
                    sp.dma_start(ring[:, s, :, :], w[:, :, ds((2 * i + s) * P + O0, P)]).then_inc(w_in[s], 16)
            sp.wait_ge(mm, free(QT + CT + OT))
            sp.dma_start(ring[:, 0, :, :], w[:, :, 4 * P:5 * P]).then_inc(w_in[0], 16)
            sp.dma_start(wv[:, :, 0:4 * P], w[:, :, V0:V0 + 4 * P]).then_inc(wv_in, 16)
            sp.dma_start(wv[:, :, 4 * P:5 * P], w[:, :, 5 * P:6 * P]).then_inc(wv_in, 16)
            sp.dma_start(wg[:, :, :], w[:, :, G0:G0 + 2 * ML_H]).then_inc(wg_in, 16)
            sp.dma_start(gb[:, :], A["b_gates_2"][0].rearrange("(t h) -> h t", h=ML_H), allow_slow_non_contiguous=True).then_inc(wg_in, 16)

        @block.tensor
        def _(pe):
            pe.sem_inc(mm, 2)

            def tile(n, s, loaded):
                pe.wait_ge(w_in[s], loaded)
                pe.wait_ge(taken, free(n))
                for j, (c, m_) in enumerate(SEQS):
                    for t in range(KD):
                        m = pe.matmul(bank[2 * s + j][:, 0:m_], ring[:, s, t, :], u[:, t, c:c + m_], start=t == 0, stop=t == KD - 1)
                m.then_inc(mm, 1)
            with pe.Fori(0, QT // 2) as i:
                for s in range(2):
                    tile(2 * i + s, s, 32 * i + 32)
            with pe.Fori(0, (CT + OT) // 2) as i:
                for s in range(2):
                    tile(2 * i + s + QT, s, 16 * i + 16 * QT + 16)
            tile(QT + CT + OT, 0, 16 * (QT + (CT + OT) // 2 + 1))
            pe.wait_ge(wv_in, 32)
            for c in range(NB):
                pe.wait_ge(vkept, free(c))
                for t in range(KD):
                    pe.matmul(bank[4 + c % 2][:, :], u[:, t, c * P:(c + 1) * P], wv[:, t, 0:4 * P], start=t == 0, stop=t == KD - 1)
                for t in range(KD):
                    m = pe.matmul(bank[6 + c % 2][:, 0:P], u[:, t, c * P:(c + 1) * P], wv[:, t, 4 * P:5 * P], start=t == 0, stop=t == KD - 1)
                m.then_inc(vmm, 1)
            pe.wait_ge(wg_in, 32)
            pe.wait_ge(taken, ready(QT + CT + OT))
            for e in range(2):
                for j, (c, n) in enumerate(SEQS):
                    for t in range(KD):
                        m = pe.matmul(bank[2 * e + j][0:ML_H, 0:n], wg[:, t, e * ML_H:(e + 1) * ML_H], u[:, t, c:c + n], start=t == 0, stop=t == KD - 1)
            m.then_inc(gmm, 1)

        @block.scalar
        def _(act):
            act.sem_inc(taken, 2)
            with act.Fori(0, QT // 2) as i:
                for s in range(2):
                    act.wait_ge(mm, ready(2 * i + s))
                    for j, (c, n) in enumerate(SEQS):
                        a = act.copy(qa[:, ds(2 * i + s, 1), c:c + n], bank[2 * s + j][:, 0:n])
                    a.then_inc(taken, 1)
            with act.Fori(0, CT // 2) as i:
                for s in range(2):
                    n_ = 2 * i + s
                    act.wait_ge(mm, ready(n_ + QT))
                    act.wait_ge(conv_used, free(n_))
                    for j, (c, n) in enumerate(SEQS):
                        a = act.copy(g[:, s, AHEAD + c:AHEAD + c + n], bank[2 * s + j][:, 0:n])
                    a.then_inc(taken, 1)
                    act.wait_ge(conv_used, ready(n_))
                    act.activation(qk[:, ds(n_, 1), :], qk[:, ds(n_, 1), :], ACT.Silu)
            with act.Fori(0, OT // 2) as i:
                for s in range(2):
                    act.wait_ge(mm, ready(2 * i + s + QT + CT))
                    for j, (c, n) in enumerate(SEQS):
                        a = act.activation(og[:, ds(2 * i + s, 1), c:c + n], bank[2 * s + j][:, 0:n], ACT.Sigmoid)
                    a.then_inc(taken, 1)
            act.wait_ge(mm, ready(QT + CT + OT))
            for j, (c, n) in enumerate(SEQS):
                a = act.copy(ka[:, P + c:P + c + n], bank[j][:, 0:n])
            a.then_inc(taken, 1)
            act.wait_ge(gmm, 1)
            for j, (c, n) in enumerate(SEQS):
                act.activation(gi[:, c:c + n], bank[j][0:ML_H, 0:n], ACT.Identity, bias=gb[:, 0:1])
                act.activation(gf[:, c:c + n], bank[2 + j][0:ML_H, 0:n], ACT.Identity, bias=gb[:, 1:2])

        @block.vector
        def _(dve):
            dve.memset(g[:, :, 0:AHEAD], 0.0).then_inc(cleared, 1)
            dve.memset(ka[:, 0:P], 0.0)
            dve.memset(va[:, 0, :], 0.0)
            dve.sem_inc(conv_used, 2)
            dve.sem_inc(vkept, 2)
            taps = vec[:, cw:cw + 4 * CT].rearrange("p (j k) -> p j k", j=4)
            dve.wait_ge(cleared, 1)
            with dve.Fori(0, CT // 2) as i:
                for s in range(2):
                    n = 2 * i + s
                    dve.wait_ge(taken, ready(n + QT))
                    t0 = qk[:, ds(n, 1), :].rearrange("p a t -> p (a t)")
                    dve.tensor_scalar(t0, g[:, s, 0:SEQ], taps[:, 0, ds(n, 1)], vec[:, ds(n + cb, 1)], ALU.mult, ALU.add).then_inc(conv, 1)
                    for j in range(1, 4):
                        dve.wait_ge(conv, 3 * n + j)
                        m = dve.scalar_tensor_tensor(t0, g[:, s, j:SEQ + j], taps[:, j, ds(n, 1)], t0, ALU.mult, ALU.add)
                        m.then_inc(conv if j < 3 else conv_used, 1)
            for c in range(NB):
                dve.wait_ge(vmm, c + 1)
                dve.tensor_copy(vm[:, c, :], bank[4 + c % 2][:, :])
                dve.tensor_copy(va[:, c + 1, :], bank[6 + c % 2][:, 0:P]).then_inc(vkept, 1)


def stage_attention(nc, ctx, A, K, bank, qa, ka, va, out, spare):
    (sinks_in, made, staged, scored, logit, maxed, bias_made, exped, turned, pt_kept, pvmm, scaled, root, normed, back, back_kept, small) = sems(
        ctx, nc, "a", "sinks_in made staged scored logit maxed bias_made exped turned pt_kept pvmm scaled root normed back back_kept small")
    ident, vec, eps = K["ident"], K["vec"], K["eps"]
    KEYS = 2 * WIN
    with ExitStack() as inner:
        sinks = buffer(inner, nc, "sinks", [P, QH])
        dist = buffer(inner, nc, "dist", [P, KEYS])
        bias = spare.rearrange("p (f h k) -> p f h k", f=2, k=KEYS)
        qc = buffer(inner, nc, "q_block", [P, 2, 4, P])
        kc = buffer(inner, nc, "k_window", [P, 2, KEYS])
        lg = buffer(inner, nc, "logits", [P, 2, QH, KEYS])
        pt = buffer(inner, nc, "probs_t", [P, 2 * QH, P])
        mx = buffer(inner, nc, "row_max", [P, 2, 3, QH])
        den = buffer(inner, nc, "row_den", [P, 2, 2, QH])
        att = buffer(inner, nc, "att_rows", [P, QH * DH])
        att2 = buffer(inner, nc, "att_normed", [P, QH * DH])
        ss = buffer(inner, nc, "att_ss", [P, 4])
        block = inner.enter_context(nc.Block())

        @block.sync
        def _(sp):
            sp.dma_start(sinks[:, :], A["att_sinks_2"].to_broadcast([P, QH])).then_inc(sinks_in, 16)
            sp.wait_ge(sinks_in, 16)

        @block.gpsimd
        def _(pool):
            pool.iota(dist[:, :], [[-1, KEYS]], base=WIN, channel_multiplier=1, allow_small_or_imprecise_dtypes=True).then_inc(made, 1)
            pool.wait_ge(made, 1)
            n = 1
            for h in range(QH):
                slope = 2.0 ** (-8.0 * (h + 1) / QH)
                pool.tensor_scalar(bias[:, 1, h, :], dist[:, :], -slope, None, ALU.mult).then_inc(made, 1)
            pool.wait_ge(made, QH + 1)
            v = bias[:, 1, :, :]
            pool.affine_select(v, v, [[0, QH], [-1, KEYS]], ALU.is_ge, NEG, base=WIN, channel_multiplier=1).then_inc(made, 1)
            pool.wait_ge(made, QH + 2)
            pool.affine_select(v, v, [[0, QH], [1, KEYS]], ALU.is_gt, NEG, base=0, channel_multiplier=-1).then_inc(made, 1)
            pool.wait_ge(made, QH + 3)
            pool.affine_select(bias[:, 0, :, :], v, [[0, QH], [1, KEYS]], ALU.is_ge, NEG, base=-WIN, channel_multiplier=0).then_inc(made, 1)

            def stage(n, s):
                pool.wait_ge(scored, free(n))
                pool.tensor_copy(qc[:, s, :, :], qa[:, :, ds(n * P, P)]).then_inc(staged, 1)
                pool.tensor_copy(kc[:, s, :], ka[:, ds(n * P, KEYS)]).then_inc(staged, 1)
            with pool.Fori(0, NB // 2) as i:
                for s in range(2):
                    stage(2 * i + s, s)

        @block.tensor
        def _(pe):
            pe.sem_inc(scored, 2)

            def scores(n, s):
                pe.wait_ge(staged, 2 * n + 2)
                pe.wait_ge(logit, 4 * n + 4)
                for e in range(2):
                    for j in range(4):
                        m = pe.matmul(bank[2 * e + j // 2][:, (j % 2) * KEYS:(j % 2 + 1) * KEYS], qc[e * DH:(e + 1) * DH, s, j, :],
                                      kc[e * DH:(e + 1) * DH, s, :], start=True, stop=True)
                m.then_inc(scored, 1)

            def output(n, s):
                for g in range(4):
                    pe.wait_ge(exped, 8 * n + 2 * g + 2)
                    pe.wait_ge(pt_kept, 4 * n + g + 1)
                    for r in range(4):
                        m = pe.transpose(bank[4 + g % 2][:, r * P:(r + 1) * P], lg[:, s, 2 * g + r // 2, (r % 2) * P:(r % 2 + 1) * P], ident[:, :])
                    m.then_inc(turned, 1)
                pe.wait_ge(pt_kept, 4 * n + 6)
                pe.wait_ge(scaled, n + 1)
                for h in range(QH):
                    kv = h // (QH // 2)
                    for r in range(2):
                        m = pe.matmul(bank[6][:, h * DH:(h + 1) * DH], pt[:, 2 * h + r, :],
                                      va[:, ds(n + r, 1), kv * DH:(kv + 1) * DH], start=r == 0, stop=r == 1)
                m.then_inc(pvmm, 1)
                pe.wait_ge(normed, n + 1)
                pe.wait_ge(back_kept, n + 1)
                for j in range(4):
                    m = pe.transpose(bank[7][:, j * P:(j + 1) * P], att2[:, j * P:(j + 1) * P], ident[:, :])
                m.then_inc(back, 1)
            scores(0, 0)
            with pe.Fori(0, NB // 2 - 1) as i:
                for s in range(2):
                    scores(2 * i + s + 1, 1 - s)
                    output(2 * i + s, s)
            scores(NB - 1, 1)
            output(NB - 2, 0)
            output(NB - 1, 1)

        @block.vector
        def _(dve):
            dve.sem_inc(logit, 4)
            dve.sem_inc(pt_kept, 2)
            dve.sem_inc(scaled, 1)
            dve.wait_ge(made, QH + 4)
            dve.wait_ge(sinks_in, 16)

            def logits(n, s, first):
                dve.wait_ge(scored, ready(n))
                for b in range(4):
                    dve.scalar_tensor_tensor(lg[:, s, 2 * b:2 * b + 2, :], bank[b][:, :].rearrange("p (h t) -> p h t", h=2), DH ** -0.5,
                                             bias[:, 1 - first, 2 * b:2 * b + 2, :], ALU.mult, ALU.add).then_inc(logit, 1)
                dve.wait_ge(logit, 4 * n + 8)
                dve.tensor_reduce(mx[:, s, 0, :], lg[:, s, :, :], AX.X, ALU.max).then_inc(maxed, 1)
                dve.wait_ge(maxed, 3 * n + 1)
                dve.tensor_tensor(mx[:, s, 0, :], mx[:, s, 0, :], sinks[:, :], ALU.max).then_inc(maxed, 1)
                dve.wait_ge(maxed, 3 * n + 2)
                dve.tensor_scalar(mx[:, s, 1, :], mx[:, s, 0, :], -1.0, None, ALU.mult)
                dve.tensor_tensor(mx[:, s, 2, :], sinks[:, :], mx[:, s, 0, :], ALU.subtract).then_inc(maxed, 1)

            def output(n, s):
                for g in range(4):
                    dve.wait_ge(turned, 4 * n + g + 1)
                    dve.tensor_copy(pt[:, 4 * g:4 * g + 4, :], bank[4 + g % 2][:, :].rearrange("p (h t) -> p h t", h=4)).then_inc(pt_kept, 1)
                dve.wait_ge(exped, 8 * n + 8)
                dve.wait_ge(root, n + 1)
                dve.tensor_tensor(den[:, s, 0, :], den[:, s, 0, :], mx[:, s, 2, :], ALU.add).then_inc(small, 1)
                dve.wait_ge(small, 2 * n + 1)
                dve.reciprocal(den[:, s, 1, :], den[:, s, 0, :]).then_inc(small, 1)
                dve.wait_ge(small, 2 * n + 2)
                dve.wait_ge(pvmm, n + 1)
                dve.tensor_tensor(att[:, :].rearrange("p (h d) -> p h d", d=DH), bank[6][:, :].rearrange("p (h d) -> p h d", d=DH),
                                  den[:, s, 1, :].unsqueeze(2).to_broadcast([P, QH, DH]), ALU.mult).then_inc(scaled, 1)
            logits(0, 0, 1)
            logits(1, 1, 0)
            output(0, 0)
            with dve.Fori(0, NB // 2 - 1) as i:
                for s in range(2):
                    logits(2 * i + s + 2, s, 0)
                    output(2 * i + s + 1, 1 - s)
            output(NB - 1, 1)

        @block.scalar
        def _(act):
            act.sem_inc(back_kept, 1)
            ga = VEC["norm_att"]

            def exponentials(n, s):
                act.wait_ge(maxed, 3 * n + 3)
                for h in range(QH):
                    act.activation(lg[:, s, h, :], lg[:, s, h, :], ACT.Exp, bias=mx[:, s, 1, h:h + 1], accum_out=den[:, s, 0, h:h + 1]).then_inc(exped, 1)
                act.activation(mx[:, s, 2, :], mx[:, s, 2, :], ACT.Exp).then_inc(root, 1)

            def output(n, s):
                act.wait_ge(scaled, n + 2)
                act.activation(att2[:, :], att[:, :], ACT.Square, accum_out=ss[:, 0:1]).then_inc(bias_made, 1)
                act.wait_ge(bias_made, 3 * n + 1)
                act.activation(ss[:, 1:2], ss[:, 0:1], ACT.Ln, bias=eps[:, 0:1], scale=1.0 / (QH * DH)).then_inc(bias_made, 1)
                act.wait_ge(bias_made, 3 * n + 2)
                act.activation(ss[:, 2:3], ss[:, 1:2], ACT.Exp, scale=-0.5).then_inc(bias_made, 1)
                act.wait_ge(bias_made, 3 * n + 3)
                act.mul(att2[:, :], att[:, :], ss[:, 2:3]).then_inc(normed, 1)
                act.wait_ge(back, n + 1)
                for j in range(4):
                    a = act.mul(out[:, j, ds(n * P, P)], bank[7][:, j * P:(j + 1) * P], vec[:, ga + j:ga + j + 1])
                a.then_inc(back_kept, 1)
            exponentials(0, 0)
            with act.Fori(0, NB // 2 - 1) as i:
                for s in range(2):
                    exponentials(2 * i + s + 1, 1 - s)
                    output(2 * i + s, s)
            exponentials(NB - 1, 1)
            output(NB - 2, 0)
            output(NB - 1, 1)


def stage_mlstm(nc, ctx, A, K, bank, qk, vm, og, gi, gf, out):
    (rows, act_rows, sel_made, aturned, a_kept, staged, fmm, used, rm_made, dec, gate_made, s_made, kt, kw_made, state, nmm, dmm, hmade, h2, cmm, nbmm,
     floor, recip, sq_made, sums, logs, rstd, gated, fin, w_made, wexp, den_abs) = sems(
        ctx, nc, "m", "rows act_rows sel_made aturned a_kept staged fmm used rm_made dec gate_made s_made kt kw_made state nmm dmm hmade h2 cmm nbmm "
        "floor recip sq_made sums logs rstd gated fin w_made wexp den_abs")
    ident, ones, vec, eps, causal, reset = (K[n] for n in ("ident", "ones", "vec", "eps", "causal", "reset"))
    with ExitStack() as inner:
        lf = buffer(inner, nc, "m_lf", [ML_H, SEQ])
        m_ = buffer(inner, nc, "m_m", [ML_H, SEQ])
        b = buffer(inner, nc, "m_b", [ML_H, SEQ])
        a = buffer(inner, nc, "m_a", [ML_H, SEQ])
        row3 = buffer(inner, nc, "m_rows", [ML_H, NB, 3, P])
        sel = buffer(inner, nc, "m_sel", [ML_H, ML_H, P])
        at = buffer(inner, nc, "m_a_tok", [P, NB, ML_H])
        kc = buffer(inner, nc, "m_k", [P, 2, BANK])
        vc = buffer(inner, nc, "m_v", [P, 2, BANK])
        rm = buffer(inner, nc, "m_r", [P, BANK])
        dd = buffer(inner, nc, "m_d", [P, BANK])
        sc = buffer(inner, nc, "m_s", [P, BANK])
        ew = buffer(inner, nc, "m_ew", [P, BANK])
        em = buffer(inner, nc, "m_em", [P, BANK])
        qw = buffer(inner, nc, "m_qw", [P, BANK])
        kw = buffer(inner, nc, "m_kw", [P, BANK])
        ws = buffer(inner, nc, "m_ws", [P, ML_H])
        st = buffer(inner, nc, "m_c", [P, 2, BANK])
        nst = buffer(inner, nc, "m_n", [P, 2, BANK])
        den = buffer(inner, nc, "m_den", [P, BANK])
        sq, rs = (t[:, :, :].rearrange("p s n -> p (s n)") for t in (kc, vc))
        block = inner.enter_context(nc.Block())

        def heads(ap):
            return ap.rearrange("p (h t) -> p h t", t=P)

        @block.gpsimd
        def _(pool):
            pool.memset(sel[:, :, :], 1.0).then_inc(sel_made, 1)
            pool.wait_ge(sel_made, 1)
            pool.affine_select(sel[:, :, :], sel[:, :, :], [[-1, ML_H], [0, P]], ALU.is_equal, 0.0, base=0, channel_multiplier=1).then_inc(sel_made, 1)
            with pool.Fori(0, NB // 2) as i:
                for s in range(2):
                    c = 2 * i + s
                    pool.wait_ge(nbmm, free(c))
                    pool.tensor_copy(heads(kc[:, s, :]), qk[:, 4:8, ds(c * P, P)]).then_inc(staged, 1)
                    pool.tensor_copy(vc[:, s, :], vm[:, ds(c, 1), :].rearrange("p a n -> p (a n)")).then_inc(staged, 1)

        @block.vector
        def _(dve):
            n = 0

            def then(ins):
                nonlocal n
                n += 1
                ins.then_inc(rows, 1)
                dve.wait_ge(rows, n)
            dve.wait_ge(act_rows, 3)
            then(dve.scalar_tensor_tensor(lf[:, :], gf[:, :], 0.0, lf[:, :], ALU.min, ALU.subtract))
            then(dve.tensor_tensor_scan(m_[:, :], lf[:, :], gi[:, :], 0.0, ALU.add, ALU.max))
            for j in range(SEQ // BANK):
                c = slice(j * BANK, (j + 1) * BANK)
                then(dve.tensor_tensor_scan(b[:, c], reset[0:ML_H, :], lf[:, c], 0.0, ALU.mult, ALU.add))
            b3, m3 = (x[:, :].rearrange("p (c t) -> p c t", t=P) for x in (b, m_))
            then(dve.tensor_tensor(a[:, :], gi[:, :], b[:, :], ALU.subtract))
            then(dve.tensor_tensor(row3[:, :, 0, :], b3, m3, ALU.subtract))
            then(dve.tensor_copy(row3[:, 0, 1, :], row3[:, 0, 0, :]))
            then(dve.tensor_tensor(row3[:, 1:, 1, :], row3[:, 1:, 0, :], m3[:, 0:NB - 1, P - 1:P].to_broadcast([ML_H, NB - 1, P]), ALU.add))
            then(dve.tensor_scalar(row3[:, :, 2, :], m3, -1.0, None, ALU.mult))
            dve.memset(st[:, 0, :], 0.0)
            dve.memset(nst[:, 0, :], 0.0).then_inc(state, 1)
            dve.wait_ge(aturned, 1)
            dve.tensor_copy(at[:, :, :], bank[7][:, 0:NB * ML_H].rearrange("p (c h) -> p c h", h=ML_H)).then_inc(a_kept, 1)
            dve.wait_ge(a_kept, 1)

            def front(c, s):
                dve.wait_ge(fmm, c + 1)
                dve.tensor_tensor(heads(rm[:, :]), heads(bank[1][:, :]), causal[:, :].unsqueeze(1).to_broadcast([P, ML_H, P]), ALU.add)
                dve.tensor_tensor(ws[:, :], at[:, ds(c, 1), :].rearrange("p a h -> p (a h)"), heads(bank[1][:, :])[:, :, P - 1], ALU.add).then_inc(rm_made, 1)
                dve.wait_ge(dec, c + 1)
                dve.scalar_tensor_tensor(sc[:, :], dd[:, :], P ** -0.5, bank[0][:, :], ALU.mult, ALU.mult).then_inc(s_made, 1)
                dve.wait_ge(gate_made, c + 1)
                dve.scalar_tensor_tensor(heads(qw[:, :]), qk[:, 0:4, ds(c * P, P)], P ** -0.5, heads(ew[:, :]), ALU.mult, ALU.mult).then_inc(s_made, 1)

            def back(c, s):
                dve.wait_ge(den_abs, c + 1)
                dve.tensor_tensor(den[:, :], den[:, :], em[:, :], ALU.max).then_inc(floor, 1)
                dve.wait_ge(floor, c + 1)
                dve.reciprocal(den[:, :], den[:, :]).then_inc(recip, 1)
                dve.wait_ge(recip, c + 1)
                dve.tensor_tensor(out[:, 4:8, ds(c * P, P)], heads(bank[5][:, :]), heads(den[:, :]), ALU.mult).then_inc(hmade, 1)
                dve.wait_ge(nbmm, ready(c))
                for h in range(ML_H):
                    col = slice(h * P, (h + 1) * P)
                    decay = ew[:, (h + 1) * P - 1:(h + 1) * P]
                    dve.scalar_tensor_tensor(st[:, 1 - s, col], st[:, s, col], decay, bank[7][:, col], ALU.mult, ALU.add)
                    x = dve.scalar_tensor_tensor(nst[:, 1 - s, col], nst[:, s, col], decay, bank[4][:, col], ALU.mult, ALU.add)
                x.then_inc(state, 1)
            with dve.Fori(0, NB // 2) as i:
                for s in range(2):
                    front(2 * i + s, s)
                    back(2 * i + s, s)
            dve.wait_ge(hmade, NB)
            for h in range(ML_H):
                dve.tensor_tensor(out[:, 4 + h, :], out[:, 4 + h, :], og[:, h, :], ALU.mult).then_inc(gated, 1)
            for h in range(ML_H):
                dve.wait_ge(rstd, 2 * h + 2)
                dve.scalar_tensor_tensor(out[:, 4 + h, :], out[:, 4 + h, :], vec[:, VEC["norm_ml"] + h:VEC["norm_ml"] + h + 1], rs[:, :],
                                         ALU.mult, ALU.mult).then_inc(fin, 1)

        @block.scalar
        def _(act):
            act.activation(lf[:, :], gf[:, :], ACT.Abs).then_inc(act_rows, 1)
            act.wait_ge(act_rows, 1)
            act.activation(lf[:, :], lf[:, :], ACT.Exp, scale=-1.0).then_inc(act_rows, 1)
            act.wait_ge(act_rows, 2)
            act.activation(lf[:, :], lf[:, :], ACT.Ln, bias=1.0).then_inc(act_rows, 1)

            def chunk(c, s):
                act.wait_ge(rm_made, c + 1)
                for h in range(ML_H):
                    x = act.activation(dd[:, h * P:(h + 1) * P], rm[:, h * P:(h + 1) * P], ACT.Exp,
                                       bias=at[:, ds(c, 1), h:h + 1].rearrange("p a h -> p (a h)"))
                x.then_inc(dec, 1)
                act.activation(ws[:, :], ws[:, :], ACT.Exp).then_inc(wexp, 1)
                act.wait_ge(state, c + 1)
                act.activation(ew[:, :], bank[2][:, :], ACT.Exp)
                act.activation(em[:, :], bank[3][:, :], ACT.Exp).then_inc(gate_made, 1)
                act.wait_ge(kt, c + 1)
                act.wait_ge(wexp, c + 1)
                for h in range(ML_H):
                    x = act.mul(kw[:, h * P:(h + 1) * P], bank[4][:, h * P:(h + 1) * P], ws[:, h:h + 1])
                x.then_inc(kw_made, 1)
                act.wait_ge(dmm, c + 1)
                act.activation(den[:, :], bank[6][:, :], ACT.Abs).then_inc(den_abs, 1)
            with act.Fori(0, NB // 2) as i:
                for s in range(2):
                    chunk(2 * i + s, s)
            for h in range(ML_H):
                act.wait_ge(gated, h + 1)
                if h:
                    act.wait_ge(sums, h)
                act.activation(sq[:, :], out[:, 4 + h, :], ACT.Square).then_inc(sq_made, 1)
                act.wait_ge(sums, h + 1)
                if h:
                    act.wait_ge(fin, h)
                inverse_root(act, [bank[j][:, :] for j in range(2)], [rs[:, c:c + n] for c, n in SEQS], eps[:, 0:1], logs, rstd, at=2 * h, width=P)

        @block.tensor
        def _(pe):
            pe.sem_inc(nbmm, 2)
            pe.wait_ge(rows, 9)
            for c in range(NB):
                m = pe.transpose(bank[7][:, c * ML_H:(c + 1) * ML_H], a[:, c * P:(c + 1) * P], ident[0:ML_H, 0:ML_H])
            m.then_inc(aturned, 1)
            pe.wait_ge(sel_made, 2)
            pe.wait_ge(a_kept, 1)

            def front(c, s):
                pe.wait_ge(staged, 2 * c + 2)
                for h in range(ML_H):
                    col = slice(h * P, (h + 1) * P)
                    pe.matmul(bank[0][:, col], kc[:, s, col], qk[:, h, ds(c * P, P)], start=True, stop=True)
                for r in range(3):
                    for h in range(ML_H):
                        m = pe.matmul(bank[1 + r][:, h * P:(h + 1) * P], sel[:, h, :], row3[:, ds(c, 1), r, :], start=True, stop=True)
                m.then_inc(fmm, 1)
                for h in range(ML_H):
                    m = pe.transpose(bank[4][:, h * P:(h + 1) * P], kc[:, s, h * P:(h + 1) * P], ident[:, :])
                m.then_inc(kt, 1)

            def back(c, s):
                pe.wait_ge(s_made, 2 * c + 2)
                pe.wait_ge(state, c + 1)
                for h in range(ML_H):
                    col = slice(h * P, (h + 1) * P)
                    pe.matmul(bank[6][:, col], ones[:, :], sc[:, col], start=True, stop=False)
                    m = pe.matmul(bank[6][:, col], nst[:, s, col], qw[:, col], start=False, stop=True)
                for h in range(ML_H):
                    col = slice(h * P, (h + 1) * P)
                    pe.matmul(bank[5][:, col], vc[:, s, col], sc[:, col], start=True, stop=False)
                    m = pe.matmul(bank[5][:, col], st[:, s, col], qw[:, col], start=False, stop=True)
                m.then_inc(dmm, 1)
                pe.wait_ge(kw_made, c + 1)
                for h in range(ML_H):
                    col = slice(h * P, (h + 1) * P)
                    pe.matmul(bank[7][:, col], kw[:, col], vc[:, s, col], start=True, stop=True)
                for h in range(ML_H):
                    m = pe.matmul(bank[4][:, h * P:(h + 1) * P], kw[:, h * P:(h + 1) * P], ones[:, :], start=True, stop=True)
                m.then_inc(nbmm, 1)
                pe.wait_ge(state, c + 2)
            with pe.Fori(0, NB // 2) as i:
                for s in range(2):
                    front(2 * i + s, s)
                    back(2 * i + s, s)
            for h in range(ML_H):
                pe.wait_ge(sq_made, h + 1)
                if h:
                    pe.wait_ge(rstd, 2 * h)
                for j, (c, n) in enumerate(SEQS):
                    m = pe.matmul(bank[j][:, 0:n], ones[:, :], sq[:, c:c + n], start=True, stop=True)
                m.then_inc(sums, 1)


def stage_residual(nc, ctx, A, K, bank, name, weights, tiles_in, x, h, u=None, u_gain=None):
    w0, w1, mm, made, squared, added, sums, logs, rstd_made = sems(ctx, nc, name, "w0 w1 mm made squared added sums logs rstd_made")
    w_in = (w0, w1)
    ones, vec, eps = K["ones"], K["vec"], K["eps"]
    w = weights.rearrange("(k p) n -> p k n", p=P)
    with ExitStack() as inner:
        ring = buffer(inner, nc, name + "_ring", [P, 2, tiles_in, P])
        sq = buffer(inner, nc, name + "_sq", [P, 2, SEQ])
        acc = buffer(inner, nc, name + "_acc", [P, SEQ])
        block = inner.enter_context(nc.Block())

        @block.sync
        def _(sp):
            with sp.Fori(0, KD // 2) as i:
                for s in range(2):
                    sp.wait_ge(mm, free(2 * i + s))
                    sp.dma_start(ring[:, s, :, :], w[:, :, ds((2 * i + s) * P, P)]).then_inc(w_in[s], 16)

        @block.tensor
        def _(pe):
            pe.sem_inc(mm, 2)
            with pe.Fori(0, KD // 2) as i:
                for s in range(2):
                    pe.wait_ge(w_in[s], 16 * i + 16)
                    pe.wait_ge(made, free(2 * i + s))
                    for j, (c, n) in enumerate(SEQS):
                        for t in range(tiles_in):
                            m = pe.matmul(bank[2 * s + j][:, 0:n], ring[:, s, t, :], x[:, t, c:c + n], start=t == 0, stop=t == tiles_in - 1)
                    m.then_inc(mm, 1)
            if u is not None:
                pe.wait_ge(added, ready(KD - 1))
                for j, (c, n) in enumerate(SEQS):
                    m = pe.matmul(bank[4 + j][:, 0:n], ones[:, :], acc[:, c:c + n], start=True, stop=True)
                m.then_inc(sums, 1)

        @block.vector
        def _(dve):
            dve.sem_inc(made, 2)
            with dve.Fori(0, KD // 2) as i:
                for s in range(2):
                    dve.wait_ge(mm, ready(2 * i + s))
                    for j, (c, n) in enumerate(SEQS):
                        hc = h[:, ds(2 * i + s, 1), c:c + n].rearrange("p a t -> p (a t)")
                        m = dve.tensor_tensor(hc, hc, bank[2 * s + j][:, 0:n], ALU.add)
                    m.then_inc(made, 1)
            if u is not None:
                dve.wait_ge(rstd_made, 2)
                dve.wait_ge(made, ready(KD - 1))
                for k in range(KD):
                    dve.scalar_tensor_tensor(u[:, k, 0:SEQ], h[:, k, :], vec[:, VEC[u_gain] + k:VEC[u_gain] + k + 1], sq[:, 0, :],
                                             ALU.mult, ALU.mult)

        if u is not None:
            @block.scalar
            def _(act):
                act.sem_inc(squared, 2)
                with act.Fori(0, KD // 2) as i:
                    for s in range(2):
                        act.wait_ge(made, ready(2 * i + s))
                        act.wait_ge(added, free(2 * i + s))
                        act.activation(sq[:, s, :], h[:, ds(2 * i + s, 1), :], ACT.Square).then_inc(squared, 1)
                act.wait_ge(sums, 1)
                inverse_root(act, [bank[4 + j][:, 0:n] for j, (c, n) in enumerate(SEQS)], [sq[:, 0, c:c + n] for c, n in SEQS],
                             eps[:, 0:1], logs, rstd_made)

            @block.gpsimd
            def _(pool):
                pool.sem_inc(added, 2)
                pool.wait_ge(squared, ready(0))
                pool.tensor_copy(acc[:, :], sq[:, 0, :]).then_inc(added, 1)
                for k in range(1, KD):
                    pool.wait_ge(squared, ready(k))
                    pool.wait_ge(added, ready(k - 1))
                    pool.tensor_tensor(acc[:, :], acc[:, :], sq[:, k % 2, :], ALU.add).then_inc(added, 1)


def stage_memory(nc, ctx, A, K, bank, mk, mv):
    m_in, wk0, wk1, wv_in, squared, normed, turned, kept, kmm, k_kept, vmm, v_kept = sems(
        ctx, nc, "e", "m_in wk0 wk1 wv_in squared normed turned kept kmm k_kept vmm v_kept")
    ident, vec, eps = K["ident"], K["vec"], K["eps"]
    w = A["w_ckv_2"][0].rearrange("(k p) n -> p k n", p=P)
    MB = MEM // P
    gm = VEC["norm_mem"]
    with ExitStack() as inner:
        rows = buffer(inner, nc, "e_rows", [P, MB, D])
        sq = buffer(inner, nc, "e_sq", [P, MB, D])
        ss = buffer(inner, nc, "e_ss", [P, MB, 3])
        mt = buffer(inner, nc, "e_mem", [P, KD, MEM])
        wk = buffer(inner, nc, "e_wk", [P, KD, 4 * P])
        wv = buffer(inner, nc, "e_wv", [P, KD, 4 * P])
        block = inner.enter_context(nc.Block())

        @block.sync
        def _(sp):
            sp.dma_start(rows[:, :, :], A["mem_2"][0].rearrange("(b p) d -> p b d", p=P)).then_inc(m_in, 16)
            sp.dma_start(wk[:, :, :], w[:, :, 0:4 * P]).then_inc(wk0, 16)
            sp.dma_start(wv[:, :, :], w[:, :, 4 * P:8 * P]).then_inc(wv_in, 16)

        @block.scalar
        def _(act):
            act.wait_ge(m_in, 16)
            for b in range(MB):
                act.activation(sq[:, b, :], rows[:, b, :], ACT.Square, accum_out=ss[:, b, 0:1]).then_inc(squared, 1)
            act.wait_ge(squared, MB)
            act.activation(ss[:, :, 1], ss[:, :, 0], ACT.Ln, bias=eps[:, 0:1], scale=1.0 / D).then_inc(squared, 1)
            act.wait_ge(squared, MB + 1)
            act.activation(ss[:, :, 2], ss[:, :, 1], ACT.Exp, scale=-0.5).then_inc(squared, 1)
            act.wait_ge(squared, MB + 2)
            for b in range(MB):
                act.mul(rows[:, b, :], rows[:, b, :], ss[:, b, 2:3]).then_inc(normed, 1)

        @block.tensor
        def _(pe):
            pe.wait_ge(normed, MB)
            for k in range(KD):
                if k >= 4:
                    pe.wait_ge(kept, k - 3)
                for b in range(MB):
                    m = pe.transpose(bank[k % 4][:, b * P:(b + 1) * P], rows[:, b, k * P:(k + 1) * P], ident[:, :])
                m.then_inc(turned, 1)
            pe.wait_ge(kept, KD)
            pe.wait_ge(wk0, 16)
            for h in range(4):
                for t in range(KD):
                    m = pe.matmul(bank[4 + h][:, 0:MEM], wk[:, t, h * P:(h + 1) * P], mt[:, t, :], start=t == 0, stop=t == KD - 1)
                m.then_inc(kmm, 1)
            pe.wait_ge(wv_in, 16)
            for b in range(MB):
                for t in range(KD):
                    m = pe.matmul(bank[b][:, :], mt[:, t, b * P:(b + 1) * P], wv[:, t, :], start=t == 0, stop=t == KD - 1)
                m.then_inc(vmm, 1)

        @block.vector
        def _(dve):
            for k in range(KD):
                dve.wait_ge(turned, k + 1)
                dve.tensor_scalar(mt[:, k, :], bank[k % 4][:, 0:MEM], vec[:, gm + k:gm + k + 1], None, ALU.mult).then_inc(kept, 1)
            for h in range(4):
                dve.wait_ge(kmm, h + 1)
                dve.tensor_copy(mk[:, h, :], bank[4 + h][:, 0:MEM])
            for b in range(MB):
                dve.wait_ge(vmm, b + 1)
                dve.tensor_copy(mv[:, b, :], bank[b][:, :])


def stage_cross(nc, ctx, A, K, bank, u, mk, mv, out):
    (w0, w1, mm, kept, staged, scored, maxed, negmax, exped, inverted, probs, turned, pt_kept, omm, o_kept) = sems(
        ctx, nc, "x", "w0 w1 mm kept staged scored maxed negmax exped inverted probs turned pt_kept omm o_kept")
    w_in = (w0, w1)
    ident = K["ident"]
    w = A["w_cq_2"][0].rearrange("(k p) n -> p k n", p=P)
    XH = 4
    SC = P ** -0.5
    with ExitStack() as inner:
        ring = buffer(inner, nc, "x_ring", [P, 2, KD, P])
        q = buffer(inner, nc, "x_q", [P, XH, SEQ])
        qc = buffer(inner, nc, "x_q_block", [P, 2, XH, P])
        pr = buffer(inner, nc, "x_probs", [P, 2, XH, MEM])
        pt = buffer(inner, nc, "x_probs_t", [P, 2 * XH, P])
        mx = buffer(inner, nc, "x_max", [P, 2, XH])
        den = buffer(inner, nc, "x_den", [P, 2, 2, XH])
        block = inner.enter_context(nc.Block())

        @block.sync
        def _(sp):
            with sp.Fori(0, XH // 2) as i:
                for s in range(2):
                    sp.wait_ge(mm, free(2 * i + s))
                    sp.dma_start(ring[:, s, :, :], w[:, :, ds((2 * i + s) * P, P)]).then_inc(w_in[s], 16)

        @block.gpsimd
        def _(pool):
            pool.wait_ge(kept, ready(XH - 1))
            with pool.Fori(0, NB // 2) as i:
                for s in range(2):
                    n = 2 * i + s
                    pool.wait_ge(scored, free(n))
                    pool.tensor_copy(qc[:, s, :, :], q[:, :, ds(n * P, P)]).then_inc(staged, 1)

        @block.tensor
        def _(pe):
            pe.sem_inc(mm, 2)
            pe.sem_inc(scored, 2)
            with pe.Fori(0, XH // 2) as i:
                for s in range(2):
                    pe.wait_ge(w_in[s], 16 * i + 16)
                    pe.wait_ge(kept, free(2 * i + s))
                    for j, (c, n) in enumerate(SEQS):
                        for t in range(KD):
                            m = pe.matmul(bank[2 * s + j][:, 0:n], ring[:, s, t, :], u[:, t, c:c + n], start=t == 0, stop=t == KD - 1)
                    m.then_inc(mm, 1)
            pe.wait_ge(kept, ready(XH - 1))

            def scores(n, s):
                pe.wait_ge(staged, n + 1)
                pe.wait_ge(exped, 4 * n + 4)
                for h in range(XH):
                    m = pe.matmul(bank[2 * s + h // 2][:, (h % 2) * MEM:(h % 2 + 1) * MEM], qc[:, s, h, :], mk[:, h, :], start=True, stop=True)
                m.then_inc(scored, 1)

            def output(n, s):
                pe.wait_ge(probs, n + 1)
                for g in range(2):
                    pe.wait_ge(pt_kept, 2 * n + g + 1)
                    for r in range(4):
                        m = pe.transpose(bank[4 + g][:, r * P:(r + 1) * P], pr[:, s, 2 * g + r // 2, (r % 2) * P:(r % 2 + 1) * P], ident[:, :])
                    m.then_inc(turned, 1)
                pe.wait_ge(pt_kept, 2 * n + 4)
                pe.wait_ge(o_kept, n + 1)
                for h in range(XH):
                    for r in range(2):
                        m = pe.matmul(bank[6][:, h * P:(h + 1) * P], mv[:, r, h * P:(h + 1) * P], pt[:, 2 * h + r, :], start=r == 0, stop=r == 1)
                m.then_inc(omm, 1)
            scores(0, 0)
            with pe.Fori(0, NB // 2 - 1) as i:
                for s in range(2):
                    scores(2 * i + s + 1, 1 - s)
                    output(2 * i + s, s)
            scores(NB - 1, 1)
            output(NB - 2, 0)
            output(NB - 1, 1)

        @block.vector
        def _(dve):
            dve.sem_inc(pt_kept, 2)

            def maxima(n, s):
                dve.wait_ge(scored, ready(n))
                for j in range(2):
                    m = dve.tensor_reduce(mx[:, s, 2 * j:2 * j + 2], bank[2 * s + j][:, :].rearrange("p (h t) -> p h t", h=2), AX.X, ALU.max)
                m.then_inc(maxed, 1)
                dve.wait_ge(maxed, n + 1)
                dve.tensor_scalar(mx[:, s, :], mx[:, s, :], -SC, None, ALU.mult).then_inc(negmax, 1)

            def output(n, s):
                dve.wait_ge(exped, 4 * n + 12)
                dve.reciprocal(den[:, s, 1, :], den[:, s, 0, :]).then_inc(inverted, 1)
                dve.wait_ge(inverted, n + 1)
                dve.tensor_tensor(pr[:, s, :, :], pr[:, s, :, :], den[:, s, 1, :].unsqueeze(2).to_broadcast([P, XH, MEM]), ALU.mult).then_inc(probs, 1)
                for g in range(2):
                    dve.wait_ge(turned, 2 * n + g + 1)
                    dve.tensor_copy(pt[:, 4 * g:4 * g + 4, :], bank[4 + g][:, :].rearrange("p (h t) -> p h t", h=4)).then_inc(pt_kept, 1)
            maxima(0, 0)
            with dve.Fori(0, NB // 2 - 1) as i:
                for s in range(2):
                    maxima(2 * i + s + 1, 1 - s)
                    output(2 * i + s, s)
            maxima(NB - 1, 1)
            output(NB - 2, 0)
            output(NB - 1, 1)

        @block.scalar
        def _(act):
            act.sem_inc(kept, 2)
            act.sem_inc(o_kept, 1)
            act.sem_inc(exped, 8)
            with act.Fori(0, XH // 2) as i:
                for s in range(2):
                    act.wait_ge(mm, ready(2 * i + s))
                    for j, (c, n) in enumerate(SEQS):
                        a = act.copy(q[:, ds(2 * i + s, 1), c:c + n], bank[2 * s + j][:, 0:n])
                    a.then_inc(kept, 1)

            def exponentials(n, s):
                act.wait_ge(negmax, n + 1)
                for h in range(XH):
                    act.activation(pr[:, s, h, :], bank[2 * s + h // 2][:, (h % 2) * MEM:(h % 2 + 1) * MEM], ACT.Exp, scale=SC,
                                   bias=mx[:, s, h:h + 1], accum_out=den[:, s, 0, h:h + 1]).then_inc(exped, 1)

            def output(n):
                act.wait_ge(omm, n + 1)
                act.copy(out[:, :, ds(n * P, P)], bank[6][:, :].rearrange("p (h t) -> p h t", h=XH)).then_inc(o_kept, 1)
            exponentials(0, 0)
            with act.Fori(0, NB // 2 - 1) as i:
                for s in range(2):
                    exponentials(2 * i + s + 1, 1 - s)
                    output(2 * i + s)
            exponentials(NB - 1, 1)
            output(NB - 2)
            output(NB - 1)


def stage_route(nc, ctx, A, K, bank, h, xt, gates, assigned, token, table, xn_d, list_d):
    (w_in, staged, turned, x_kept, lmm, squared, rstd_made, xn_made, stored_a, stored_b, gw, rmm, cnt, iotas, zeroed, zero_stored, scattered, rows, act_rows, slots_made,
     list_in, list_float, list_turned, listed) = sems(
        ctx, nc, "r", "w_in staged turned x_kept lmm squared rstd_made xn_made stored_a stored_b gw rmm cnt iotas zeroed zero_stored scattered rows act_rows slots_made "
        "list_in list_float list_turned listed")
    ident, ones, vec, eps, lower = (K[n] for n in ("ident", "ones", "vec", "eps", "lower"))
    stored = (stored_a, stored_b)
    BIG = 64.0
    gn = VEC["norm_ffn2"]
    with ExitStack() as inner:
        hs = buffer(inner, nc, "r_block", [P, 2, KD, P])
        wr = buffer(inner, nc, "r_w", [P, KD, ROUTER])
        br = buffer(inner, nc, "r_bias", [P, ROUTER])
        gain = buffer(inner, nc, "r_gain", [P, D])
        sq = buffer(inner, nc, "r_sq", [P, D])
        xn = buffer(inner, nc, "r_xn", [P, 2, D])
        ss = buffer(inner, nc, "r_ss", [P, 3, NB])
        lg = buffer(inner, nc, "r_logits", [P, NB, ROUTER])
        em = buffer(inner, nc, "r_em", [P, NB, NE])
        em2 = buffer(inner, nc, "r_em2", [P, NB, NE])
        tt = buffer(inner, nc, "r_tmp", [P, NB, NE])
        oh1 = buffer(inner, nc, "r_first", [P, NB, NE])
        oh2 = buffer(inner, nc, "r_second", [P, NB, NE])
        both = buffer(inner, nc, "r_both", [P, NB + 1, NE])
        before = buffer(inner, nc, "r_before", [P, NB, NE])
        rank = buffer(inner, nc, "r_rank", [P, NB, NE])
        g4 = buffer(inner, nc, "r_g4", [P, NB, NG])
        g4b = buffer(inner, nc, "r_g4b", [P, NB, NG])
        sm = buffer(inner, nc, "r_small", [P, 10, NB])
        iota = buffer(inner, nc, "r_iota", [P, NE])
        stepf = buffer(inner, nc, "r_steps", [P, MAXB])
        own = buffer(inner, nc, "r_assignments", [P, 2 * NB], I32)
        empty = buffer(inner, nc, "r_empty", [MAXB, P], I32)
        slots = buffer(inner, nc, "r_slot", [P, 2 * NB], I32)
        lists = buffer(inner, nc, "r_list", [MAXB, P], I32)
        listf = buffer(inner, nc, "r_list_float", [MAXB, P])
        ex = buffer(inner, nc, "r_experts", [P, 5, NE])
        big = buffer(inner, nc, "r_big", [P, MAXB, NE])
        tf = buffer(inner, nc, "r_table", [1, 64])
        sf = buffer(inner, nc, "r_slots", [P, 2, NB])
        block = inner.enter_context(nc.Block())

        @block.sync
        def _(sp):
            sp.dma_start(wr[:, :, 0:NG], A["w_router_group_2"][0].rearrange("(k p) n -> p k n", p=P)).then_inc(w_in, 16)
            sp.dma_start(wr[:, :, NG:ROUTER], A["w_router_expert_2"][0].rearrange("(k p) n -> p k n", p=P)).then_inc(w_in, 16)
            sp.dma_start(br[:, 0:NG], A["b_router_group_2"].to_broadcast([P, NG])).then_inc(w_in, 16)
            sp.dma_start(br[:, NG:ROUTER], A["b_router_expert_2"].to_broadcast([P, NE])).then_inc(w_in, 16)
            sp.dma_start(gain[:, :], A["norm_ffn_2"].to_broadcast([P, D])).then_inc(w_in, 16)
            sp.wait_ge(zeroed, 1)
            sp.dma_start(list_d.rearrange("(b p) o -> b (p o)", p=P), empty[:, :]).then_inc(zero_stored, 16)
            with sp.Fori(0, NB // 2) as i:
                for s in range(2):
                    n = 2 * i + s
                    sp.wait_ge(xn_made, n + 1)
                    sp.dma_start(xn_d[ds(n * P, P), :], xn[:, s, :]).then_inc(stored[s], 16)
            sp.wait_ge(stored[0], 8 * NB)
            sp.wait_ge(stored[1], 8 * NB)
            sp.wait_ge(scattered, 32 * NB)
            sp.dma_start(lists[:, :], list_d.rearrange("(b p) o -> b (p o)", p=P)).then_inc(list_in, 16)

        @block.gpsimd
        def _(pool):
            pool.iota(empty[:, :], [[1, P]], base=2 * SEQ, channel_multiplier=0).then_inc(zeroed, 1)
            pool.iota(iota[:, :], [[1, NE]], base=0, channel_multiplier=0, allow_small_or_imprecise_dtypes=True).then_inc(iotas, 1)
            pool.iota(stepf[:, :], [[1, MAXB]], base=0, channel_multiplier=0, allow_small_or_imprecise_dtypes=True).then_inc(iotas, 1)
            pool.iota(own[:, :], [[P, 2 * NB]], base=0, channel_multiplier=1).then_inc(iotas, 1)
            with pool.Fori(0, NB // 2) as i:
                for s in range(2):
                    pool.wait_ge(lmm, free(2 * i + s))
                    pool.tensor_copy(hs[:, s, :, :], h[:, :, ds((2 * i + s) * P, P)]).then_inc(staged, 1)
            pool.wait_ge(slots_made, 1)
            pool.wait_ge(zero_stored, 16)
            pool.wait_ge(iotas, 3)
            for j in range(2):
                for b in range(NB):
                    pool.indirect_dma_start(out=list_d, out_offset=bass.IndirectOffsetOnAxis(ap=slots[:, j * NB + b:j * NB + b + 1], axis=0),
                                            in_=own[:, j * NB + b:j * NB + b + 1], in_offset=None).then_inc(scattered, 16)
            pool.wait_ge(scattered, 32 * NB)

        @block.tensor
        def _(pe):
            pe.sem_inc(lmm, 2)
            pe.wait_ge(gw, KD)
            with pe.Fori(0, NB // 2) as i:
                for s in range(2):
                    n = 2 * i + s
                    pe.wait_ge(staged, n + 1)
                    pe.wait_ge(x_kept, free(n))
                    for k in range(KD):
                        m = pe.transpose(bank[2 * s + k // 4][:, (k % 4) * P:(k % 4 + 1) * P], hs[:, s, k, :], ident[:, :])
                    m.then_inc(turned, 1)
                    for k in range(KD):
                        m = pe.matmul(bank[4][:, ds(n * ROUTER, ROUTER)], hs[:, s, k, :], wr[:, k, :], start=k == 0, stop=k == KD - 1)
                    m.then_inc(lmm, 1)
            pe.wait_ge(rmm, 1)
            pe.matmul(bank[5][:, 0:NB * NE], lower[:, :], both[:, 0:NB, :], start=True, stop=False)
            pe.matmul(bank[5][:, 0:NB * NE], ones[:, :], before[:, :, :], start=False, stop=True).then_inc(cnt, 1)
            pe.matmul(bank[6][:, 0:NE], ones[:, :], both[:, NB, :], start=True, stop=True).then_inc(cnt, 1)
            pe.wait_ge(list_float, 1)
            pe.transpose(bank[7][:, 0:MAXB], listf[:, :], ident[0:MAXB, 0:MAXB]).then_inc(list_turned, 1)

        @block.scalar
        def _(act):
            act.sem_inc(x_kept, 2)
            with act.Fori(0, NB // 2) as i:
                for s in range(2):
                    n = 2 * i + s
                    act.wait_ge(turned, n + 1)
                    act.copy(xt[:, ds(n, 1), 0:BANK], bank[2 * s][:, :])
                    act.copy(xt[:, ds(n, 1), BANK:D], bank[2 * s + 1][:, :]).then_inc(x_kept, 1)
                    act.wait_ge(x_kept, ready(n))
                    act.wait_ge(squared, n + 1)
                    act.activation(sq[:, :], xt[:, ds(n, 1), :].rearrange("p a d -> p (a d)"), ACT.Square,
                                   accum_out=ss[:, 0, ds(n, 1)]).then_inc(squared, 1)
            act.wait_ge(squared, NB + 1)
            act.activation(ss[:, 1, :], ss[:, 0, :], ACT.Ln, bias=eps[:, 0:1], scale=1.0 / D).then_inc(squared, 1)
            act.wait_ge(squared, NB + 2)
            act.activation(ss[:, 2, :], ss[:, 1, :], ACT.Exp, scale=-0.5).then_inc(rstd_made, 1)
            act.wait_ge(act_rows, 1)
            act.activation(g4b[:, :, :], g4b[:, :, :], ACT.Exp).then_inc(act_rows, 1)
            act.wait_ge(act_rows, 3)
            act.activation(sm[:, 6, :], sm[:, 6, :], ACT.Exp).then_inc(act_rows, 1)

        @block.vector
        def _(dve):
            n = 0

            def then(ins):
                nonlocal n
                n += 1
                ins.then_inc(rows, 1)
                dve.wait_ge(rows, n)

            def over(ap, m):
                return ap.unsqueeze(2).to_broadcast([P, NB, m])

            def along(ap, m):
                return ap.unsqueeze(1).to_broadcast([P, NB, m])
            dve.sem_inc(squared, 1)
            then(dve.memset(tf[:, :], 0.0))
            dve.wait_ge(w_in, 80)
            for k in range(KD):
                dve.tensor_scalar(wr[:, k, :], wr[:, k, :], vec[:, gn + k:gn + k + 1], None, ALU.mult).then_inc(gw, 1)
            dve.wait_ge(rstd_made, 1)
            dve.wait_ge(x_kept, ready(NB - 1))
            dve.wait_ge(lmm, ready(NB - 1))
            for b in range(NB):
                if b >= 2:
                    dve.wait_ge(stored[b % 2], 16 * (b // 2))
                dve.scalar_tensor_tensor(xn[:, b % 2, :], xt[:, b, :], ss[:, 2, b:b + 1], gain[:, :], ALU.mult, ALU.mult).then_inc(xn_made, 1)
            then(dve.tensor_tensor(lg[:, :, :], bank[4][:, 0:NB * ROUTER].rearrange("p (b n) -> p b n", n=ROUTER), over(ss[:, 2, :], ROUTER), ALU.mult))
            then(dve.tensor_tensor(lg[:, :, :], lg[:, :, :], along(br[:, :], ROUTER), ALU.add))
            dve.wait_ge(iotas, 3)
            then(dve.tensor_reduce(sm[:, 0, :], lg[:, :, 0:NG], AX.X, ALU.max))
            dve.tensor_tensor(g4b[:, :, :], lg[:, :, 0:NG], over(sm[:, 0, :], NG), ALU.subtract).then_inc(act_rows, 1)
            then(dve.tensor_tensor(g4[:, :, :], lg[:, :, 0:NG], over(sm[:, 0, :], NG), ALU.is_equal))
            then(dve.scalar_tensor_tensor(g4[:, :, :], g4[:, :, :], -BIG, along(iota[:, 0:NG], NG), ALU.mult, ALU.add))
            then(dve.tensor_reduce(sm[:, 1, :], g4[:, :, :], AX.X, ALU.min))
            then(dve.tensor_scalar(sm[:, 1, :], sm[:, 1, :], BIG, None, ALU.add))
            then(dve.tensor_tensor(g4[:, :, :], over(sm[:, 1, :], NG), along(iota[:, 0:NG], NG), ALU.is_equal))
            then(dve.tensor_scalar(g4[:, :, :], g4[:, :, :], -NEG, NEG, ALU.mult, ALU.add))
            for g in range(NG):
                then(dve.tensor_tensor(em[:, :, g * EPG:(g + 1) * EPG], lg[:, :, NG + g * EPG:NG + (g + 1) * EPG],
                                       g4[:, :, g:g + 1].to_broadcast([P, NB, EPG]), ALU.add))
            for j, (src, oh) in enumerate(((em, oh1), (em2, oh2))):
                then(dve.tensor_reduce(sm[:, 2 + j, :], src[:, :, :], AX.X, ALU.max))
                then(dve.tensor_tensor(tt[:, :, :], src[:, :, :], over(sm[:, 2 + j, :], NE), ALU.is_equal))
                then(dve.scalar_tensor_tensor(tt[:, :, :], tt[:, :, :], -BIG, along(iota[:, :], NE), ALU.mult, ALU.add))
                then(dve.tensor_reduce(sm[:, 4, :], tt[:, :, :], AX.X, ALU.min))
                then(dve.tensor_scalar(sm[:, 4, :], sm[:, 4, :], BIG, None, ALU.add))
                then(dve.tensor_tensor(oh[:, :, :], over(sm[:, 4, :], NE), along(iota[:, :], NE), ALU.is_equal))
                if j == 0:
                    then(dve.scalar_tensor_tensor(em2[:, :, :], oh[:, :, :], 2 * NEG, em[:, :, :], ALU.mult, ALU.add))
            dve.wait_ge(act_rows, 2)
            dve.tensor_tensor(sm[:, 6, :], sm[:, 3, :], sm[:, 2, :], ALU.subtract).then_inc(act_rows, 1)
            then(dve.tensor_reduce(sm[:, 5, :], g4b[:, :, :], AX.X, ALU.add))
            dve.wait_ge(act_rows, 4)
            then(dve.tensor_scalar(sm[:, 7, :], sm[:, 6, :], 1.0, None, ALU.add))
            then(dve.tensor_tensor(sm[:, 7, :], sm[:, 7, :], sm[:, 5, :], ALU.mult))
            then(dve.reciprocal(gates[:, 0:NB], sm[:, 7, :]))
            then(dve.tensor_tensor(gates[:, NB:2 * NB], gates[:, 0:NB], sm[:, 6, :], ALU.mult))
            then(dve.tensor_tensor(both[:, 0:NB, :], oh1[:, :, :], oh2[:, :, :], ALU.add))
            then(dve.memset(before[:, 0, :], 0.0))
            for b in range(1, NB):
                then(dve.tensor_tensor(before[:, b, :], before[:, b - 1, :], both[:, b - 1, :], ALU.add))
            dve.tensor_tensor(both[:, NB, :], before[:, NB - 1, :], both[:, NB - 1, :], ALU.add).then_inc(rmm, 1)
            dve.wait_ge(cnt, 2)
            then(dve.tensor_copy(ex[:, 0, :], bank[6][:, 0:NE]))
            then(dve.tensor_scalar(ex[:, 1, :], ex[:, 0, :], 0.0, None, ALU.is_gt))
            for j in range(1, SEQ // P):
                then(dve.scalar_tensor_tensor(ex[:, 1, :], ex[:, 0, :], float(j * P), ex[:, 1, :], ALU.is_gt, ALU.add))
            then(dve.tensor_tensor_scan(ex[:, 2, :], ones[:, 0:NE], ex[:, 1, :], 0.0, ALU.mult, ALU.add))
            then(dve.tensor_tensor(ex[:, 3, :], ex[:, 2, :], ex[:, 1, :], ALU.subtract))
            then(dve.tensor_scalar(ex[:, 4, :], ex[:, 3, :], float(P), None, ALU.mult))
            then(dve.tensor_tensor(rank[:, :, :], bank[5][:, 0:NB * NE].rearrange("p (b n) -> p b n", n=NE), along(ex[:, 4, :], NE), ALU.add))
            for j, oh in enumerate((oh1, oh2)):
                then(dve.tensor_tensor(tt[:, :, :], oh[:, :, :], rank[:, :, :], ALU.mult))
                then(dve.tensor_reduce(sf[:, j, :], tt[:, :, :], AX.X, ALU.add))
            dve.tensor_copy(slots[:, :], sf[:, :, :].rearrange("p j b -> p (j b)")).then_inc(slots_made, 1)
            then(dve.tensor_tensor(big[0:1, :, :], stepf[0:1, :].unsqueeze(2).to_broadcast([1, MAXB, NE]), ex[0:1, 2, :].unsqueeze(1).to_broadcast([1, MAXB, NE]), ALU.is_ge))
            then(dve.tensor_reduce(tf[:, 0:MAXB], big[0:1, :, :], AX.X, ALU.add))
            then(dve.tensor_scalar(tf[:, 0:MAXB], tf[:, 0:MAXB], float(NE - 1), None, ALU.min))
            then(dve.tensor_scalar(big[0:1, 0:MAXB // 2, 0], stepf[0:1, 0:MAXB // 2], 2.0, None, ALU.mult))
            then(dve.tensor_scalar(big[0:1, 0:MAXB // 2, 1], big[0:1, 0:MAXB // 2, 0], ex[0:1, 2, NE - 1:NE], None, ALU.is_lt))
            then(dve.tensor_reduce(tf[:, PAIRS:PAIRS + 1], big[0:1, 0:MAXB // 2, 1], AX.X, ALU.add))
            dve.tensor_copy(table[:, :], tf[:, :])
            then(dve.memset(assigned[:, MAXB:MAXB + 2], 0))
            dve.wait_ge(list_in, 16)
            dve.tensor_copy(listf[:, :], lists[:, :]).then_inc(list_float, 1)
            dve.wait_ge(list_turned, 1)
            then(dve.tensor_copy(assigned[:, 0:MAXB], bank[7][:, 0:MAXB]))
            then(dve.tensor_scalar(token[:, :], assigned[:, :], SEQ - 1, None, ALU.bitwise_and))


def stage_experts(nc, ctx, A, K, bank, assigned, token, table, xn_d, y_d):
    (g0, g1, turned, x_hi, x_lo, used, hi_made, lo_made, silu_made, hb_made, hturned, h_hi, h_lo,
     y_kept_a, y_kept_b, s0, s1, index_made, waited, ended, y_stored) = sems(
        ctx, nc, "k", "g0 g1 turned x_hi x_lo used hi_made lo_made silu_made hb_made hturned h_hi h_lo "
        "y_kept_a y_kept_b s0 s1 index_made waited ended y_stored")
    PIECES, RAW, SPLIT = 6, 6, 3
    pieces_in = sems(ctx, nc, "k", " ".join(f"piece_in{r}" for r in range(RAW)))
    gathered, stored = (g0, g1), (s0, s1)
    ident = K["ident"]
    w_gate = A["w_e_gate_2"][0].rearrange("e (k p) n -> e p k n", p=P)
    w_up = A["w_e_up_2"][0].rearrange("e (k p) n -> e p k n", p=P)
    w_down = A["w_e_down_2"][0].rearrange("e (k p) n -> e p k n", p=P)
    with ExitStack() as inner:
        raw = buffer(inner, nc, "k_raw", [P, RAW, KE, BANK])
        wh = buffer(inner, nc, "k_w_hi", [P, SPLIT, KE, BANK], F32R)
        wl = buffer(inner, nc, "k_w_lo", [P, SPLIT, KE, BANK], F32R)
        from_ = buffer(inner, nc, "k_from", [P, 2], I32)
        to = buffer(inner, nc, "k_to", [P, 2], I32)
        xg = buffer(inner, nc, "k_rows", [P, 2, D])
        xh = buffer(inner, nc, "k_x_hi", [P, KD, P], F32R)
        xl = buffer(inner, nc, "k_x_lo", [P, KD, P], F32R)
        sg = buffer(inner, nc, "k_silu", [P, BANK])
        hb = buffer(inner, nc, "k_h", [P, BANK])
        hh = buffer(inner, nc, "k_h_hi", [P, KE, P], F32R)
        hl = buffer(inner, nc, "k_h_lo", [P, KE, P], F32R)
        y = buffer(inner, nc, "k_y", [P, 2, D])
        block = inner.enter_context(nc.Block())

        def tiles(ap):
            return ap.rearrange("p (k t) -> p k t", t=P)

        def source(e, j):
            if j < 4:
                w, k, c = (w_gate, w_up)[j // 2], KE * (j % 2), 0
            else:
                w, k, c = w_down, 0, BANK * (j - 4)
            return w[ds(e, 1), :, k:k + KE, c:c + BANK].rearrange("a p k n -> (a p) k n")

        @block.sync
        def _(sp):
            pairs = sp.value_load(table[0:1, PAIRS:PAIRS + 1], min_val=1, max_val=MAXB // 2)

            def load(n, r, e, j):
                sp.wait_ge(lo_made, n + 1)
                sp.dma_start(raw[:, r, :, :], source(e, j)).then_inc(pieces_in[r], 16)
            with sp.Fori(0, pairs) as i:
                for s in range(2):
                    e = sp.value_load(table[0:1, ds(2 * i + s, 1)], min_val=0, max_val=NE - 1)
                    for j in range(PIECES):
                        load(2 * PIECES * i + PIECES * s + j, (PIECES * s + j) % RAW, e, j)
            for j in range(2):
                load(2 * PIECES * pairs + j, j, 0, j)

        @block.gpsimd
        def _(pool):
            pool.sem_inc(y_stored, 2)
            pairs = pool.value_load(table[0:1, PAIRS:PAIRS + 1], min_val=1, max_val=MAXB // 2)

            def gather(g, b, s):
                pool.wait_ge(turned, b + 1)
                pool.tensor_copy(from_[:, s:s + 1], token[:, ds(b, 1)]).then_inc(index_made, 1)
                pool.wait_ge(index_made, g)
                pool.sem_inc(waited, 1)
                pool.wait_ge(waited, 1)
                pool.indirect_dma_start(out=xg[:, s, :], out_offset=None, in_=xn_d,
                                        in_offset=bass.IndirectOffsetOnAxis(ap=from_[:, s:s + 1], axis=0)).then_inc(gathered[s], 16)

            def scatter(g, b, s):
                pool.tensor_copy(to[:, s:s + 1], assigned[:, ds(b, 1)]).then_inc(index_made, 1)
                pool.wait_ge(index_made, g)
                pool.wait_ge(y_kept_a, b + 2)
                pool.wait_ge(y_kept_b, b + 2)
                pool.sem_inc(waited, 1)
                pool.wait_ge(waited, 1)
                pool.indirect_dma_start(out=y_d, out_offset=bass.IndirectOffsetOnAxis(ap=to[:, s:s + 1], axis=0),
                                        in_=y[:, s, :], in_offset=None).then_inc(stored[s], 16)

            def end(i, s):
                pool.wait_ge(stored[s], 16 * i + 16)
                pool.sem_inc(y_stored, 1)
            gather(1, 0, 0)
            gather(2, 1, 1)
            with pool.Fori(0, pairs) as i:
                for s in range(2):
                    gather(4 * i + 2 * s + 3, 2 * i + s + 2, s)
                    scatter(4 * i + 2 * s + 4, 2 * i + s, s)
                    end(i, s)
            pool.wait_ge(gathered[0], 16 * pairs + 16)
            pool.sem_inc(ended, 1)
            pool.wait_ge(gathered[1], 16 * pairs + 16)
            pool.sem_inc(ended, 1)
            pool.wait_ge(ended, 2)

        @block.tensor
        def _(pe):
            pe.sem_inc(turned, 2)
            pe.sem_inc(used, SPLIT)
            pairs = pe.value_load(table[0:1, PAIRS:PAIRS + 1], min_val=1, max_val=MAXB // 2)

            def rows(n_in, s):
                pe.wait_ge(gathered[s], 16 * n_in)
                for k in range(KD):
                    m = pe.transpose(bank[k // 4][:, (k % 4) * P:(k % 4 + 1) * P], xg[:, s, k * P:(k + 1) * P], ident[:, :])
                m.then_inc(turned, 1)

            def piece(n, r, x, out, first, last):
                pe.wait_ge(lo_made, n + RAW + 1)
                hi, lo = x
                for k in range(KE):
                    pe.matmul(out, hi[:, k, :], wh[:, r, k, :], start=first and k == 0, stop=False)
                    pe.matmul(out, hi[:, k, :], wl[:, r, k, :], start=False, stop=False)
                    m = pe.matmul(out, lo[:, k, :], wh[:, r, k, :], start=False, stop=last and k == KE - 1)
                m.then_inc(used, 1)
            rows(1, 0)
            with pe.Fori(0, pairs) as i:
                for s in range(2):
                    b, n = 2 * i + s, 2 * PIECES * i + PIECES * s
                    pe.wait_ge(x_lo, 2 * b + 2)
                    for j in range(4):
                        half = j % 2
                        x = (xh[:, KE * half:KE * half + KE, :], xl[:, KE * half:KE * half + KE, :])
                        piece(n + j, (PIECES * s + j) % SPLIT, x, bank[2 + j // 2][:, :], half == 0, half == 1)
                    rows(i + 1 + s, 1 - s)
                    pe.wait_ge(hb_made, b + 1)
                    for k in range(KE):
                        m = pe.transpose(bank[4][:, k * P:(k + 1) * P], hb[:, k * P:(k + 1) * P], ident[:, :])
                    m.then_inc(hturned, 1)
                    pe.wait_ge(h_lo, b + 1)
                    pe.wait_ge(y_kept_a, b + 1)
                    piece(n + 4, (PIECES * s + 4) % SPLIT, (hh, hl), bank[5][:, :], True, True)
                    pe.wait_ge(y_kept_b, b + 1)
                    piece(n + 5, (PIECES * s + 5) % SPLIT, (hh, hl), bank[6][:, :], True, True)

        @block.scalar
        def _(act):
            act.sem_inc(y_kept_a, 1)
            pairs = act.value_load(table[0:1, PAIRS:PAIRS + 1], min_val=1, max_val=MAXB // 2)

            def high(n, r, q, n_in):
                act.wait_ge(pieces_in[r], 16 * n_in)
                act.wait_ge(used, n + 1)
                act.copy(wh[:, q, :, :], raw[:, r, :, :]).then_inc(hi_made, 1)

            def rows_high(b):
                act.wait_ge(turned, b + 3)
                for h in range(2):
                    act.copy(xh[:, KE * h:KE * h + KE, :], tiles(bank[h][:, :])).then_inc(x_hi, 1)
            high(0, 0, 0, 1)
            high(1, 1, 1, 1)
            rows_high(0)
            with act.Fori(0, pairs) as i:
                for s in range(2):
                    b, n = 2 * i + s, 2 * PIECES * i + PIECES * s

                    def piece(j):
                        high(n + j, j % RAW, j % SPLIT, 2 * i + s + 1 + j // RAW)
                    piece(2)
                    piece(3)
                    act.wait_ge(used, n + 5)
                    act.activation(sg[:, :], bank[2][:, :], ACT.Silu).then_inc(silu_made, 1)
                    piece(4)
                    piece(5)
                    rows_high(b + 1)
                    act.wait_ge(hturned, b + 1)
                    act.copy(hh[:, :, :], tiles(bank[4][:, :])).then_inc(h_hi, 1)
                    piece(6)
                    piece(7)
                    act.wait_ge(y_stored, b + 1)
                    act.wait_ge(used, n + 8)
                    act.copy(y[:, s, 0:BANK], bank[5][:, :]).then_inc(y_kept_a, 1)

        @block.vector
        def _(dve):
            dve.sem_inc(y_kept_b, 1)
            dve.sem_inc(lo_made, RAW)
            pairs = dve.value_load(table[0:1, PAIRS:PAIRS + 1], min_val=1, max_val=MAXB // 2)

            def low(n, r, q):
                dve.wait_ge(hi_made, n + 1)
                dve.tensor_tensor(wl[:, q, :, :], raw[:, r, :, :], wh[:, q, :, :], ALU.subtract).then_inc(lo_made, 1)

            def rows_low(b):
                for h in range(2):
                    dve.wait_ge(x_hi, 2 * b + h + 1)
                    half = slice(KE * h, KE * h + KE)
                    dve.tensor_tensor(xl[:, half, :], tiles(bank[h][:, :]), xh[:, half, :], ALU.subtract).then_inc(x_lo, 1)
            low(0, 0, 0)
            low(1, 1, 1)
            rows_low(0)
            with dve.Fori(0, pairs) as i:
                for s in range(2):
                    b, n = 2 * i + s, 2 * PIECES * i + PIECES * s

                    def piece(j):
                        low(n + j, j % RAW, j % SPLIT)
                    piece(2)
                    piece(3)
                    piece(4)
                    dve.wait_ge(silu_made, b + 1)
                    dve.wait_ge(used, n + 7)
                    dve.tensor_tensor(hb[:, :], sg[:, :], bank[3][:, :], ALU.mult).then_inc(hb_made, 1)
                    rows_low(b + 1)
                    dve.wait_ge(h_hi, b + 1)
                    dve.tensor_tensor(hl[:, :, :], tiles(bank[4][:, :]), hh[:, :, :], ALU.subtract).then_inc(h_lo, 1)
                    piece(5)
                    piece(6)
                    piece(7)
                    dve.wait_ge(y_stored, b + 1)
                    dve.wait_ge(used, n + 9)
                    dve.tensor_copy(y[:, s, BANK:D], bank[6][:, :]).then_inc(y_kept_b, 1)


def stage_finish(nc, ctx, A, K, bank, xt, gates, y_d, out):
    a0, a1, b0, b1, gain_in, first, mixed, squared, normed, stored = sems(ctx, nc, "o2", "a0 a1 b0 b1 gain_in first mixed squared normed stored")
    ga, gb = (a0, a1), (b0, b1)
    eps = K["eps"]
    with ExitStack() as inner:
        ya = buffer(inner, nc, "ya", [P, 2, D])
        yb = buffer(inner, nc, "yb", [P, 2, D])
        sq = buffer(inner, nc, "y_sq", [P, D])
        gain = buffer(inner, nc, "y_gain", [P, D])
        ss = buffer(inner, nc, "y_ss", [P, 3, NB])
        block = inner.enter_context(nc.Block())

        @block.sync
        def _(sp):
            sp.dma_start(gain[:, :], A["norm_final_2"].rearrange("(a d) -> a d", a=1).to_broadcast([P, D])).then_inc(gain_in, 16)
            for b in range(NB + 2):
                if b < NB:
                    if b >= 2:
                        sp.wait_ge(mixed, b - 1)
                    for j, (buf, sem) in enumerate(((ya, ga), (yb, gb))):
                        sp.dma_start(buf[:, b % 2, :], y_d[j * SEQ + b * P:j * SEQ + (b + 1) * P, :]).then_inc(sem[b % 2], 16)
                if b >= 2:
                    sp.wait_ge(normed, b - 1)
                    sp.dma_start(out[0, (b - 2) * P:(b - 1) * P, :], xt[:, b - 2, :]).then_inc(stored, 16)
            sp.wait_ge(stored, 16 * NB)

        @block.vector
        def _(dve):
            def norm(b):
                dve.wait_ge(squared, 3 * b + 3)
                if b == 0:
                    dve.wait_ge(gain_in, 16)
                dve.scalar_tensor_tensor(xt[:, b, :], xt[:, b, :], ss[:, 2, b:b + 1], gain[:, :], ALU.mult, ALU.mult).then_inc(normed, 1)
            for b in range(NB):
                dve.wait_ge(ga[b % 2], 16 * (b // 2 + 1))
                dve.scalar_tensor_tensor(xt[:, b, :], ya[:, b % 2, :], gates[:, b:b + 1], xt[:, b, :], ALU.mult, ALU.add).then_inc(first, 1)
                dve.wait_ge(gb[b % 2], 16 * (b // 2 + 1))
                dve.wait_ge(first, b + 1)
                dve.scalar_tensor_tensor(xt[:, b, :], yb[:, b % 2, :], gates[:, NB + b:NB + b + 1], xt[:, b, :], ALU.mult, ALU.add).then_inc(mixed, 1)
                if b:
                    norm(b - 1)
            norm(NB - 1)

        @block.scalar
        def _(act):
            for b in range(NB):
                act.wait_ge(mixed, b + 1)
                if b:
                    act.wait_ge(squared, 3 * b)
                act.activation(sq[:, :], xt[:, b, :], ACT.Square, accum_out=ss[:, 0, b:b + 1]).then_inc(squared, 1)
                act.wait_ge(squared, 3 * b + 1)
                act.activation(ss[:, 1, b:b + 1], ss[:, 0, b:b + 1], ACT.Ln, bias=eps[:, 0:1], scale=1.0 / D).then_inc(squared, 1)
                act.wait_ge(squared, 3 * b + 2)
                act.activation(ss[:, 2, b:b + 1], ss[:, 1, b:b + 1], ACT.Exp, scale=-0.5).then_inc(squared, 1)




def end_part(nc, before):
    nc.clear_and_free_semaphores(nc.allocated_since(before))
    nc.all_engine_barrier()


def program(nc, A, out):
    h0_d = nc.dram_tensor("h0_scratch", [P, KD, WIDE], F32).ap()
    h1_d = nc.dram_tensor("h1_scratch", [P, KD, LIVE], F32).ap()
    xn_d = nc.dram_tensor("xn_scratch", [SEQ, D], F32).ap()
    list_d = nc.dram_tensor("slot_assignments", [MAXB * P, 1], I32).ap()
    y_d = nc.dram_tensor("y_scratch", [2 * SEQ + P, D], F32).ap()
    with ExitStack() as ctx:
        K = constants(ctx, nc)
        bank = [ctx.enter_context(nc.psum_tensor(f"bank{j}", [P, BANK], F32)) for j in range(8)]
        before = nc.snapshot_sems()
        stage_constants(nc, ctx, A, K, bank)
        with ExitStack() as first:
            z_flat = buffer(first, nc, "z", [P, KD * LIVE], side="right")
            z = z_flat[:, :].rearrange("p (k t) -> p k t", k=KD)
            v = z_flat[:, 0:CHUNKS * BANK].rearrange("p (c n) -> p c n", c=CHUNKS)
            with ExitStack() as mixers:
                u = buffer(mixers, nc, "u", [P, KD, WIDE])
                o = buffer(mixers, nc, "o", [P, HALF, WIDE])
                with ExitStack() as tokens:
                    h0 = buffer(tokens, nc, "h0", [P, KD, WIDE])
                    stage_load(nc, ctx, A, K, bank, h0, u, h0_d)
                with ExitStack() as recurrence:
                    q = buffer(recurrence, nc, "q", [P, HALF, WIDE])
                    k = buffer(recurrence, nc, "k", [P, HALF, WIDE])
                    lf = buffer(recurrence, nc, "lf", [P, HALF, WIDE])
                    stage_hgrn_in(nc, ctx, A, K, bank, u, q, k, lf, v)
                    stage_hgrn(nc, ctx, A, K, bank, q, k, lf, v, o, z_flat[:, CHUNKS * BANK:])
                with ExitStack() as branches:
                    p = buffer(branches, nc, "p", [P, HALF, LIVE])
                    stage_branches(nc, ctx, A, K, bank, u, o, p)
                    stage_mix(nc, ctx, A, K, bank, u, o, p, z)
            pair = ExitStack()
            u_pair = tuple(buffer(pair, nc, n, [P, KD, LIVE], F32R) for n in ("u_ffn_hi", "u_ffn_lo"))
            with ExitStack() as post:
                y = buffer(post, nc, "mixed", [P, KD, LIVE])
                h1 = buffer(post, nc, "h1", [P, KD, LIVE])
                stage_project(nc, ctx, A, K, bank, "wo1", A["w_out"][0], KD, z, y, h1, "mix_post", LIVES, h0_d[:, :, FIRST:], h1_d,
                              u_pair, "ffn_pre")
        with ExitStack() as ffn:
            hidden = buffer(ffn, nc, "hidden", [P, KF, SEQ], side="right")
            with pair:
                stage_ffn(nc, ctx, A, K, bank, u_pair, hidden)
            state = buffer(ctx, nc, "state", [P, KD, SEQ])
            h = buffer(ctx, nc, "stream", [P, KD, SEQ])
            stage_down(nc, ctx, A, K, bank, hidden, state, h, h1_d[:, :, TAPS - 1:], state)
        end_part(nc, before)
        with ExitStack() as mixers:
            qk = buffer(mixers, nc, "qk", [P, KD, SEQ])
            vm = buffer(mixers, nc, "vm", [P, NB, BANK])
            og = buffer(mixers, nc, "og", [P, 4, SEQ])
            gi = buffer(mixers, nc, "gi", [ML_H, SEQ])
            gf = buffer(mixers, nc, "gf", [ML_H, SEQ])
            with ExitStack() as attention:
                qa = buffer(attention, nc, "qa", [P, 4, SEQ])
                ka = buffer(attention, nc, "ka", [P, WIDE])
                va = buffer(attention, nc, "va", [P, CHUNKS, P])
                stage_in2(nc, ctx, A, K, bank, state, qa, ka, va, qk, vm, og, gi, gf)
                stage_attention(nc, ctx, A, K, bank, qa, ka, va, state, state[:, KD // 2:, :].rearrange("p k t -> p (k t)"))
            stage_mlstm(nc, ctx, A, K, bank, qk, vm, og, gi, gf, state)
        stage_residual(nc, ctx, A, K, bank, "wo2", A["w_out_2"][0], KD, state, h, state, "norm_cross")
        with ExitStack() as cross:
            mk = buffer(cross, nc, "mk", [P, 4, MEM])
            mv = buffer(cross, nc, "mv", [P, MEM // P, BANK])
            co = buffer(cross, nc, "co", [P, 4, SEQ])
            stage_memory(nc, ctx, A, K, bank, mk, mv)
            stage_cross(nc, ctx, A, K, bank, state, mk, mv, co)
            stage_residual(nc, ctx, A, K, bank, "wc", A["w_co_2"][0], 4, co, h)
        end_part(nc, before)
        gates = buffer(ctx, nc, "gates", [P, 2 * NB])
        assigned = buffer(ctx, nc, "assigned", [P, MAXB + 2], I32)
        token = buffer(ctx, nc, "token", [P, MAXB + 2], I32)
        table = buffer(ctx, nc, "table", [1, 64], I32)
        stage_route(nc, ctx, A, K, bank, h, state, gates, assigned, token, table, xn_d, list_d)
        stage_experts(nc, ctx, A, K, bank, assigned, token, table, xn_d, y_d)
        stage_finish(nc, ctx, A, K, bank, state, gates, y_d, out)


_INS = ["x", "meta_tokens", "mix_norm_pre", "mix_norm_post", "w_in", "hgrn_lower_bounds", "hgrn_out_norm", "w_branch_hgrn",
        "pool_proj", "pool_scale", "w_branch_pool", "w_out", "ffn_norm_pre", "ffn_norm_post", "ffn_w_gate", "ffn_w_up",
        "ffn_conv_w", "ffn_conv_b", "ffn_w_down", "mem_2", "norm_mix_2", "w_in_2", "b_gates_2", "conv_w_2", "conv_b_2",
        "att_sinks_2", "norm_att_out_2", "norm_ml_out_2", "w_out_2", "norm_cross_2", "norm_mem_2", "w_cq_2", "w_ckv_2",
        "w_co_2", "norm_ffn_2", "w_router_group_2", "b_router_group_2", "w_router_expert_2", "b_router_expert_2",
        "w_e_gate_2", "w_e_up_2", "w_e_down_2", "norm_final_2"]


def kernel(**inputs):
    import numpy as _np
    import concourse.bacc as _bacc
    from concourse import mybir as _mybir
    from concourse.bass_utils import run_bass_kernel_spmd as _run

    nc = _bacc.Bacc("TRN2", target_bir_lowering=False, num_devices=1)
    arrays, args = {}, {}
    for name in _INS:
        a = _np.ascontiguousarray(inputs[name])
        arrays[f"in_{name}_dram"] = a
        args[name] = nc.dram_tensor(f"in_{name}_dram", a.shape, _mybir.dt.from_np(a.dtype), kind="ExternalInput").ap()
    out = nc.dram_tensor("out_0_dram", (1, SEQ, D), F32, kind="ExternalOutput").ap()
    program(nc, args, out)
    r = _run(nc, [arrays], core_ids=[0])
    return r.results[0]["out_0_dram"]
```

```python
from contextlib import ExitStack

import concourse.bass as bass
from concourse import mybir

F32 = mybir.dt.float32
F32R = mybir.dt.float32r
I32 = mybir.dt.int32
U32 = mybir.dt.uint32
ALU = mybir.AluOpType
ACT = mybir.ActivationFunctionType
AX = mybir.AxisListType
ds = bass.ds

P = 128
D = 1024
KD = D // P
SEQ = 1024
META = 16
HEAD = P - META
WIDE = SEQ + P
CHUNKS = WIDE // P
HALF = 4
TAPS = 3
LIVE = SEQ + TAPS - 1
FIRST = WIDE - LIVE
DFF = 2816
KF = DFF // P
EPS = 1e-6
LEVELS = 7
BANK = 512
REAL = ((HEAD, 352), (464, 344), (808, 344))
FULL = ((0, 384), (384, 384), (768, 384))
LIVES = ((0, 342), (342, 342), (684, 342))
SEQS = ((0, 512), (512, 512))

NEG = -1e30
LN2 = 0.6931471805599453

QH, DH = 8, 64
WIN = 128
NB = SEQ // P
ML_H = 4
MEM = 256
NE, NG, EPG = 32, 4, 8
DE = 512
KE = DE // P
MAXB = 2 * SEQ // P + NE
PAIRS = 63
ROUTER = NG + NE


def sems(ctx, nc, stage, names):
    return [nc.alloc_semaphore(name=f"{stage}_{n}") for n in names.split()]


def free(n):
    return n + 1


def ready(n):
    return n + 3


def buffer(ctx, nc, name, shape, dt=F32, side="left"):
    return ctx.enter_context(nc.sbuf_tensor(name, shape, dt, side=side))


VECS = (("mix_pre", "mix_norm_pre", 8), ("mix_post", "mix_norm_post", 8), ("ffn_pre", "ffn_norm_pre", 8),
        ("ffn_post", "ffn_norm_post", 8), ("lb", "hgrn_lower_bounds", 4), ("out_norm", "hgrn_out_norm", 4),
        ("pool_scale", "pool_scale", 4), ("conv_w", "ffn_conv_w", 66),
        ("conv_b", "ffn_conv_b", 22), ("norm_mix2", "norm_mix_2", 8), ("conv_w2", "conv_w_2", 32),
        ("conv_b2", "conv_b_2", 8), ("norm_ml", "norm_ml_out_2", 4), ("norm_cross", "norm_cross_2", 8),
        ("norm_mem", "norm_mem_2", 8), ("norm_ffn2", "norm_ffn_2", 8), ("norm_att", "norm_att_out_2", 4))


def vec_columns():
    at, out = 0, {}
    for name, _, n in VECS:
        if at < P < at + n:
            at = P
        out[name] = at
        at += n
    assert at <= 2 * P
    return out


VEC = vec_columns()


def stage_constants(nc, ctx, A, K, bank):
    rows_in, rows_zero, made, turned, kept = sems(ctx, nc, "c", "rows_in rows_zero made turned kept")
    ident, ones, vec, level, causal, sums_d = (K[n] for n in ("ident", "ones", "vec", "level", "causal", "reset"))
    lower = K["lower"]
    with ExitStack() as inner:
        rows = buffer(inner, nc, "vec_rows", [P, 2, P])
        block = inner.enter_context(nc.Block())

        @block.sync
        def _(sp):
            sp.wait_ge(rows_zero, 1)
            for name, source, n in VECS:
                a = A[source]
                v = a.rearrange("o (k p) -> (o k) p", p=P) if len(a.shape) == 2 else a.rearrange("o t (k p) -> (o t k) p", p=P)
                c = VEC[name]
                sp.dma_start(rows[c % P:c % P + n, c // P, :], v).then_inc(rows_in, 16)
            sp.wait_ge(rows_in, 16 * len(VECS))

        @block.gpsimd
        def _(pool):
            pool.memset(rows[:, :, :], 0.0).then_inc(rows_zero, 1)
            pool.memset(ones[:, :], 1.0).then_inc(made, 1)
            pool.memset(ident[:, :], 0.0).then_inc(made, 1)
            pool.memset(sums_d[:, :], 1.0).then_inc(made, 1)
            pool.memset(causal[:, :], 0.0).then_inc(made, 1)
            pool.memset(lower[:, :], 1.0).then_inc(made, 1)
            pool.wait_ge(made, 5)
            pool.affine_select(ident[:, :], ident[:, :], [[-1, P]], ALU.not_equal, 1.0, base=0, channel_multiplier=1).then_inc(made, 1)
            v = sums_d[:, :].rearrange("p (c t) -> p c t", t=P)
            pool.affine_select(v, v, [[0, HALF], [1, P]], ALU.not_equal, 0.0, base=0, channel_multiplier=0).then_inc(made, 1)
            pool.affine_select(causal[:, :], causal[:, :], [[1, P]], ALU.is_ge, NEG, base=0, channel_multiplier=-1).then_inc(made, 1)
            pool.affine_select(lower[:, :], lower[:, :], [[1, P]], ALU.is_gt, 0.0, base=0, channel_multiplier=-1).then_inc(made, 1)
            pool.wait_ge(made, 9)
            n = 9
            for l in range(LEVELS + 1):
                m = level[:, l, :]
                pool.memset(m, 1).then_inc(made, 1)
                n += 1
                pool.wait_ge(made, n)
                if l == LEVELS:
                    pool.affine_select(m, m, [[1, P]], ALU.is_equal, 0.0, base=0, channel_multiplier=-1).then_inc(made, 1)
                    n += 1
                    continue
                h = 1 << l
                blocks = P // (2 * h)
                v = m.rearrange("p (b u t) -> p b u t", u=2, t=h)
                for steps, base, sign in (([[0, blocks], [1, 2], [0, h]], -1, 0),
                                          ([[-2 * h, blocks], [0, 2], [0, h]], 0, 1),
                                          ([[2 * h, blocks], [0, 2], [0, h]], h - 1, -1)):
                    pool.affine_select(v, v, steps, ALU.is_ge, 0.0, base=base, channel_multiplier=sign).then_inc(made, 1)
                    n += 1
                    pool.wait_ge(made, n)

        @block.tensor
        def _(pe):
            pe.wait_ge(rows_in, 16 * len(VECS))
            pe.wait_ge(made, 6)
            for j in range(2):
                pe.transpose(bank[0][:, j * P:(j + 1) * P], rows[:, j, :], ident[:, :]).then_inc(turned, 1)

        @block.vector
        def _(dve):
            dve.memset(K["eps"][:, :], EPS)
            dve.wait_ge(turned, 2)
            dve.tensor_copy(vec[:, :], bank[0][:, 0:2 * P]).then_inc(kept, 1)


def product(pe, out, w, x, c, n, made=None):
    (wh, wl), (xh, xl) = w, x
    tiles = wh.shape[1]
    for t in range(tiles):
        if made is not None:
            pe.wait_ge(made, t + 1)
        pe.matmul(out, wh[:, t, :], xh[:, t, c:c + n], start=t == 0, stop=False)
        pe.matmul(out, wh[:, t, :], xl[:, t, c:c + n], start=False, stop=False)
        m = pe.matmul(out, wl[:, t, :], xh[:, t, c:c + n], start=False, stop=t == tiles - 1)
    return m


def split_high(act, x, xh, made, first=0, end=None):
    for t in range(first, end or xh.shape[1]):
        act.copy(xh[:, t, :], x[:, t, :]).then_inc(made, 1)


def split_low(dve, x, xh, xl, hi_made, made):
    for t in range(xh.shape[1]):
        dve.wait_ge(hi_made, t + 1)
        dve.tensor_tensor(xl[:, t, :], x[:, t, :], xh[:, t, :], ALU.subtract).then_inc(made, 1)


class Weights:

    def __init__(self, ctx, inner, nc, name, tiles, used):
        self.loaded0, self.loaded1, self.hi_made, self.lo_made = sems(ctx, nc, name, "w_in0 w_in1 w_hi w_lo")
        self.raw = buffer(inner, nc, name + "_w", [P, 2, tiles, P])
        self.hi = buffer(inner, nc, name + "_w_hi", [P, 2, tiles, P], F32R)
        self.lo = buffer(inner, nc, name + "_w_lo", [P, 2, tiles, P], F32R)
        self.used = used

    def load(self, sp, n, s, source):
        sp.wait_ge(self.lo_made, free(n))
        sp.dma_start(self.raw[:, s, :, :], source).then_inc((self.loaded0, self.loaded1)[s], 16)

    def high(self, act, n, s, round_):
        act.wait_ge((self.loaded0, self.loaded1)[s], 16 * round_ + 16)
        act.wait_ge(self.used, free(n))
        act.copy(self.hi[:, s, :, :], self.raw[:, s, :, :]).then_inc(self.hi_made, 1)

    def low(self, pool, n, s):
        pool.wait_ge(self.hi_made, n + 1)
        pool.tensor_tensor(self.lo[:, s, :, :], self.raw[:, s, :, :], self.hi[:, s, :, :], ALU.subtract).then_inc(self.lo_made, 1)

    def pair(self, s):
        return self.hi[:, s], self.lo[:, s]


def squares(act, x, cols, sq, sq_made, sq_used):
    for k in range(KD):
        act.wait_ge(sq_used, free(k))
        act.activation(sq[:, k % 2, 0:cols], x[:, k, 0:cols], ACT.Square).then_inc(sq_made, 1)


def sum_squares(pe, splits, sq, banks, ones, sq_made, sq_used):
    pe.sem_inc(sq_used, 2)
    for k in range(KD):
        pe.wait_ge(sq_made, k + 1)
        for j, (c, n) in enumerate(splits):
            m = pe.matmul(banks[j][:, 0:n], ones[:, :], sq[:, k % 2, c:c + n], start=k == 0, stop=k == KD - 1)
        m.then_inc(sq_used, 1)


def inverse_root(act, sums, out, eps, log_made, made, n=1, at=0, width=D):
    for j, (s, o) in enumerate(zip(sums, out)):
        act.activation(o, s, ACT.Ln, bias=eps, scale=1.0 / width).then_inc(log_made, 1)
    for j, o in enumerate(out):
        act.wait_ge(log_made, at + j + 1)
        act.activation(o, o, ACT.Exp, scale=-0.5).then_inc(made, 1)


def stage_load(nc, ctx, A, K, bank, h0, u, h0_dram):
    meta_in, x_in0, x_in1, low_turned, high_turned, meta_turned, low_kept, high_kept, sq_made, sq_used, logs, rstd_made, zeroed, stored = sems(
        ctx, nc, "l", "meta_in x_in0 x_in1 low_turned high_turned meta_turned low_kept high_kept sq_made sq_used logs rstd_made zeroed stored")
    x_in = (x_in0, x_in1)
    ident, ones, vec, eps = K["ident"], K["ones"], K["vec"], K["eps"]
    x = A["x"]
    with ExitStack() as inner:
        xs = buffer(inner, nc, "x_rows", [P, 2, D])
        mt = buffer(inner, nc, "meta_rows", [META, D])
        sq = buffer(inner, nc, "l_sq", [P, 2, WIDE])
        rstd = buffer(inner, nc, "l_rstd", [P, WIDE])
        block = inner.enter_context(nc.Block())

        @block.sync
        def _(sp):
            sp.dma_start(mt[:, :], A["meta_tokens"]).then_inc(meta_in, 16)
            with sp.Fori(0, NB // 2) as i:
                for s in range(2):
                    sp.wait_ge(high_turned, free(2 * i + s))
                    sp.dma_start(xs[:, s, :], x[0, ds((2 * i + s) * P, P), :]).then_inc(x_in[s], 16)
            sp.wait_ge(low_kept, ready(NB - 1))
            sp.wait_ge(high_kept, ready(NB - 1))
            sp.wait_ge(zeroed, 2)
            sp.dma_start(h0_dram, h0[:, :, :]).then_inc(stored, 16)
            sp.wait_ge(stored, 16)

        @block.tensor
        def _(pe):
            pe.sem_inc(high_turned, 2)
            pe.wait_ge(meta_in, 16)
            for k in range(KD):
                m = pe.transpose(bank[4][:, k * META:(k + 1) * META], mt[:, k * P:(k + 1) * P], ident[0:META, 0:META])
            m.then_inc(meta_turned, 1)
            with pe.Fori(0, NB // 2) as i:
                for s in range(2):
                    pe.wait_ge(x_in[s], 16 * i + 16)
                    pe.wait_ge(low_kept, free(2 * i + s))
                    for k in range(4):
                        m = pe.transpose(bank[2 * s][:, k * P:(k + 1) * P], xs[:, s, k * P:(k + 1) * P], ident[:, :])
                    m.then_inc(low_turned, 1)
                    pe.wait_ge(high_kept, free(2 * i + s))
                    for k in range(4):
                        m = pe.transpose(bank[2 * s + 1][:, k * P:(k + 1) * P], xs[:, s, (k + 4) * P:(k + 5) * P], ident[:, :])
                    m.then_inc(high_turned, 1)
            sum_squares(pe, FULL, sq, bank[5:8], ones, sq_made, sq_used)

        @block.vector
        def _(dve):
            dve.sem_inc(low_kept, 2)
            dve.memset(h0[:, :, 0:HEAD], 0.0).then_inc(zeroed, 1)
            dve.wait_ge(meta_turned, 1)
            dve.tensor_copy(h0[:, :, HEAD:P], bank[4][:, 0:KD * META].rearrange("p (k t) -> p k t", t=META)).then_inc(zeroed, 1)
            with dve.Fori(0, NB // 2) as i:
                for s in range(2):
                    dve.wait_ge(low_turned, 2 * i + s + 1)
                    dve.tensor_copy(h0[:, 0:4, ds((2 * i + s) * P + P, P)],
                                    bank[2 * s][:, :].rearrange("p (k t) -> p k t", t=P)).then_inc(low_kept, 1)
            dve.wait_ge(rstd_made, len(FULL))
            dve.wait_ge(high_kept, ready(NB - 1))
            for k in range(KD):
                dve.scalar_tensor_tensor(u[:, k, :], h0[:, k, :], vec[:, VEC["mix_pre"] + k:VEC["mix_pre"] + k + 1],
                                         rstd[:, :], ALU.mult, ALU.mult)

        @block.scalar
        def _(act):
            act.sem_inc(high_kept, 2)
            with act.Fori(0, NB // 2) as i:
                for s in range(2):
                    act.wait_ge(high_turned, ready(2 * i + s))
                    act.copy(h0[:, 4:8, ds((2 * i + s) * P + P, P)],
                             bank[2 * s + 1][:, :].rearrange("p (k t) -> p k t", t=P)).then_inc(high_kept, 1)
            act.wait_ge(low_kept, ready(NB - 1))
            act.wait_ge(high_kept, ready(NB - 1))
            act.wait_ge(zeroed, 2)
            squares(act, h0, WIDE, sq, sq_made, sq_used)
            act.wait_ge(sq_used, ready(KD - 1))
            inverse_root(act, [bank[5 + j][:, 0:n] for j, (c, n) in enumerate(FULL)],
                         [rstd[:, c:c + n] for c, n in FULL], eps[:, 0:1], logs, rstd_made)


def stage_hgrn_in(nc, ctx, A, K, bank, u, q, k, lf, v):
    w0, w1, wv0, mm, taken, vmm, vkept, lb_made, sig, logged, small, fixed = sems(
        ctx, nc, "p", "w0 w1 wv0 mm taken vmm vkept lb_made sig logged small fixed")
    w_in = (w0, w1)
    vec = K["vec"]
    w = A["w_in"][0].rearrange("(k p) n -> p k n", p=P)
    lbc = VEC["lb"]
    with ExitStack() as inner:
        ring = buffer(inner, nc, "p_ring", [P, 2, KD, P])
        wv = buffer(inner, nc, "p_wv", [P, KD, 4 * P])
        lb = buffer(inner, nc, "lb", [P, 4, 4])
        f = buffer(inner, nc, "f_tile", [P, WIDE])
        tiny = buffer(inner, nc, "f_tiny", [P, WIDE])
        block = inner.enter_context(nc.Block())

        @block.sync
        def _(sp):
            with sp.Fori(0, HALF) as i:
                for s in range(2):
                    sp.wait_ge(mm, free(2 * i + s))
                    sp.dma_start(ring[:, s, :, :], w[:, :, ds((2 * i + s) * P, P)]).then_inc(w_in[s], 16)
            sp.dma_start(wv[:, :, :], w[:, :, 8 * P:12 * P]).then_inc(wv0, 16)

        @block.tensor
        def _(pe):
            pe.sem_inc(mm, 2)
            with pe.Fori(0, HALF) as i:
                for s in range(2):
                    pe.wait_ge(w_in[s], 16 * i + 16)
                    pe.wait_ge(taken, free(2 * i + s))
                    for j, (c, n) in enumerate(REAL):
                        for t in range(KD):
                            m = pe.matmul(bank[3 * s + j][:, 0:n], ring[:, s, t, :], u[:, t, c:c + n], start=t == 0, stop=t == KD - 1)
                    m.then_inc(mm, 1)
            pe.wait_ge(wv0, 16)
            for c in range(CHUNKS):
                pe.wait_ge(vkept, free(c))
                for t in range(KD):
                    m = pe.matmul(bank[6 + c % 2][:, :], u[:, t, c * P:(c + 1) * P], wv[:, t, :], start=t == 0, stop=t == KD - 1)
                m.then_inc(vmm, 1)

        @block.scalar
        def _(act):
            act.wait_ge(lb_made, 1)
            act.activation(lb[:, 0, :], lb[:, 1, :], ACT.Exp).then_inc(lb_made, 1)
            act.sem_inc(taken, 2)
            with act.Fori(0, HALF // 2) as i:
                for s in range(2):
                    act.wait_ge(mm, ready(2 * i + s))
                    for j, (c, n) in enumerate(REAL):
                        a = act.copy(q[:, ds(2 * i + s, 1), c:c + n], bank[3 * s + j][:, 0:n])
                    a.then_inc(taken, 1)
            for t in range(HALF):
                s = t % 2
                act.wait_ge(mm, ready(HALF + t))
                act.wait_ge(small, t + 1)
                for j, (c, n) in enumerate(REAL):
                    act.activation(f[:, c:c + n], bank[3 * s + j][:, 0:n], ACT.Sigmoid)
                    a = act.activation(k[:, t, c:c + n], bank[3 * s + j][:, 0:n], ACT.Sigmoid, scale=-1.0)
                a.then_inc(taken, 1)
                act.wait_ge(fixed, t + 1)
                act.activation(lf[:, t, HEAD:], f[:, HEAD:], ACT.Ln).then_inc(logged, 1)

        @block.vector
        def _(dve):
            n = 0

            def then(ins):
                nonlocal n
                n += 1
                ins.then_inc(logged_own, 1)
                dve.wait_ge(logged_own, n)
            logged_own = sig
            then(dve.memset(q[:, :, 0:HEAD], 0.0))
            dve.memset(k[:, :, 0:HEAD], 0.0)
            dve.memset(lf[:, :, 0:HEAD], 0.0)
            dve.tensor_tensor(lb[:, 1, :], vec[:, lbc:lbc + 4], vec[:, lbc:lbc + 4], ALU.subtract).then_inc(lb_made, 1)
            dve.wait_ge(lb_made, 2)
            then(dve.reciprocal(lb[:, 1, :], lb[:, 0, :]))
            then(dve.tensor_tensor(lb[:, 0, :], lb[:, 0, :], lb[:, 1, :], ALU.mult))
            then(dve.tensor_tensor(lb[:, 2, :], lb[:, 0, :], lb[:, 0, :], ALU.subtract))
            then(dve.tensor_scalar(lb[:, 2, :], lb[:, 2, :], 0.0, 1.0, ALU.max, ALU.min))
            then(dve.tensor_scalar(lb[:, 3, :], lb[:, 2, :], -1.0, 1.0, ALU.mult, ALU.add))
            dve.sem_inc(small, 1)
            for t in range(HALF):
                dve.wait_ge(taken, ready(HALF + t))
                then(dve.tensor_scalar(f[:, HEAD:], f[:, HEAD:], lb[:, 3, t:t + 1], lb[:, 2, t:t + 1], ALU.mult, ALU.add))
                then(dve.tensor_scalar(f[:, HEAD:], f[:, HEAD:], 1e-30, None, ALU.max))
                then(dve.tensor_scalar(tiny[:, HEAD:], f[:, HEAD:], 2.0 ** -60, None, ALU.is_lt))
                then(dve.tensor_scalar(tiny[:, HEAD:], tiny[:, HEAD:], 2.0 ** 64 - 1.0, 1.0, ALU.mult, ALU.add))
                dve.tensor_tensor(f[:, HEAD:], f[:, HEAD:], tiny[:, HEAD:], ALU.mult).then_inc(fixed, 1)
                dve.wait_ge(fixed, t + 1)
                then(dve.tensor_scalar(tiny[:, HEAD:], tiny[:, HEAD:], 2.0, -64 * LN2, ALU.is_ge, ALU.mult))
                dve.wait_ge(logged, t + 1)
                then(dve.tensor_tensor(lf[:, t, HEAD:], lf[:, t, HEAD:], tiny[:, HEAD:], ALU.add))
                then(dve.tensor_scalar(k[:, t, HEAD:], k[:, t, HEAD:], lb[:, 3, t:t + 1], None, ALU.mult))
                dve.sem_inc(small, 1)
            dve.sem_inc(vkept, 2)
            for c in range(CHUNKS):
                dve.wait_ge(vmm, c + 1)
                dve.tensor_copy(v[:, c, :], bank[6 + c % 2][:, :]).then_inc(vkept, 1)


def constants(ctx, nc):
    return {"ident": buffer(ctx, nc, "ident", [P, P]), "ones": buffer(ctx, nc, "ones", [P, P]),
            "vec": buffer(ctx, nc, "vec", [P, 2 * P]), "level": buffer(ctx, nc, "level", [P, LEVELS + 1, P], I32),
            "causal": buffer(ctx, nc, "causal", [P, P]), "reset": buffer(ctx, nc, "reset", [P, BANK]),
            "lower": buffer(ctx, nc, "lower", [P, P]), "eps": buffer(ctx, nc, "eps", [P, 1])}


def stage_hgrn(nc, ctx, A, K, bank, q, k, lf, v, o, spare):
    staged, summed, subbed, exped, scaled, scored, picked, turned, kd_kept, added, state_made, o_mm, o_kept, cleared, waited = sems(
        ctx, nc, "h", "staged summed subbed exped scaled scored picked turned kd_kept added state_made o_mm o_kept cleared waited")
    ident, level, reset = K["ident"], K["level"], K["reset"]
    NX = LEVELS + 2
    LAST = CHUNKS - 1
    with ExitStack() as inner:
        lfc = buffer(inner, nc, "lf_chunk", [P, 2, BANK])
        kc = buffer(inner, nc, "k_chunk", [P, 2, BANK])
        vc = buffer(inner, nc, "v_chunk", [P, 2, BANK])
        b = buffer(inner, nc, "b_chunk", [P, BANK])
        x = buffer(inner, nc, "scaled_chunk", [P, 2, NX, BANK])
        kdt = buffer(inner, nc, "kd_tok", [P, BANK])
        qe, sc, st = (spare[:, j * 2 * BANK:(j + 1) * 2 * BANK].rearrange("p (s n) -> p s n", s=2) for j in range(3))
        block = inner.enter_context(nc.Block())

        def heads(ap):
            return ap.rearrange("p (h t) -> p h t", t=P)

        def halves(ap, l):
            w = ap.rearrange("p (n u t) -> p n u t", u=2, t=1 << l)
            return w[:, :, 0, :], w[:, :, 1, :]

        @block.gpsimd
        def _(pool):
            def stage(c, s):
                pool.wait_ge(o_mm, free(c))
                pool.tensor_copy(heads(lfc[:, s, :]), lf[:, :, ds(c * P, P)]).then_inc(staged, 1)
                pool.tensor_copy(heads(kc[:, s, :]), k[:, :, ds(c * P, P)]).then_inc(staged, 1)
                pool.tensor_copy(vc[:, s, :], v[:, ds(c, 1), :].rearrange("p a n -> p (a n)")).then_inc(staged, 1)
            with pool.Fori(0, LAST // 2) as i:
                for s in range(2):
                    stage(2 * i + s, s)
            stage(LAST, LAST % 2)

        @block.vector
        def _(dve):
            dve.memset(sc[:, :, :], 0.0).then_inc(cleared, 1)
            dve.memset(st[:, 0, :], 0.0).then_inc(state_made, 1)
            dve.sem_inc(picked, 4)

            def differences(c, s):
                dve.wait_ge(staged, 3 * c + 3)
                dve.tensor_tensor_scan(b[:, :], reset[:, :], lfc[:, s, :], 0.0, ALU.mult, ALU.add).then_inc(summed, 1)
                dve.wait_ge(summed, c + 1)
                for l in range(LEVELS):
                    left, right = halves(b[:, :], l)
                    x_left, x_right = halves(x[:, s, l, :], l)
                    middle = left[:, :, (1 << l) - 1:1 << l].to_broadcast(list(left.shape))
                    dve.tensor_tensor(x_left, middle, left, ALU.subtract)
                    dve.tensor_tensor(x_right, right, middle, ALU.subtract)
                last = heads(b[:, :])[:, :, P - 1:P].to_broadcast([P, HALF, P])
                dve.tensor_tensor(heads(x[:, s, LEVELS + 1, :]), last, heads(b[:, :]), ALU.subtract).then_inc(subbed, 1)

            def scale(c, s):
                qc = q[:, :, ds(c * P, P)]
                for l in range(LEVELS):
                    if l % 3 == 0:
                        dve.wait_ge(exped, 3 * c + l // 3 + 1)
                    x_left, x_right = halves(x[:, s, l, :], l)
                    k_left, _ = halves(kc[:, s, :], l)
                    dve.tensor_tensor(x_left, x_left, k_left, ALU.mult)
                    w = qc.rearrange("p h (n u t) -> p h n u t", u=2, t=1 << l)[:, :, :, 1, :]
                    y = x[:, s, l, :].rearrange("p (h n u t) -> p h n u t", h=HALF, u=2, t=1 << l)[:, :, :, 1, :]
                    dve.tensor_tensor(y, y, w, ALU.mult).then_inc(scaled, 1)
                dve.tensor_tensor(heads(qe[:, s, :]), heads(x[:, s, LEVELS, :]), qc, ALU.mult).then_inc(scaled, 1)
                dve.tensor_tensor(x[:, s, LEVELS + 1, :], x[:, s, LEVELS + 1, :], kc[:, s, :], ALU.mult).then_inc(scaled, 1)

            def pick(c, s):
                for l in range(LEVELS + 1):
                    dve.wait_ge(scored, 8 * c + l + 1)
                    dve.wait_ge(picked, 8 * c + l + 4)
                    dve.sem_inc(waited, 1)
                    dve.wait_ge(cleared, 1)
                    mask = level[:, l:l + 1, :].to_broadcast([P, HALF, P])
                    dve.copy_predicated(heads(sc[:, s, :]), mask, heads(bank[l % 4][:, :])).then_inc(picked, 1)
                dve.wait_ge(added, c + 1)
                for h in range(HALF):
                    m = dve.scalar_tensor_tensor(st[:, 1 - s, h * P:(h + 1) * P], st[:, s, h * P:(h + 1) * P],
                                                 x[:, s, LEVELS, (h + 1) * P - 1:(h + 1) * P],
                                                 bank[6][:, h * P:(h + 1) * P], ALU.mult, ALU.add)
                m.then_inc(state_made, 1)
            differences(0, 0)
            with dve.Fori(0, LAST // 2) as i:
                for s in range(2):
                    scale(2 * i + s, s)
                    differences(2 * i + s + 1, 1 - s)
                    pick(2 * i + s, s)
            scale(LAST, LAST % 2)
            pick(LAST, LAST % 2)

        @block.scalar
        def _(act):
            act.sem_inc(kd_kept, 1)
            act.sem_inc(o_kept, 1)

            def exponentials(c, s):
                act.wait_ge(subbed, c + 1)
                for g in range(2):
                    y = x[:, s, 3 * g:3 * g + 3, :]
                    act.activation(y, y, ACT.Exp).then_inc(exped, 1)
                act.activation(x[:, s, LEVELS, :], b[:, :], ACT.Exp)
                for l in (LEVELS - 1, LEVELS + 1):
                    e = act.activation(x[:, s, l, :], x[:, s, l, :], ACT.Exp)
                e.then_inc(exped, 1)

            def evacuate(c):
                act.wait_ge(turned, c + 1)
                act.copy(kdt[:, :], bank[4][:, :]).then_inc(kd_kept, 1)
                act.wait_ge(o_mm, ready(c))
                act.copy(o[:, :, ds(c * P, P)], heads(bank[5][:, :])).then_inc(o_kept, 1)
            exponentials(0, 0)
            with act.Fori(0, LAST // 2) as i:
                for s in range(2):
                    exponentials(2 * i + s + 1, 1 - s)
                    evacuate(2 * i + s)
            evacuate(LAST)

        @block.tensor
        def _(pe):
            pe.sem_inc(o_mm, 2)

            def chunk(c, s):
                for l in range(LEVELS + 1):
                    pe.wait_ge(scaled, 9 * c + min(l, LEVELS - 1) + 1)
                    pe.wait_ge(picked, 8 * c + l + 1)
                    for h in range(HALF):
                        col = slice(h * P, (h + 1) * P)
                        if l < LEVELS:
                            m = pe.matmul(bank[l % 4][:, col], x[:, s, l, col], x[:, s, l, col], start=True, stop=True)
                        else:
                            m = pe.matmul(bank[l % 4][:, col], kc[:, s, col], q[:, ds(h, 1), ds(c * P, P)], start=True, stop=True)
                    m.then_inc(scored, 1)
                pe.wait_ge(scaled, 9 * c + 9)
                pe.wait_ge(kd_kept, c + 1)
                for h in range(HALF):
                    m = pe.transpose(bank[4][:, h * P:(h + 1) * P], x[:, s, LEVELS + 1, h * P:(h + 1) * P], ident[:, :])
                m.then_inc(turned, 1)
                pe.wait_ge(state_made, c + 1)
                pe.wait_ge(kd_kept, c + 2)
                for h in range(HALF):
                    col = slice(h * P, (h + 1) * P)
                    m = pe.matmul(bank[6][:, col], kdt[:, col], vc[:, s, col], start=True, stop=True)
                m.then_inc(added, 1)
                pe.wait_ge(picked, 8 * c + 12)
                pe.wait_ge(o_kept, c + 1)
                for h in range(HALF):
                    col = slice(h * P, (h + 1) * P)
                    pe.matmul(bank[5][:, col], vc[:, s, col], sc[:, s, col], start=True, stop=False)
                    m = pe.matmul(bank[5][:, col], st[:, s, col], qe[:, s, col], start=False, stop=True)
                m.then_inc(o_mm, 1)
            with pe.Fori(0, LAST // 2) as i:
                for s in range(2):
                    chunk(2 * i + s, s)
            chunk(LAST, LAST % 2)


def stage_branches(nc, ctx, A, K, bank, u, o, p):
    (sq_made, sums, logs, rstd_made, normed, w0, w1, mm, g_taken, gated, v_taken, chain, pooled, proj_in, ymm, y_taken) = sems(
        ctx, nc, "b", "sq_made sums logs rstd_made normed w0 w1 mm g_taken gated v_taken chain pooled proj_in ymm y_taken")
    w_in = (w0, w1)
    ones, vec, eps = K["ones"], K["vec"], K["eps"]
    w = A["w_in"][0].rearrange("(k p) n -> p k n", p=P)
    G0, V0 = 3 * HALF, 4 * HALF
    with ExitStack() as inner:
        ring = buffer(inner, nc, "b_ring", [P, 2, KD, P])
        proj = buffer(inner, nc, "pool_proj", [P, HALF, P])
        sq = buffer(inner, nc, "b_sq", [P, LIVE])
        rstd = buffer(inner, nc, "b_rstd", [P, LIVE])
        sig = buffer(inner, nc, "b_sig", [P, 2, LIVE])
        v = buffer(inner, nc, "pool_v", [P, HALF, WIDE])
        s0 = buffer(inner, nc, "pool_sum0", [P, HALF, WIDE])
        s1 = buffer(inner, nc, "pool_sum1", [P, HALF, WIDE])
        block = inner.enter_context(nc.Block())

        @block.sync
        def _(sp):
            sp.dma_start(proj[:, :, :], A["pool_proj"][0].rearrange("g c d -> c g d")).then_inc(proj_in, 16)
            with sp.Fori(0, HALF) as i:
                for s in range(2):
                    sp.wait_ge(mm, free(2 * i + s))
                    sp.dma_start(ring[:, s, :, :], w[:, :, ds((2 * i + s + G0) * P, P)]).then_inc(w_in[s], 16)

        @block.tensor
        def _(pe):
            pe.sem_inc(mm, 2)
            for h in range(HALF):
                pe.wait_ge(sq_made, h + 1)
                if h:
                    pe.wait_ge(rstd_made, 3 * h)
                for j, (c, n) in enumerate(LIVES):
                    m = pe.matmul(bank[5 + j][:, 0:n], ones[:, :], sq[:, c:c + n], start=True, stop=True)
                m.then_inc(sums, 1)
            pe.wait_ge(rstd_made, 12)
            with pe.Fori(0, HALF // 2) as i:
                for s in range(2):
                    pe.wait_ge(w_in[s], 16 * i + 16)
                    pe.wait_ge(g_taken, free(2 * i + s))
                    for j, (c, n) in enumerate(LIVES):
                        for t in range(KD):
                            m = pe.matmul(bank[3 * s + j][:, 0:n], ring[:, s, t, :], u[:, t, FIRST + c:FIRST + c + n], start=t == 0, stop=t == KD - 1)
                    m.then_inc(mm, 1)
            with pe.Fori(0, HALF // 2) as i:
                for s in range(2):
                    pe.wait_ge(w_in[s], 16 * i + 48)
                    pe.wait_ge(g_taken, ready(HALF - 1))
                    pe.wait_ge(v_taken, free(2 * i + s))
                    for j, (c, n) in enumerate(REAL):
                        for t in range(KD):
                            m = pe.matmul(bank[3 * s + j][:, 0:n], ring[:, s, t, :], u[:, t, c:c + n], start=t == 0, stop=t == KD - 1)
                    m.then_inc(mm, 1)
            pe.wait_ge(proj_in, 16)
            pe.wait_ge(v_taken, ready(HALF - 1))
            for g in range(HALF):
                pe.wait_ge(pooled, g + 1)
                pe.wait_ge(y_taken, free(g))
                for j, (c, n) in enumerate(LIVES):
                    m = pe.matmul(bank[3 * (g % 2) + j][:, 0:n], proj[:, g, :], s0[:, g, FIRST + c:FIRST + c + n], start=True, stop=True)
                m.then_inc(ymm, 1)

        @block.scalar
        def _(act):
            act.sem_inc(g_taken, 2)
            act.sem_inc(v_taken, 2)
            act.sem_inc(y_taken, 2)
            for h in range(HALF):
                if h:
                    act.wait_ge(sums, h)
                act.activation(sq[:, :], o[:, h, FIRST:], ACT.Square).then_inc(sq_made, 1)
                act.wait_ge(sums, h + 1)
                if h:
                    act.wait_ge(normed, h)
                inverse_root(act, [bank[5 + j][:, 0:n] for j, (c, n) in enumerate(LIVES)],
                             [rstd[:, c:c + n] for c, n in LIVES], eps[:, 0:1], logs, rstd_made, at=3 * h, width=P)
            for t in range(HALF):
                s = t % 2
                act.wait_ge(mm, ready(t))
                if t >= 2:
                    act.wait_ge(gated, t - 1)
                for j, (c, n) in enumerate(LIVES):
                    a = act.activation(sig[:, s, c:c + n], bank[3 * s + j][:, 0:n], ACT.Sigmoid)
                a.then_inc(g_taken, 1)
            for t in range(HALF):
                act.wait_ge(mm, ready(HALF + t))
                for j, (c, n) in enumerate(REAL):
                    a = act.copy(v[:, t, c:c + n], bank[3 * (t % 2) + j][:, 0:n])
                a.then_inc(v_taken, 1)
            for g in range(HALF):
                act.wait_ge(ymm, g + 1)
                for j, (c, n) in enumerate(LIVES):
                    a = act.mul(p[:, g, c:c + n], bank[3 * (g % 2) + j][:, 0:n], vec[:, VEC["pool_scale"] + g:VEC["pool_scale"] + g + 1])
                a.then_inc(y_taken, 1)

        @block.vector
        def _(dve):
            n = 0

            def then(ins):
                nonlocal n
                n += 1
                ins.then_inc(chain, 1)
                dve.wait_ge(chain, n)
            dve.memset(v[:, :, 0:HEAD], 0.0)
            for h in range(HALF):
                dve.wait_ge(rstd_made, 3 * h + 3)
                dve.scalar_tensor_tensor(o[:, h, FIRST:], o[:, h, FIRST:], vec[:, VEC["out_norm"] + h:VEC["out_norm"] + h + 1],
                                         rstd[:, :], ALU.mult, ALU.mult).then_inc(normed, 1)
            for t in range(HALF):
                dve.wait_ge(g_taken, ready(t))
                dve.wait_ge(normed, t + 1)
                dve.tensor_tensor(o[:, t, FIRST:], o[:, t, FIRST:], sig[:, t % 2, :], ALU.mult).then_inc(gated, 1)
            for g in range(HALF):
                dve.wait_ge(v_taken, ready(g))
                src = v
                for e in range(g + 1):
                    dst = (s0, s1)[(g - e) % 2]
                    back = 1 << e
                    lo = P - 16 + back
                    then(dve.tensor_tensor(dst[:, g, lo:], src[:, g, lo:], src[:, g, lo - back:WIDE - back], ALU.add))
                    if e < g:
                        then(dve.tensor_copy(dst[:, g, HEAD:lo], src[:, g, HEAD:lo]))
                    src = dst
                size = 2 << g
                if size > FIRST - HEAD + 1:
                    short = FIRST - HEAD + 1
                    then(dve.scalar_tensor_tensor(s0[:, g, FIRST:FIRST + 1], s0[:, g, FIRST:FIRST + 1], 1.0 / short, v[:, g, FIRST:FIRST + 1], ALU.mult, ALU.subtract))
                    dve.scalar_tensor_tensor(s0[:, g, FIRST + 1:], s0[:, g, FIRST + 1:], 1.0 / size, v[:, g, FIRST + 1:], ALU.mult, ALU.subtract).then_inc(pooled, 1)
                else:
                    dve.scalar_tensor_tensor(s0[:, g, FIRST:], s0[:, g, FIRST:], 1.0 / size, v[:, g, FIRST:], ALU.mult, ALU.subtract).then_inc(pooled, 1)


def stage_split(nc, ctx, name, x, pair):
    hi_made, lo_made = sems(ctx, nc, name, "hi_made lo_made")
    with nc.Block() as block:
        @block.scalar
        def _(act):
            split_high(act, x, pair[0], hi_made)

        @block.vector
        def _(dve):
            split_low(dve, x, pair[0], pair[1], hi_made, lo_made)


def stage_mix(nc, ctx, A, K, bank, u, o, p, z):
    w_in, hi_made, lo_made, b0, b1, mm, sig_made, multiplied, added = sems(
        ctx, nc, "z", "w_in hi_made lo_made b0 b1 mm sig_made multiplied added")
    b_in = (b0, b1)
    w = A["w_in"][0].rearrange("(k p) n -> p k n", p=P)
    w_hgrn = A["w_branch_hgrn"][0].rearrange("(k p) n -> p k n", p=P)
    w_pool = A["w_branch_pool"][0].rearrange("(k p) n -> p k n", p=P)
    GA, GB = 5 * HALF, 7 * HALF
    with ExitStack() as inner:
        raw = buffer(inner, nc, "z_w", [P, 2 * KD, P])
        wh = buffer(inner, nc, "z_w_hi", [P, 2, 2 * KD, P], F32R)
        wl = buffer(inner, nc, "z_w_lo", [P, 2, 2 * KD, P], F32R)
        ring = buffer(inner, nc, "z_branches", [P, 2, 2 * HALF, P])
        sig = buffer(inner, nc, "z_sig", [P, 2, 2, 342])
        block = inner.enter_context(nc.Block())

        @block.sync
        def _(sp):
            with sp.Fori(0, KD // 2) as i:
                for s in range(2):
                    n = 2 * i + s
                    sp.wait_ge(lo_made, n + 1)
                    sp.dma_start(raw[:, 0:KD, :], w[:, :, ds((n + GA) * P, P)]).then_inc(w_in, 16)
                    sp.dma_start(raw[:, KD:, :], w[:, :, ds((n + GB) * P, P)]).then_inc(w_in, 16)
                    sp.wait_ge(mm, 6 * i + 3 * s + 3)
                    sp.dma_start(ring[:, s, 0:HALF, :], w_hgrn[:, :, ds(n * P, P)]).then_inc(b_in[s], 16)
                    sp.dma_start(ring[:, s, HALF:, :], w_pool[:, :, ds(n * P, P)]).then_inc(b_in[s], 16)

        @block.tensor
        def _(pe):
            pe.sem_inc(mm, 6)
            with pe.Fori(0, KD // 2) as i:
                for s in range(2):
                    pe.wait_ge(lo_made, 2 * i + s + 2)
                    pe.wait_ge(b_in[s], 32 * i + 32)
                    for j, (c, n) in enumerate(LIVES):
                        e = 3 * s + j
                        b = bank[4 * (e % 2):4 * (e % 2) + 4]
                        pe.wait_ge(multiplied, 6 * i + e + 1)
                        for g in range(2):
                            tiles = slice(KD * g, KD * (g + 1))
                            product(pe, b[g][:, 0:n], (wh[:, s, tiles, :], wl[:, s, tiles, :]), u, c, n)
                        for t in range(HALF):
                            pe.matmul(b[2][:, 0:n], ring[:, s, t, :], o[:, t, FIRST + c:FIRST + c + n], start=t == 0, stop=t == HALF - 1)
                        for t in range(HALF):
                            m = pe.matmul(b[3][:, 0:n], ring[:, s, HALF + t, :], p[:, t, c:c + n], start=t == 0, stop=t == HALF - 1)
                        m.then_inc(mm, 1)

        @block.scalar
        def _(act):
            def high(n, s):
                act.wait_ge(w_in, 32 * n + 32)
                act.wait_ge(mm, 3 * n + 3)
                act.copy(wh[:, s, :, :], raw[:, :, :]).then_inc(hi_made, 1)

            def gates(t, s):
                for j, (c, n) in enumerate(LIVES):
                    e = 3 * s + j
                    act.wait_ge(mm, 3 * t + j + 7)
                    act.wait_ge(added, 3 * t + j + 1)
                    act.activation(sig[:, e % 2, 0, 0:n], bank[4 * (e % 2)][:, 0:n], ACT.Sigmoid)
                    act.activation(sig[:, e % 2, 1, 0:n], bank[4 * (e % 2) + 1][:, 0:n], ACT.Sigmoid).then_inc(sig_made, 1)
            high(0, 0)
            with act.Fori(0, KD // 2 - 1) as i:
                for s in range(2):
                    high(2 * i + s + 1, 1 - s)
                    gates(2 * i + s, s)
            high(KD - 1, 1)
            gates(KD - 2, 0)
            gates(KD - 1, 1)

        @block.vector
        def _(dve):
            dve.sem_inc(multiplied, 2)
            with dve.Fori(0, KD // 2) as i:
                for e in range(6):
                    n = LIVES[e % 3][1]
                    dve.wait_ge(sig_made, 6 * i + e + 1)
                    for g in range(2):
                        m = dve.tensor_tensor(sig[:, e % 2, g, 0:n], sig[:, e % 2, g, 0:n], bank[4 * (e % 2) + 2 + g][:, 0:n], ALU.mult)
                    m.then_inc(multiplied, 1)

        @block.gpsimd
        def _(pool):
            pool.sem_inc(added, 2)
            pool.sem_inc(lo_made, 1)

            def low(n, s):
                pool.wait_ge(hi_made, n + 1)
                pool.tensor_tensor(wl[:, s, :, :], raw[:, :, :], wh[:, s, :, :], ALU.subtract).then_inc(lo_made, 1)

            def add(t, s):
                for j, (c, n) in enumerate(LIVES):
                    e = 3 * s + j
                    pool.wait_ge(multiplied, 3 * t + j + 3)
                    pool.tensor_tensor(z[:, ds(t, 1), c:c + n], sig[:, e % 2, 0, 0:n], sig[:, e % 2, 1, 0:n], ALU.add).then_inc(added, 1)
            low(0, 0)
            with pool.Fori(0, KD // 2 - 1) as i:
                for s in range(2):
                    low(2 * i + s + 1, 1 - s)
                    add(2 * i + s, s)
            low(KD - 1, 1)
            add(KD - 2, 0)
            add(KD - 1, 1)


def stage_project(nc, ctx, A, K, bank, name, weights, tiles_in, x, y, acc, splits, h, h_load):
    mm, kept, squared, added, h_in, x_hi, x_lo = sems(ctx, nc, name, "mm kept squared added h_in x_hi x_lo")
    w = weights.rearrange("(k p) n -> p k n", p=P)
    cols = splits[-1][0] + splits[-1][1]
    ns = len(splits)
    with ExitStack() as inner:
        wt = Weights(ctx, inner, nc, name, tiles_in, mm)
        xh, xl = (buffer(inner, nc, name + n, [P, tiles_in, cols], F32R) for n in ("_x_hi", "_x_lo"))
        sq = buffer(inner, nc, name + "_sq", [P, 2, cols])
        block = inner.enter_context(nc.Block())

        @block.sync
        def _(sp):
            sp.dma_start(h[:, :, :], h_load).then_inc(h_in, 16)
            with sp.Fori(0, KD // 2) as i:
                for s in range(2):
                    wt.load(sp, 2 * i + s, s, w[:, :, ds((2 * i + s) * P, P)])
            sp.wait_ge(h_in, 16)

        @block.tensor
        def _(pe):
            pe.sem_inc(mm, 2)

            def tile(n, s, made=None):
                pe.wait_ge(wt.lo_made, ready(n))
                pe.wait_ge(kept, free(n))
                for j, (c, w_) in enumerate(splits):
                    m = product(pe, bank[ns * s + j][:, 0:w_], wt.pair(s), (xh, xl), c, w_, made)
                m.then_inc(mm, 1)
            tile(0, 0, x_lo)
            tile(1, 1)
            with pe.Fori(1, KD // 2) as i:
                for s in range(2):
                    tile(2 * i + s, s)

        @block.vector
        def _(dve):
            dve.sem_inc(kept, 2)
            split_low(dve, x, xh, xl, x_hi, x_lo)
            with dve.Fori(0, KD // 2) as i:
                for s in range(2):
                    dve.wait_ge(mm, ready(2 * i + s))
                    for j, (c, n) in enumerate(splits):
                        m = dve.tensor_copy(y[:, ds(2 * i + s, 1), c:c + n], bank[ns * s + j][:, 0:n])
                    m.then_inc(kept, 1)

        @block.scalar
        def _(act):
            act.sem_inc(squared, 2)

            def square(n, s):
                act.wait_ge(kept, ready(n))
                act.wait_ge(added, free(n))
                act.activation(sq[:, s, :], y[:, ds(n, 1), 0:cols], ACT.Square).then_inc(squared, 1)
            split_high(act, x, xh, x_hi, 0, 2)
            wt.high(act, 0, 0, 0)
            split_high(act, x, xh, x_hi, 2)
            wt.high(act, 1, 1, 0)
            with act.Fori(0, KD // 2 - 1) as i:
                for s in range(2):
                    wt.high(act, 2 * i + s + 2, s, i + 1)
                    square(2 * i + s, s)
            square(KD - 2, 0)
            square(KD - 1, 1)

        @block.gpsimd
        def _(pool):
            pool.sem_inc(added, 2)
            pool.sem_inc(wt.lo_made, 2)
            wt.low(pool, 0, 0)
            wt.low(pool, 1, 1)
            for n in range(KD):
                if n + 2 < KD:
                    wt.low(pool, n + 2, n % 2)
                pool.wait_ge(squared, ready(n))
                if n == 0:
                    pool.tensor_copy(acc[:, :], sq[:, 0, :]).then_inc(added, 1)
                else:
                    pool.wait_ge(added, ready(n - 1))
                    pool.tensor_tensor(acc[:, :], acc[:, :], sq[:, n % 2, :], ALU.add).then_inc(added, 1)


def stage_add_norm(nc, ctx, A, K, bank, name, y, acc, h, gain, splits, h_store, u, u_gain):
    sums, logs, rstd_made, scaled, h_even, h_odd, sq_made, sq_used, logs2, rstd2, u_made, u_hi, stored = sems(
        ctx, nc, name, "sums logs rstd_made scaled h_even h_odd sq_made sq_used logs2 rstd2 u_made u_hi stored")
    ones, vec, eps = K["ones"], K["vec"], K["eps"]
    cols = splits[-1][0] + splits[-1][1]
    ns = len(splits)
    with ExitStack() as inner:
        sq = buffer(inner, nc, name + "_h_sq", [P, 2, cols])
        rstd = buffer(inner, nc, name + "_rstd", [P, cols])
        block = inner.enter_context(nc.Block())

        @block.sync
        def _(sp):
            for g in range(2):
                sp.wait_ge(h_even, KD // 4 * (g + 1))
                sp.wait_ge(h_odd, KD // 4 * (g + 1))
                half = slice(KD // 2 * g, KD // 2 * (g + 1))
                sp.dma_start(h_store[:, half, :], h[:, half, :]).then_inc(stored, 16)
            sp.wait_ge(stored, 32)

        @block.tensor
        def _(pe):
            for j, (c, n) in enumerate(splits):
                m = pe.matmul(bank[j][:, 0:n], ones[:, :], acc[:, c:c + n], start=True, stop=True)
            m.then_inc(sums, 1)
            pe.sem_inc(sq_used, 2)
            for k in range(KD):
                pe.wait_ge(sq_made, k + 1)
                for j, (c, n) in enumerate(splits):
                    m = pe.matmul(bank[ns + j][:, 0:n], ones[:, :], sq[:, k % 2, c:c + n], start=k == 0, stop=k == KD - 1)
                m.then_inc(sq_used, 1)

        @block.vector
        def _(dve):
            dve.wait_ge(rstd_made, ns)

            def add(k):
                dve.wait_ge(scaled, k + 1)
                dve.tensor_tensor(h[:, k, :], h[:, k, :], y[:, k, 0:cols], ALU.add).then_inc(h_odd, 1)
            for k in range(KD):
                dve.scalar_tensor_tensor(y[:, k, 0:cols], y[:, k, 0:cols], vec[:, VEC[gain] + k:VEC[gain] + k + 1], rstd[:, :],
                                         ALU.mult, ALU.mult).then_inc(scaled, 1)
                if k % 2 == 0 and k:
                    add(k - 1)
            add(KD - 1)
            dve.wait_ge(rstd2, ns)
            dve.wait_ge(h_even, KD // 2)
            dve.wait_ge(h_odd, KD // 2)

            def low(k):
                dve.wait_ge(u_hi, k + 1)
                dve.tensor_tensor(u[1][:, k, 0:cols], y[:, k, 0:cols], u[0][:, k, 0:cols], ALU.subtract)
            for k in range(KD):
                dve.scalar_tensor_tensor(y[:, k, 0:cols], h[:, k, :], vec[:, VEC[u_gain] + k:VEC[u_gain] + k + 1], acc[:, :],
                                         ALU.mult, ALU.mult).then_inc(u_made, 1)
                if k % 2 and k > 1:
                    low(k - 2)
            low(KD - 1)

        @block.scalar
        def _(act):
            act.wait_ge(sums, 1)
            inverse_root(act, [bank[j][:, 0:n] for j, (c, n) in enumerate(splits)], [rstd[:, c:c + n] for c, n in splits],
                         eps[:, 0:1], logs, rstd_made)
            for k in range(KD):
                act.wait_ge((h_even, h_odd)[k % 2], k // 2 + 1)
                act.wait_ge(sq_used, free(k))
                act.activation(sq[:, k % 2, :], h[:, k, :], ACT.Square).then_inc(sq_made, 1)
            act.wait_ge(sq_used, ready(KD - 1))
            inverse_root(act, [bank[ns + j][:, 0:n] for j, (c, n) in enumerate(splits)], [acc[:, c:c + n] for c, n in splits],
                         eps[:, 0:1], logs2, rstd2)
            for k in range(KD):
                act.wait_ge(u_made, k + 1)
                act.copy(u[0][:, k, 0:cols], y[:, k, 0:cols]).then_inc(u_hi, 1)

        @block.gpsimd
        def _(pool):
            for k in range(0, KD, 2):
                pool.wait_ge(scaled, k + 1)
                pool.tensor_tensor(h[:, k, :], h[:, k, :], y[:, k, 0:cols], ALU.add).then_inc(h_even, 1)
            for k in range(0, KD, 2):
                pool.wait_ge(u_hi, k + 1)
                pool.tensor_tensor(u[1][:, k, 0:cols], y[:, k, 0:cols], u[0][:, k, 0:cols], ALU.subtract)


def stage_ffn(nc, ctx, A, K, bank, u, inner_):
    wg_in, wu_in, hi_g, hi_u, lo_g, lo_u, gmm, umm, g_kept, conv1, conv2, conv3, gelu_made, inner_made = sems(
        ctx, nc, "f", "wg_in wu_in hi_g hi_u lo_g lo_u gmm umm g_kept conv1 conv2 conv3 gelu_made inner_made")
    w_in, hi_made, lo_made = (wg_in, wu_in), (hi_g, hi_u), (lo_g, lo_u)
    vec = K["vec"]
    sources = [A[n][0].rearrange("(k p) n -> p k n", p=P) for n in ("ffn_w_gate", "ffn_w_up")]
    cw, cb = VEC["conv_w"], VEC["conv_b"]
    with ExitStack() as inner:
        raw = buffer(inner, nc, "f_raw", [P, 2, KD, P])
        wh = buffer(inner, nc, "f_w_hi", [P, 2, KD, P], F32R)
        wl = buffer(inner, nc, "f_w_lo", [P, 2, KD, P], F32R)
        g = buffer(inner, nc, "f_gate", [P, LIVE])
        block = inner.enter_context(nc.Block())

        @block.sync
        def _(sp):
            with sp.Fori(0, KF) as n:
                for e in range(2):
                    sp.wait_ge(lo_made[e], n + 1)
                    sp.dma_start(raw[:, e, :, :], sources[e][:, :, ds(n * P, P)]).then_inc(w_in[e], 16)

        @block.gpsimd
        def _(pool):
            pool.sem_inc(lo_g, 1)
            pool.sem_inc(lo_u, 1)
            with pool.Fori(0, KF) as n:
                for e in range(2):
                    pool.wait_ge(hi_made[e], n + 1)
                    pool.tensor_tensor(wl[:, e, :, :], raw[:, e, :, :], wh[:, e, :, :], ALU.subtract).then_inc(lo_made[e], 1)

        @block.tensor
        def _(pe):
            pe.sem_inc(umm, 2)
            with pe.Fori(0, KF // 2) as i:
                for s in range(2):
                    n = 2 * i + s
                    pe.wait_ge(lo_g, n + 2)
                    pe.wait_ge(g_kept, n + 1)
                    for j, (c, w) in enumerate(LIVES):
                        m = product(pe, bank[j][:, 0:w], (wh[:, 0], wl[:, 0]), u, c, w)
                    m.then_inc(gmm, 1)
                    pe.wait_ge(lo_u, n + 2)
                    pe.wait_ge(inner_made, free(n))
                    for j, (c, w) in enumerate(SEQS):
                        m = product(pe, bank[3 + 2 * s + j][:, 0:w], (wh[:, 1], wl[:, 1]), u, TAPS - 1 + c, w)
                    m.then_inc(umm, 1)

        @block.scalar
        def _(act):
            act.sem_inc(g_kept, 1)

            def high(e, n):
                act.wait_ge(w_in[e], 16 * n + 16)
                act.copy(wh[:, e, :, :], raw[:, e, :, :]).then_inc(hi_made[e], 1)

            def step(n, more):
                act.wait_ge(gmm, n + 1)
                act.wait_ge(conv3, n + 1)
                for j, (c, w) in enumerate(LIVES):
                    a = act.copy(g[:, c:c + w], bank[j][:, 0:w])
                a.then_inc(g_kept, 1)
                if more:
                    high(0, n + 1)
                act.wait_ge(conv3, n + 2)
                tile = inner_[:, ds(n, 1), :]
                act.activation(tile, tile, ACT.Gelu_apprx_tanh).then_inc(gelu_made, 1)
                if more:
                    act.wait_ge(umm, ready(n))
                    high(1, n + 1)
            high(0, 0)
            high(1, 0)
            with act.Fori(0, KF - 1) as n:
                step(n, True)
            step(KF - 1, False)

        @block.vector
        def _(dve):
            dve.sem_inc(inner_made, 2)
            dve.sem_inc(conv3, 1)
            taps = vec[:, cw:cw + TAPS * KF].rearrange("p (j k) -> p j k", j=TAPS)
            with dve.Fori(0, KF // 2) as i:
                for s in range(2):
                    n = 2 * i + s
                    tile = inner_[:, ds(n, 1), :].rearrange("p a t -> p (a t)")
                    dve.wait_ge(g_kept, n + 2)
                    dve.tensor_scalar(tile, g[:, 0:SEQ], taps[:, 0, ds(n, 1)], vec[:, ds(n + cb, 1)], ALU.mult, ALU.add).then_inc(conv1, 1)
                    dve.wait_ge(conv1, n + 1)
                    dve.scalar_tensor_tensor(tile, g[:, 1:SEQ + 1], taps[:, 1, ds(n, 1)], tile, ALU.mult, ALU.add).then_inc(conv2, 1)
                    dve.wait_ge(conv2, n + 1)
                    dve.scalar_tensor_tensor(tile, g[:, 2:SEQ + 2], taps[:, 2, ds(n, 1)], tile, ALU.mult, ALU.add).then_inc(conv3, 1)
                    dve.wait_ge(gelu_made, n + 1)
                    dve.wait_ge(umm, ready(n))
                    for j, (c, w) in enumerate(SEQS):
                        part = inner_[:, ds(n, 1), c:c + w].rearrange("p a t -> p (a t)")
                        m = dve.tensor_tensor(part, part, bank[3 + 2 * s + j][:, 0:w], ALU.mult)
                    m.then_inc(inner_made, 1)


def stage_down(nc, ctx, A, K, bank, hidden, y, acc, h, h_load):
    w0, w1, hi_made, lo_made, used, mm, kept, squared, added, h_in = sems(
        ctx, nc, "d", "w0 w1 hi_made lo_made used mm kept squared added h_in")
    w_in = (w0, w1)
    w = A["ffn_w_down"][0]
    PAIRS_K = KF // 2
    with ExitStack() as inner:
        raw = buffer(inner, nc, "d_raw", [P, 2, D])
        wh = buffer(inner, nc, "d_w_hi", [P, 2, D], F32R)
        wl = buffer(inner, nc, "d_w_lo", [P, 2, D], F32R)
        xh = buffer(inner, nc, "d_x_hi", [P, 2, BANK], F32R)
        xl = buffer(inner, nc, "d_x_lo", [P, 2, BANK], F32R)
        sqs = buffer(inner, nc, "d_sq", [P, 4, BANK])
        block = inner.enter_context(nc.Block())

        @block.sync
        def _(sp):
            sp.dma_start(h[:, :, :], h_load).then_inc(h_in, 16)
            for half in range(2):
                with sp.Fori(0, PAIRS_K) as i:
                    for s in range(2):
                        sp.wait_ge(lo_made, free(KF * half + 2 * i + s))
                        sp.dma_start(raw[:, s, :], w[ds((2 * i + s) * P, P), :]).then_inc(w_in[s], 16)
            sp.wait_ge(h_in, 16)

        @block.tensor
        def _(pe):
            pe.sem_inc(used, 2)

            def step(half, k, s, first=False, last=False):
                pe.wait_ge(lo_made, ready(KF * half + k))
                for j in range(KD):
                    if first and half:
                        pe.wait_ge(kept, j + 1)
                    col = slice(j * P, (j + 1) * P)
                    pe.matmul(bank[j][:, :], wh[:, s, col], xh[:, s, :], start=first, stop=False)
                    pe.matmul(bank[j][:, :], wh[:, s, col], xl[:, s, :], start=False, stop=False)
                    m = pe.matmul(bank[j][:, :], wl[:, s, col], xh[:, s, :], start=False, stop=last)
                    if last:
                        m.then_inc(mm, 1)
                if last:
                    pe.wait_ge(mm, KD * (half + 1))
                    pe.sem_inc(used, 1)
                else:
                    m.then_inc(used, 1)
            for half in range(2):
                step(half, 0, 0, first=True)
                step(half, 1, 1)
                with pe.Fori(1, PAIRS_K - 1) as i:
                    for s in range(2):
                        step(half, 2 * i + s, s)
                step(half, KF - 2, 0)
                step(half, KF - 1, 1, last=True)

        @block.vector
        def _(dve):
            dve.sem_inc(lo_made, 2)

            def low(half, k, s):
                dve.wait_ge(hi_made, KF * half + k + 1)
                part = hidden[:, ds(k, 1), half * BANK:(half + 1) * BANK].rearrange("p a t -> p (a t)")
                dve.tensor_tensor(wl[:, s, :], raw[:, s, :], wh[:, s, :], ALU.subtract)
                dve.tensor_tensor(xl[:, s, :], part, xh[:, s, :], ALU.subtract).then_inc(lo_made, 1)

            def keep(half):
                for j in range(KD):
                    dve.wait_ge(mm, KD * half + j + 1)
                    dve.tensor_copy(y[:, j, half * BANK:(half + 1) * BANK], bank[j][:, :]).then_inc(kept, 1)
            with dve.Fori(0, PAIRS_K) as i:
                for s in range(2):
                    low(0, 2 * i + s, s)
            low(1, 0, 0)
            keep(0)
            low(1, 1, 1)
            with dve.Fori(1, PAIRS_K) as i:
                for s in range(2):
                    low(1, 2 * i + s, s)
            keep(1)

        @block.scalar
        def _(act):
            def high(half, k, s, n_in):
                act.wait_ge(w_in[s], 16 * n_in)
                act.wait_ge(used, free(KF * half + k))
                act.copy(wh[:, s, :], raw[:, s, :])
                part = hidden[:, ds(k, 1), half * BANK:(half + 1) * BANK].rearrange("p a t -> p (a t)")
                act.copy(xh[:, s, :], part).then_inc(hi_made, 1)

            def square(half):
                for j in range(KD):
                    n = KD * half + j
                    act.wait_ge(kept, n + 1)
                    if n >= 4:
                        act.wait_ge(added, n - 3)
                    act.activation(sqs[:, n % 4, :], y[:, j, half * BANK:(half + 1) * BANK], ACT.Square).then_inc(squared, 1)
            with act.Fori(0, PAIRS_K) as i:
                for s in range(2):
                    high(0, 2 * i + s, s, i + 1)
            high(1, 0, 0, PAIRS_K + 1)
            high(1, 1, 1, PAIRS_K + 1)
            square(0)
            with act.Fori(1, PAIRS_K) as i:
                for s in range(2):
                    high(1, 2 * i + s, s, i + PAIRS_K + 1)
            square(1)

        @block.gpsimd
        def _(pool):
            for half in range(2):
                part = acc[:, half * BANK:(half + 1) * BANK]
                for j in range(KD):
                    n = KD * half + j
                    pool.wait_ge(squared, n + 1)
                    if j == 0:
                        pool.tensor_copy(part, sqs[:, n % 4, :]).then_inc(added, 1)
                    else:
                        pool.wait_ge(added, n)
                        pool.tensor_tensor(part, part, sqs[:, n % 4, :], ALU.add).then_inc(added, 1)


AHEAD = 3


def stage_in2(nc, ctx, A, K, bank, u, qa, ka, va, qk, vm, og, gi, gf):
    (w0, w1, wg_in, hi_made, lo_made, gw_hi, gw_lo, mm, taken, conv_used, conv, vmm, vkept, gmm, cleared) = sems(
        ctx, nc, "i", "w0 w1 wg_in hi_made lo_made gw_hi gw_lo mm taken conv_used conv vmm vkept gmm cleared")
    w_in = (w0, w1)
    vec = K["vec"]
    w = A["w_in_2"][0].rearrange("(k p) n -> p k n", p=P)
    QT, CT, OT = 4, 8, 4
    VT, AT, KT = 16, 20, 21
    C0, V0, O0, G0 = 768, 1792, 2304, 2816
    cw, cb = VEC["conv_w2"], VEC["conv_b2"]
    with ExitStack() as inner:
        raw = buffer(inner, nc, "i_raw", [P, 2, KD, P])
        wh = buffer(inner, nc, "i_w_hi", [P, KD, 2, P], F32R)
        wl = buffer(inner, nc, "i_w_lo", [P, KD, 2, P], F32R)
        wg = buffer(inner, nc, "i_wg", [P, KD, 2 * ML_H])
        wgh = buffer(inner, nc, "i_wg_hi", [P, KD, 2 * ML_H], F32R)
        wgl = buffer(inner, nc, "i_wg_lo", [P, KD, 2 * ML_H], F32R)
        gb = buffer(inner, nc, "i_gate_bias", [ML_H, 2])
        g = buffer(inner, nc, "i_conv_in", [P, AHEAD + SEQ])
        block = inner.enter_context(nc.Block())

        def weights(s):
            return wh[:, :, s, :], wl[:, :, s, :]

        @block.sync
        def _(sp):
            def load(n, s, column):
                sp.wait_ge(lo_made, free(n))
                sp.dma_start(raw[:, s, :, :], w[:, :, column]).then_inc(w_in[s], 16)
            with sp.Fori(0, QT // 2) as i:
                for s in range(2):
                    sp.wait_ge(lo_made, free(2 * i + s))
                    for e in range(2):
                        sp.dma_start(raw[:, s, :, e * DH:(e + 1) * DH], w[:, :, ds((2 * i + s + QT * e) * DH, DH)]).then_inc(w_in[s], 16)
            with sp.Fori(0, CT // 2) as i:
                for s in range(2):
                    load(2 * i + s + QT, s, ds((2 * i + s) * P + C0, P))
            with sp.Fori(0, OT // 2) as i:
                for s in range(2):
                    load(2 * i + s + QT + CT, s, ds((2 * i + s) * P + O0, P))
            for t in range(4):
                load(VT + t, t % 2, slice(V0 + t * P, V0 + (t + 1) * P))
            load(AT, 0, slice(5 * P, 6 * P))
            load(KT, 1, slice(4 * P, 5 * P))
            sp.dma_start(wg[:, :, :], w[:, :, G0:G0 + 2 * ML_H]).then_inc(wg_in, 16)
            sp.dma_start(gb[:, :], A["b_gates_2"][0].rearrange("(t h) -> h t", h=ML_H), allow_slow_non_contiguous=True).then_inc(wg_in, 16)
            sp.wait_ge(wg_in, 32)

        @block.gpsimd
        def _(pool):
            pool.sem_inc(lo_made, 2)
            with pool.Fori(0, (KT + 1) // 2) as i:
                for s in range(2):
                    pool.wait_ge(hi_made, 2 * i + s + 1)
                    pool.tensor_tensor(wl[:, :, s, :], raw[:, s, :, :], wh[:, :, s, :], ALU.subtract).then_inc(lo_made, 1)
            pool.wait_ge(gw_hi, 1)
            pool.tensor_tensor(wgl[:, :, :], wg[:, :, :], wgh[:, :, :], ALU.subtract).then_inc(gw_lo, 1)

        @block.tensor
        def _(pe):
            pe.sem_inc(mm, 2)

            def tile(n, s):
                pe.wait_ge(lo_made, ready(n))
                pe.wait_ge(taken, free(n))
                for j, (c, m_) in enumerate(SEQS):
                    m = product(pe, bank[2 * s + j][:, 0:m_], weights(s), u, c, m_)
                m.then_inc(mm, 1)

            def values(c, slots):
                pe.wait_ge(vkept, free(values.n))
                out = bank[4 + values.n % 2][:, 0:slots * P]
                for t in range(KD):
                    xh, xl = (x[:, t, c * P:(c + 1) * P] for x in u)
                    pe.matmul(out, xh, wh[:, t, 0:slots, :], start=t == 0, stop=False)
                    pe.matmul(out, xh, wl[:, t, 0:slots, :], start=False, stop=False)
                    m = pe.matmul(out, xl, wh[:, t, 0:slots, :], start=False, stop=t == KD - 1)
                m.then_inc(vmm, 1)
                values.n += 1
            values.n = 0
            with pe.Fori(0, VT // 2) as i:
                for s in range(2):
                    tile(2 * i + s, s)
            for t in (VT, VT + 2, AT):
                slots = 1 if t == AT else 2
                pe.wait_ge(lo_made, ready(t + slots - 1))
                for c in range(NB):
                    values(c, slots)
                pe.wait_ge(vmm, values.n)
                for s in range(slots):
                    pe.sem_inc(mm, 1)
            pe.wait_ge(lo_made, ready(KT))
            for j, (c, n) in enumerate(SEQS):
                m = product(pe, bank[2 + j][:, 0:n], weights(1), u, c, n)
            m.then_inc(mm, 1)
            pe.wait_ge(gw_lo, 1)
            pe.wait_ge(taken, ready(VT))
            for e in range(2):
                for j, (c, n) in enumerate(SEQS):
                    gate = slice(e * ML_H, (e + 1) * ML_H)
                    m = product(pe, bank[2 * e + j][0:ML_H, 0:n], (wgh[:, :, gate], wgl[:, :, gate]), u, c, n)
            m.then_inc(gmm, 1)

        @block.scalar
        def _(act):
            act.sem_inc(taken, 2)

            def high(n, s, loaded):
                act.wait_ge(w_in[s], loaded)
                act.wait_ge(mm, free(n))
                act.copy(wh[:, :, s, :], raw[:, s, :, :]).then_inc(hi_made, 1)

            def keep_q(n, s):
                act.wait_ge(mm, ready(n))
                for j, (c, m_) in enumerate(SEQS):
                    a = act.copy(qa[:, ds(n, 1), c:c + m_], bank[2 * s + j][:, 0:m_])
                a.then_inc(taken, 1)

            def keep_conv(n, s):
                act.wait_ge(mm, ready(n + QT))
                act.wait_ge(conv_used, n + 1)
                for j, (c, m_) in enumerate(SEQS):
                    a = act.copy(g[:, AHEAD + c:AHEAD + c + m_], bank[2 * s + j][:, 0:m_])
                a.then_inc(taken, 1)

            def silu(n):
                act.wait_ge(conv_used, n + 2)
                act.activation(qk[:, ds(n, 1), :], qk[:, ds(n, 1), :], ACT.Silu)

            def keep_o(n, s):
                act.wait_ge(mm, ready(n + QT + CT))
                for j, (c, m_) in enumerate(SEQS):
                    a = act.activation(og[:, ds(n, 1), c:c + m_], bank[2 * s + j][:, 0:m_], ACT.Sigmoid)
                a.then_inc(taken, 1)
            high(0, 0, 32)
            high(1, 1, 32)
            for n in range(QT):
                keep_q(n, n % 2)
                high(n + 2, n % 2, 64 if n < 2 else 80)
            with act.Fori(0, CT // 2) as i:
                for s in range(2):
                    keep_conv(2 * i + s, s)
                    high(2 * i + s + QT + 2, s, 16 * i + 96)
                    silu(2 * i + s)
            for n in range(OT):
                t = QT + CT + n + 2
                keep_o(n, n % 2)
                high(t, t % 2, 64 + 16 * (t // 2 - 1))
            for t in range(VT + 2, KT + 1):
                high(t, t % 2, 64 + 16 * (t // 2 - 1))
            act.wait_ge(wg_in, 32)
            act.copy(wgh[:, :, :], wg[:, :, :]).then_inc(gw_hi, 1)
            act.wait_ge(mm, ready(KT))
            for j, (c, n) in enumerate(SEQS):
                a = act.copy(ka[:, P + c:P + c + n], bank[2 + j][:, 0:n])
            a.then_inc(taken, 1)
            act.wait_ge(gmm, 1)
            for j, (c, n) in enumerate(SEQS):
                act.activation(gi[:, c:c + n], bank[j][0:ML_H, 0:n], ACT.Identity, bias=gb[:, 0:1])
                act.activation(gf[:, c:c + n], bank[2 + j][0:ML_H, 0:n], ACT.Identity, bias=gb[:, 1:2])

        @block.vector
        def _(dve):
            dve.memset(g[:, 0:AHEAD], 0.0).then_inc(cleared, 1)
            dve.memset(ka[:, 0:P], 0.0)
            dve.memset(va[:, 0, :], 0.0)
            dve.sem_inc(conv_used, 1)
            dve.sem_inc(vkept, 2)
            taps = vec[:, cw:cw + 4 * CT].rearrange("p (j k) -> p j k", j=4)
            dve.wait_ge(cleared, 1)
            with dve.Fori(0, CT) as n:
                dve.wait_ge(taken, ready(n + QT))
                t0 = qk[:, ds(n, 1), :].rearrange("p a t -> p (a t)")
                dve.tensor_scalar(t0, g[:, 0:SEQ], taps[:, 0, ds(n, 1)], vec[:, ds(n + cb, 1)], ALU.mult, ALU.add).then_inc(conv, 1)
                for j in range(1, 4):
                    dve.wait_ge(conv, 3 * n + j)
                    m = dve.scalar_tensor_tensor(t0, g[:, j:SEQ + j], taps[:, j, ds(n, 1)], t0, ALU.mult, ALU.add)
                    m.then_inc(conv if j < 3 else conv_used, 1)
            n = 0
            for t in (0, 2 * P, 4 * P):
                for c in range(NB):
                    dve.wait_ge(vmm, n + 1)
                    out, width = (va[:, c + 1, :], P) if t == 4 * P else (vm[:, c, t:t + 2 * P], 2 * P)
                    dve.tensor_copy(out, bank[4 + n % 2][:, 0:width]).then_inc(vkept, 1)
                    n += 1


def stage_attention(nc, ctx, A, K, bank, qa, ka, va, out, spare):
    (sinks_in, made, staged, scored, logit, maxed, bias_made, exped, turned, pt_kept, pvmm, scaled, root, normed, back, back_kept, small, biased) = sems(
        ctx, nc, "a", "sinks_in made staged scored logit maxed bias_made exped turned pt_kept pvmm scaled root normed back back_kept small biased")
    ident, vec, eps = K["ident"], K["vec"], K["eps"]
    KEYS = 2 * WIN
    with ExitStack() as inner:
        sinks = buffer(inner, nc, "sinks", [P, QH])
        dist = buffer(inner, nc, "dist", [P, 2, KEYS])
        bias = spare.rearrange("p (f h k) -> p f h k", f=2, k=KEYS)
        qc = buffer(inner, nc, "q_block", [P, 2, 4, P])
        kc = buffer(inner, nc, "k_window", [P, 2, KEYS])
        lg = buffer(inner, nc, "logits", [P, 2, QH, KEYS])
        pt = buffer(inner, nc, "probs_t", [P, 2 * QH, P])
        mx = buffer(inner, nc, "row_max", [P, 2, 3, QH])
        den = buffer(inner, nc, "row_den", [P, 2, 2, QH])
        att = buffer(inner, nc, "att_rows", [P, QH * DH])
        att2 = buffer(inner, nc, "att_normed", [P, QH * DH])
        ss = buffer(inner, nc, "att_ss", [P, 4])
        block = inner.enter_context(nc.Block())

        @block.sync
        def _(sp):
            sp.dma_start(sinks[:, :], A["att_sinks_2"].to_broadcast([P, QH])).then_inc(sinks_in, 16)
            sp.wait_ge(sinks_in, 16)

        @block.gpsimd
        def _(pool):
            pool.iota(dist[:, 1, :], [[-1, KEYS]], base=WIN, channel_multiplier=1, allow_small_or_imprecise_dtypes=True).then_inc(made, 1)
            pool.wait_ge(made, 1)
            d = dist[:, 1, :]
            pool.affine_select(d, d, [[-1, KEYS]], ALU.is_ge, -NEG, base=WIN, channel_multiplier=1).then_inc(made, 1)
            pool.wait_ge(made, 2)
            pool.affine_select(d, d, [[1, KEYS]], ALU.is_gt, -NEG, base=0, channel_multiplier=-1).then_inc(made, 1)
            pool.wait_ge(made, 3)
            pool.affine_select(dist[:, 0, :], d, [[1, KEYS]], ALU.is_ge, -NEG, base=-WIN, channel_multiplier=0).then_inc(made, 1)

            def stage(n, s):
                pool.wait_ge(scored, free(n))
                pool.tensor_copy(qc[:, s, :, :], qa[:, :, ds(n * P, P)]).then_inc(staged, 1)
                pool.tensor_copy(kc[:, s, :], ka[:, ds(n * P, KEYS)]).then_inc(staged, 1)
            with pool.Fori(0, NB // 2) as i:
                for s in range(2):
                    stage(2 * i + s, s)

        @block.tensor
        def _(pe):
            pe.sem_inc(scored, 2)

            def scores(n, s):
                pe.wait_ge(staged, 2 * n + 2)
                pe.wait_ge(logit, 4 * n + 4)
                for e in range(2):
                    for j in range(4):
                        m = pe.matmul(bank[2 * e + j // 2][:, (j % 2) * KEYS:(j % 2 + 1) * KEYS], qc[e * DH:(e + 1) * DH, s, j, :],
                                      kc[e * DH:(e + 1) * DH, s, :], start=True, stop=True)
                m.then_inc(scored, 1)

            def output(n, s):
                for g in range(4):
                    pe.wait_ge(exped, 8 * n + 2 * g + 2)
                    pe.wait_ge(pt_kept, 4 * n + g + 1)
                    for r in range(4):
                        m = pe.transpose(bank[4 + g % 2][:, r * P:(r + 1) * P], lg[:, s, 2 * g + r // 2, (r % 2) * P:(r % 2 + 1) * P], ident[:, :])
                    m.then_inc(turned, 1)
                pe.wait_ge(pt_kept, 4 * n + 6)
                pe.wait_ge(scaled, n + 1)
                for h in range(QH):
                    kv = h // (QH // 2)
                    for r in range(2):
                        m = pe.matmul(bank[6][:, h * DH:(h + 1) * DH], pt[:, 2 * h + r, :],
                                      va[:, ds(n + r, 1), kv * DH:(kv + 1) * DH], start=r == 0, stop=r == 1)
                m.then_inc(pvmm, 1)

            def turn_back(n):
                pe.wait_ge(normed, n + 2)
                pe.wait_ge(back_kept, n + 1)
                for j in range(4):
                    m = pe.transpose(bank[7][:, j * P:(j + 1) * P], att2[:, j * P:(j + 1) * P], ident[:, :])
                m.then_inc(back, 1)
            scores(0, 0)
            scores(1, 1)
            output(0, 0)
            with pe.Fori(0, NB // 2 - 1) as i:
                for s in range(2):
                    scores(2 * i + s + 2, s)
                    output(2 * i + s + 1, 1 - s)
                    turn_back(2 * i + s)
            output(NB - 1, 1)
            turn_back(NB - 2)
            turn_back(NB - 1)

        @block.vector
        def _(dve):
            dve.sem_inc(logit, 4)
            dve.sem_inc(pt_kept, 2)
            dve.sem_inc(scaled, 1)
            dve.wait_ge(made, 4)
            for f in range(2):
                for h in range(QH):
                    slope = 2.0 ** (-8.0 * (h + 1) / QH)
                    dve.tensor_scalar(bias[:, f, h, :], dist[:, f, :], -slope, None, ALU.mult).then_inc(biased, 1)
            dve.wait_ge(biased, 2 * QH)
            dve.wait_ge(sinks_in, 16)

            def logits(n, s, first):
                dve.wait_ge(scored, ready(n))
                for b in range(4):
                    dve.scalar_tensor_tensor(lg[:, s, 2 * b:2 * b + 2, :], bank[b][:, :].rearrange("p (h t) -> p h t", h=2), DH ** -0.5,
                                             bias[:, 1 - first, 2 * b:2 * b + 2, :], ALU.mult, ALU.add).then_inc(logit, 1)
                dve.wait_ge(logit, 4 * n + 8)
                dve.tensor_reduce(mx[:, s, 0, :], lg[:, s, :, :], AX.X, ALU.max).then_inc(maxed, 1)
                dve.wait_ge(maxed, 3 * n + 1)
                dve.tensor_tensor(mx[:, s, 0, :], mx[:, s, 0, :], sinks[:, :], ALU.max).then_inc(maxed, 1)
                dve.wait_ge(maxed, 3 * n + 2)
                dve.tensor_scalar(mx[:, s, 1, :], mx[:, s, 0, :], -1.0, None, ALU.mult)
                dve.tensor_tensor(mx[:, s, 2, :], sinks[:, :], mx[:, s, 0, :], ALU.subtract).then_inc(maxed, 1)

            def output(n, s):
                for g in range(4):
                    dve.wait_ge(turned, 4 * n + g + 1)
                    dve.tensor_copy(pt[:, 4 * g:4 * g + 4, :], bank[4 + g % 2][:, :].rearrange("p (h t) -> p h t", h=4)).then_inc(pt_kept, 1)
                dve.wait_ge(exped, 8 * n + 8)
                dve.wait_ge(root, n + 1)
                dve.tensor_tensor(den[:, s, 0, :], den[:, s, 0, :], mx[:, s, 2, :], ALU.add).then_inc(small, 1)
                dve.wait_ge(small, 2 * n + 1)
                dve.reciprocal(den[:, s, 1, :], den[:, s, 0, :]).then_inc(small, 1)
                dve.wait_ge(small, 2 * n + 2)
                dve.wait_ge(pvmm, n + 1)
                dve.wait_ge(normed, n + 1)
                dve.tensor_tensor(att[:, :].rearrange("p (h d) -> p h d", d=DH), bank[6][:, :].rearrange("p (h d) -> p h d", d=DH),
                                  den[:, s, 1, :].unsqueeze(2).to_broadcast([P, QH, DH]), ALU.mult).then_inc(scaled, 1)
            logits(0, 0, 1)
            logits(1, 1, 0)
            output(0, 0)
            with dve.Fori(0, NB // 2 - 1) as i:
                for s in range(2):
                    logits(2 * i + s + 2, s, 0)
                    output(2 * i + s + 1, 1 - s)
            output(NB - 1, 1)

        @block.scalar
        def _(act):
            act.sem_inc(back_kept, 1)
            act.sem_inc(normed, 1)
            ga = VEC["norm_att"]

            def exponentials(n, s):
                act.wait_ge(maxed, 3 * n + 3)
                for h in range(QH):
                    act.activation(lg[:, s, h, :], lg[:, s, h, :], ACT.Exp, bias=mx[:, s, 1, h:h + 1], accum_out=den[:, s, 0, h:h + 1]).then_inc(exped, 1)
                act.activation(mx[:, s, 2, :], mx[:, s, 2, :], ACT.Exp).then_inc(root, 1)

            def norm(n):
                act.wait_ge(scaled, n + 2)
                act.activation(att2[:, :], att[:, :], ACT.Square, accum_out=ss[:, 0:1]).then_inc(bias_made, 1)
                act.wait_ge(bias_made, 3 * n + 1)
                act.activation(ss[:, 1:2], ss[:, 0:1], ACT.Ln, bias=eps[:, 0:1], scale=1.0 / (QH * DH)).then_inc(bias_made, 1)
                act.wait_ge(bias_made, 3 * n + 2)
                act.activation(ss[:, 2:3], ss[:, 1:2], ACT.Exp, scale=-0.5).then_inc(bias_made, 1)
                act.wait_ge(bias_made, 3 * n + 3)
                act.mul(att2[:, :], att[:, :], ss[:, 2:3]).then_inc(normed, 1)

            def output(n):
                act.wait_ge(back, n + 1)
                for j in range(4):
                    a = act.mul(out[:, j, ds(n * P, P)], bank[7][:, j * P:(j + 1) * P], vec[:, ga + j:ga + j + 1])
                a.then_inc(back_kept, 1)
            exponentials(0, 0)
            exponentials(1, 1)
            norm(0)
            with act.Fori(0, NB // 2 - 1) as i:
                for s in range(2):
                    exponentials(2 * i + s + 2, s)
                    output(2 * i + s)
                    norm(2 * i + s + 1)
            output(NB - 2)
            norm(NB - 1)
            output(NB - 1)


def stage_mlstm(nc, ctx, A, K, bank, qk, vm, og, gi, gf, out):
    (rows, act_rows, sel_made, aturned, a_kept, staged, fmm, used, rm_made, dec, gate_made, s_made, kt, kw_made, state, dmm, hmade, nbmm,
     floor, recip, sq_made, sums, logs, rstd, gated, fin, wexp, den_abs) = sems(
        ctx, nc, "m", "rows act_rows sel_made aturned a_kept staged fmm used rm_made dec gate_made s_made kt kw_made state dmm hmade nbmm "
        "floor recip sq_made sums logs rstd gated fin wexp den_abs")
    ident, ones, vec, eps, causal, reset = (K[n] for n in ("ident", "ones", "vec", "eps", "causal", "reset"))
    with ExitStack() as inner:
        ew, em, sc = (buffer(inner, nc, n, [P, 2, BANK]) for n in ("m_ew", "m_em", "m_s"))
        lf, m_, b = (t[0:ML_H, :, :].rearrange("p s n -> p (s n)") for t in (ew, em, sc))
        a = buffer(inner, nc, "m_a", [ML_H, SEQ])
        row3 = buffer(inner, nc, "m_rows", [ML_H, NB, 3, P])
        sel = buffer(inner, nc, "m_sel", [ML_H, ML_H, P])
        at = buffer(inner, nc, "m_a_tok", [P, NB, ML_H])
        kc = buffer(inner, nc, "m_k", [P, 2, BANK])
        vc = buffer(inner, nc, "m_v", [P, 2, BANK])
        rm = buffer(inner, nc, "m_r", [P, BANK])
        dd = buffer(inner, nc, "m_d", [P, BANK])
        qw = buffer(inner, nc, "m_qw", [P, 2, BANK])
        kw = buffer(inner, nc, "m_kw", [P, BANK])
        ws = buffer(inner, nc, "m_ws", [P, 2, ML_H])
        st = buffer(inner, nc, "m_c", [P, 2, BANK])
        nst = buffer(inner, nc, "m_n", [P, 2, BANK])
        den = buffer(inner, nc, "m_den", [P, BANK])
        sq, rs = (t[:, :, :].rearrange("p s n -> p (s n)") for t in (kc, vc))
        block = inner.enter_context(nc.Block())

        def heads(ap):
            return ap.rearrange("p (h t) -> p h t", t=P)

        @block.gpsimd
        def _(pool):
            pool.memset(sel[:, :, :], 1.0).then_inc(sel_made, 1)
            pool.wait_ge(sel_made, 1)
            pool.affine_select(sel[:, :, :], sel[:, :, :], [[-1, ML_H], [0, P]], ALU.is_equal, 0.0, base=0, channel_multiplier=1).then_inc(sel_made, 1)
            with pool.Fori(0, NB // 2) as i:
                for s in range(2):
                    c = 2 * i + s
                    pool.wait_ge(nbmm, free(c))
                    pool.tensor_copy(heads(kc[:, s, :]), qk[:, 4:8, ds(c * P, P)]).then_inc(staged, 1)
                    pool.tensor_copy(vc[:, s, :], vm[:, ds(c, 1), :].rearrange("p a n -> p (a n)")).then_inc(staged, 1)

        @block.vector
        def _(dve):
            n = 0

            def then(ins):
                nonlocal n
                n += 1
                ins.then_inc(rows, 1)
                dve.wait_ge(rows, n)
            dve.wait_ge(act_rows, 3)
            then(dve.scalar_tensor_tensor(lf[:, :], gf[:, :], 0.0, lf[:, :], ALU.min, ALU.subtract))
            then(dve.tensor_tensor_scan(m_[:, :], lf[:, :], gi[:, :], 0.0, ALU.add, ALU.max))
            for j in range(SEQ // BANK):
                c = slice(j * BANK, (j + 1) * BANK)
                then(dve.tensor_tensor_scan(b[:, c], reset[0:ML_H, :], lf[:, c], 0.0, ALU.mult, ALU.add))
            b3, m3 = (x[:, :].rearrange("p (c t) -> p c t", t=P) for x in (b, m_))
            then(dve.tensor_tensor(a[:, :], gi[:, :], b[:, :], ALU.subtract))
            then(dve.tensor_tensor(row3[:, :, 0, :], b3, m3, ALU.subtract))
            then(dve.tensor_copy(row3[:, 0, 1, :], row3[:, 0, 0, :]))
            then(dve.tensor_tensor(row3[:, 1:, 1, :], row3[:, 1:, 0, :], m3[:, 0:NB - 1, P - 1:P].to_broadcast([ML_H, NB - 1, P]), ALU.add))
            then(dve.tensor_scalar(row3[:, :, 2, :], m3, -1.0, None, ALU.mult))
            dve.memset(st[:, 0, :], 0.0)
            dve.memset(nst[:, 0, :], 0.0).then_inc(state, 1)
            dve.wait_ge(aturned, 1)
            dve.tensor_copy(at[:, :, :], bank[7][:, 0:NB * ML_H].rearrange("p (c h) -> p c h", h=ML_H)).then_inc(a_kept, 1)
            dve.wait_ge(a_kept, 1)

            def front(c, s):
                dve.wait_ge(fmm, c + 1)
                dve.tensor_tensor(heads(rm[:, :]), heads(bank[1][:, :]), causal[:, :].unsqueeze(1).to_broadcast([P, ML_H, P]), ALU.add)
                dve.tensor_tensor(ws[:, s, :], at[:, ds(c, 1), :].rearrange("p a h -> p (a h)"), heads(bank[1][:, :])[:, :, P - 1], ALU.add).then_inc(rm_made, 1)

            def middle(c, s):
                dve.wait_ge(dec, c + 1)
                dve.scalar_tensor_tensor(sc[:, s, :], dd[:, :], P ** -0.5, bank[0][:, :], ALU.mult, ALU.mult).then_inc(s_made, 1)
                dve.wait_ge(gate_made, c + 1)
                dve.scalar_tensor_tensor(heads(qw[:, s, :]), qk[:, 0:4, ds(c * P, P)], P ** -0.5, heads(ew[:, s, :]), ALU.mult, ALU.mult).then_inc(s_made, 1)

            def invert(c, s):
                dve.wait_ge(den_abs, c + 1)
                dve.tensor_tensor(den[:, :], den[:, :], em[:, s, :], ALU.max).then_inc(floor, 1)
                dve.wait_ge(floor, c + 1)
                dve.reciprocal(den[:, :], den[:, :]).then_inc(recip, 1)

            def back(c, s):
                dve.wait_ge(nbmm, ready(c))
                for h in range(ML_H):
                    col = slice(h * P, (h + 1) * P)
                    decay = ew[:, s, (h + 1) * P - 1:(h + 1) * P]
                    dve.scalar_tensor_tensor(st[:, 1 - s, col], st[:, s, col], decay, bank[7][:, col], ALU.mult, ALU.add)
                    x = dve.scalar_tensor_tensor(nst[:, 1 - s, col], nst[:, s, col], decay, bank[4][:, col], ALU.mult, ALU.add)
                x.then_inc(state, 1)
                dve.wait_ge(recip, c + 1)
                dve.tensor_tensor(out[:, 4:8, ds(c * P, P)], heads(bank[5][:, :]), heads(den[:, :]), ALU.mult).then_inc(hmade, 1)
            dve.sem_inc(hmade, 1)
            dve.sem_inc(s_made, 2)

            def chunk(c, s):
                invert(c, s)
                front(c + 1, 1 - s)
                back(c, s)
                middle(c + 1, 1 - s)
            front(0, 0)
            middle(0, 0)
            with dve.Fori(0, NB // 2 - 1) as i:
                for s in range(2):
                    chunk(2 * i + s, s)
            chunk(NB - 2, 0)
            invert(NB - 1, 1)
            back(NB - 1, 1)
            dve.wait_ge(hmade, NB + 1)
            for h in range(ML_H):
                dve.tensor_tensor(out[:, 4 + h, :], out[:, 4 + h, :], og[:, h, :], ALU.mult).then_inc(gated, 1)
            for h in range(ML_H):
                dve.wait_ge(rstd, 2 * h + 2)
                dve.scalar_tensor_tensor(out[:, 4 + h, :], out[:, 4 + h, :], vec[:, VEC["norm_ml"] + h:VEC["norm_ml"] + h + 1], rs[:, :],
                                         ALU.mult, ALU.mult).then_inc(fin, 1)

        @block.scalar
        def _(act):
            act.activation(lf[:, :], gf[:, :], ACT.Abs).then_inc(act_rows, 1)
            act.wait_ge(act_rows, 1)
            act.activation(lf[:, :], lf[:, :], ACT.Exp, scale=-1.0).then_inc(act_rows, 1)
            act.wait_ge(act_rows, 2)
            act.activation(lf[:, :], lf[:, :], ACT.Ln, bias=1.0).then_inc(act_rows, 1)

            def front(c, s):
                act.wait_ge(rm_made, c + 1)
                act.wait_ge(s_made, 2 * c + 1)
                for h in range(ML_H):
                    x = act.activation(dd[:, h * P:(h + 1) * P], rm[:, h * P:(h + 1) * P], ACT.Exp,
                                       bias=at[:, ds(c, 1), h:h + 1].rearrange("p a h -> p (a h)"))
                x.then_inc(dec, 1)
                act.activation(ws[:, s, :], ws[:, s, :], ACT.Exp).then_inc(wexp, 1)
                act.activation(ew[:, s, :], bank[2][:, :], ACT.Exp)
                act.activation(em[:, s, :], bank[3][:, :], ACT.Exp).then_inc(gate_made, 1)

            def back(c, s):
                act.wait_ge(kt, c + 1)
                act.wait_ge(wexp, c + 1)
                for h in range(ML_H):
                    x = act.mul(kw[:, h * P:(h + 1) * P], bank[4][:, h * P:(h + 1) * P], ws[:, s, h:h + 1])
                x.then_inc(kw_made, 1)
                act.wait_ge(dmm, c + 1)
                act.activation(den[:, :], bank[6][:, :], ACT.Abs).then_inc(den_abs, 1)
            front(0, 0)
            with act.Fori(0, NB // 2 - 1) as i:
                for s in range(2):
                    back(2 * i + s, s)
                    front(2 * i + s + 1, 1 - s)
            back(NB - 2, 0)
            front(NB - 1, 1)
            back(NB - 1, 1)
            for h in range(ML_H):
                act.wait_ge(gated, h + 1)
                if h:
                    act.wait_ge(sums, h)
                act.activation(sq[:, :], out[:, 4 + h, :], ACT.Square).then_inc(sq_made, 1)
                act.wait_ge(sums, h + 1)
                if h:
                    act.wait_ge(fin, h)
                inverse_root(act, [bank[j][:, :] for j in range(2)], [rs[:, c:c + n] for c, n in SEQS], eps[:, 0:1], logs, rstd, at=2 * h, width=P)

        @block.tensor
        def _(pe):
            pe.sem_inc(nbmm, 2)
            pe.wait_ge(rows, 9)
            for c in range(NB):
                m = pe.transpose(bank[7][:, c * ML_H:(c + 1) * ML_H], a[:, c * P:(c + 1) * P], ident[0:ML_H, 0:ML_H])
            m.then_inc(aturned, 1)
            pe.wait_ge(sel_made, 2)
            pe.wait_ge(a_kept, 1)

            def front(c, s):
                pe.wait_ge(staged, 2 * c + 2)
                pe.wait_ge(s_made, 2 * c + 2)
                for h in range(ML_H):
                    col = slice(h * P, (h + 1) * P)
                    pe.matmul(bank[0][:, col], kc[:, s, col], qk[:, h, ds(c * P, P)], start=True, stop=True)
                for r in range(3):
                    for h in range(ML_H):
                        m = pe.matmul(bank[1 + r][:, h * P:(h + 1) * P], sel[:, h, :], row3[:, ds(c, 1), r, :], start=True, stop=True)
                m.then_inc(fmm, 1)

            def turn(c, s):
                pe.wait_ge(state, c + 1)
                for h in range(ML_H):
                    m = pe.transpose(bank[4][:, h * P:(h + 1) * P], kc[:, s, h * P:(h + 1) * P], ident[:, :])
                m.then_inc(kt, 1)

            def back(c, s):
                pe.wait_ge(hmade, c + 1)
                pe.wait_ge(s_made, 2 * c + 4)
                for h in range(ML_H):
                    col = slice(h * P, (h + 1) * P)
                    pe.matmul(bank[6][:, col], ones[:, :], sc[:, s, col], start=True, stop=False)
                    m = pe.matmul(bank[6][:, col], nst[:, s, col], qw[:, s, col], start=False, stop=True)
                for h in range(ML_H):
                    col = slice(h * P, (h + 1) * P)
                    pe.matmul(bank[5][:, col], vc[:, s, col], sc[:, s, col], start=True, stop=False)
                    m = pe.matmul(bank[5][:, col], st[:, s, col], qw[:, s, col], start=False, stop=True)
                m.then_inc(dmm, 1)

            def update(c, s):
                pe.wait_ge(kw_made, c + 1)
                for h in range(ML_H):
                    col = slice(h * P, (h + 1) * P)
                    pe.matmul(bank[7][:, col], kw[:, col], vc[:, s, col], start=True, stop=True)
                for h in range(ML_H):
                    m = pe.matmul(bank[4][:, h * P:(h + 1) * P], kw[:, h * P:(h + 1) * P], ones[:, :], start=True, stop=True)
                m.then_inc(nbmm, 1)

            def chunk(c, s):
                turn(c, s)
                back(c, s)
                front(c + 1, 1 - s)
                update(c, s)
            front(0, 0)
            with pe.Fori(0, NB // 2 - 1) as i:
                for s in range(2):
                    chunk(2 * i + s, s)
            chunk(NB - 2, 0)
            turn(NB - 1, 1)
            back(NB - 1, 1)
            update(NB - 1, 1)
            for h in range(ML_H):
                pe.wait_ge(sq_made, h + 1)
                if h:
                    pe.wait_ge(rstd, 2 * h)
                for j, (c, n) in enumerate(SEQS):
                    m = pe.matmul(bank[j][:, 0:n], ones[:, :], sq[:, c:c + n], start=True, stop=True)
                m.then_inc(sums, 1)


def stage_residual(nc, ctx, A, K, bank, name, weights, tiles_in, x, h, u=None, u_gain=None, h_load=None):
    mm, made, squared, added, sums, logs, rstd_made, h_in, x_hi, x_lo = sems(
        ctx, nc, name, "mm made squared added sums logs rstd_made h_in x_hi x_lo")
    ones, vec, eps = K["ones"], K["vec"], K["eps"]
    w = weights.rearrange("(k p) n -> p k n", p=P)
    with ExitStack() as inner:
        wt = Weights(ctx, inner, nc, name, tiles_in, mm)
        xh, xl = (buffer(inner, nc, name + n, [P, tiles_in, SEQ], F32R) for n in ("_x_hi", "_x_lo"))
        sq = buffer(inner, nc, name + "_sq", [P, 2, SEQ])
        acc = buffer(inner, nc, name + "_acc", [P, SEQ])
        block = inner.enter_context(nc.Block())

        @block.sync
        def _(sp):
            if h_load is not None:
                sp.dma_start(h[:, :, :], h_load).then_inc(h_in, 16)
            with sp.Fori(0, KD // 2) as i:
                for s in range(2):
                    wt.load(sp, 2 * i + s, s, w[:, :, ds((2 * i + s) * P, P)])

        @block.tensor
        def _(pe):
            pe.sem_inc(mm, 2)

            def tile(n, s, split=None):
                pe.wait_ge(wt.lo_made, ready(n))
                pe.wait_ge(made, free(n))
                for j, (c, w_) in enumerate(SEQS):
                    m = product(pe, bank[2 * s + j][:, 0:w_], wt.pair(s), (xh, xl), c, w_, split)
                m.then_inc(mm, 1)
            tile(0, 0, x_lo)
            tile(1, 1)
            with pe.Fori(1, KD // 2) as i:
                for s in range(2):
                    tile(2 * i + s, s)
            if u is not None:
                pe.wait_ge(added, ready(KD - 1))
                for j, (c, n) in enumerate(SEQS):
                    m = pe.matmul(bank[4 + j][:, 0:n], ones[:, :], acc[:, c:c + n], start=True, stop=True)
                m.then_inc(sums, 1)

        @block.vector
        def _(dve):
            dve.sem_inc(made, 2)
            split_low(dve, x, xh, xl, x_hi, x_lo)
            if h_load is not None:
                dve.wait_ge(h_in, 16)
            with dve.Fori(0, KD // 2) as i:
                for s in range(2):
                    dve.wait_ge(mm, ready(2 * i + s))
                    for j, (c, n) in enumerate(SEQS):
                        hc = h[:, ds(2 * i + s, 1), c:c + n].rearrange("p a t -> p (a t)")
                        m = dve.tensor_tensor(hc, hc, bank[2 * s + j][:, 0:n], ALU.add)
                    m.then_inc(made, 1)
            if u is not None:
                dve.wait_ge(rstd_made, 2)
                dve.wait_ge(made, ready(KD - 1))
                for k in range(KD):
                    dve.scalar_tensor_tensor(u[:, k, 0:SEQ], h[:, k, :], vec[:, VEC[u_gain] + k:VEC[u_gain] + k + 1], sq[:, 0, :],
                                             ALU.mult, ALU.mult)

        @block.scalar
        def _(act):
            act.sem_inc(squared, 2)

            def square(n, s):
                if u is not None:
                    act.wait_ge(made, ready(n))
                    act.wait_ge(added, free(n))
                    act.activation(sq[:, s, :], h[:, ds(n, 1), :], ACT.Square).then_inc(squared, 1)
            split_high(act, x, xh, x_hi, 0, 2)
            wt.high(act, 0, 0, 0)
            split_high(act, x, xh, x_hi, 2)
            wt.high(act, 1, 1, 0)
            with act.Fori(0, KD // 2 - 1) as i:
                for s in range(2):
                    wt.high(act, 2 * i + s + 2, s, i + 1)
                    square(2 * i + s, s)
            square(KD - 2, 0)
            square(KD - 1, 1)
            if u is not None:
                act.wait_ge(sums, 1)
                inverse_root(act, [bank[4 + j][:, 0:n] for j, (c, n) in enumerate(SEQS)], [sq[:, 0, c:c + n] for c, n in SEQS],
                             eps[:, 0:1], logs, rstd_made)

        @block.gpsimd
        def _(pool):
            pool.sem_inc(added, 2)
            pool.sem_inc(wt.lo_made, 2)
            wt.low(pool, 0, 0)
            wt.low(pool, 1, 1)
            for n in range(KD):
                if n + 2 < KD:
                    wt.low(pool, n + 2, n % 2)
                if u is None:
                    continue
                pool.wait_ge(squared, ready(n))
                if n == 0:
                    pool.tensor_copy(acc[:, :], sq[:, 0, :]).then_inc(added, 1)
                else:
                    pool.wait_ge(added, ready(n - 1))
                    pool.tensor_tensor(acc[:, :], acc[:, :], sq[:, n % 2, :], ALU.add).then_inc(added, 1)


def stage_memory(nc, ctx, A, K, bank, mk, mv):
    m_in, wk0, wv_in, squared, normed, turned, kept, kmm, vmm = sems(
        ctx, nc, "e", "m_in wk0 wv_in squared normed turned kept kmm vmm")
    ident, vec, eps = K["ident"], K["vec"], K["eps"]
    w = A["w_ckv_2"][0].rearrange("(k p) n -> p k n", p=P)
    MB = MEM // P
    gm = VEC["norm_mem"]
    with ExitStack() as inner:
        rows = buffer(inner, nc, "e_rows", [P, MB, D])
        sq = buffer(inner, nc, "e_sq", [P, MB, D])
        ss = buffer(inner, nc, "e_ss", [P, MB, 3])
        mt = buffer(inner, nc, "e_mem", [P, KD, MEM])
        wk = buffer(inner, nc, "e_wk", [P, KD, 4 * P])
        wv = buffer(inner, nc, "e_wv", [P, KD, 4 * P])
        block = inner.enter_context(nc.Block())

        @block.sync
        def _(sp):
            sp.dma_start(rows[:, :, :], A["mem_2"][0].rearrange("(b p) d -> p b d", p=P)).then_inc(m_in, 16)
            sp.dma_start(wk[:, :, :], w[:, :, 0:4 * P]).then_inc(wk0, 16)
            sp.dma_start(wv[:, :, :], w[:, :, 4 * P:8 * P]).then_inc(wv_in, 16)

        @block.scalar
        def _(act):
            act.wait_ge(m_in, 16)
            for b in range(MB):
                act.activation(sq[:, b, :], rows[:, b, :], ACT.Square, accum_out=ss[:, b, 0:1]).then_inc(squared, 1)
            act.wait_ge(squared, MB)
            act.activation(ss[:, :, 1], ss[:, :, 0], ACT.Ln, bias=eps[:, 0:1], scale=1.0 / D).then_inc(squared, 1)
            act.wait_ge(squared, MB + 1)
            act.activation(ss[:, :, 2], ss[:, :, 1], ACT.Exp, scale=-0.5).then_inc(squared, 1)
            act.wait_ge(squared, MB + 2)
            for b in range(MB):
                act.mul(rows[:, b, :], rows[:, b, :], ss[:, b, 2:3]).then_inc(normed, 1)

        @block.tensor
        def _(pe):
            pe.wait_ge(normed, MB)
            for k in range(KD):
                if k >= 4:
                    pe.wait_ge(kept, k - 3)
                for b in range(MB):
                    m = pe.transpose(bank[k % 4][:, b * P:(b + 1) * P], rows[:, b, k * P:(k + 1) * P], ident[:, :])
                m.then_inc(turned, 1)
            pe.wait_ge(kept, KD)
            pe.wait_ge(wk0, 16)
            for h in range(4):
                for t in range(KD):
                    m = pe.matmul(bank[4 + h][:, 0:MEM], wk[:, t, h * P:(h + 1) * P], mt[:, t, :], start=t == 0, stop=t == KD - 1)
                m.then_inc(kmm, 1)
            pe.wait_ge(wv_in, 16)
            for b in range(MB):
                for t in range(KD):
                    m = pe.matmul(bank[b][:, :], mt[:, t, b * P:(b + 1) * P], wv[:, t, :], start=t == 0, stop=t == KD - 1)
                m.then_inc(vmm, 1)

        @block.vector
        def _(dve):
            for k in range(KD):
                dve.wait_ge(turned, k + 1)
                dve.tensor_scalar(mt[:, k, :], bank[k % 4][:, 0:MEM], vec[:, gm + k:gm + k + 1], None, ALU.mult).then_inc(kept, 1)
            for h in range(4):
                dve.wait_ge(kmm, h + 1)
                dve.tensor_copy(mk[:, h, :], bank[4 + h][:, 0:MEM])
            for b in range(MB):
                dve.wait_ge(vmm, b + 1)
                dve.tensor_copy(mv[:, b, :], bank[b][:, :])


XH = 4


def stage_cross_q(nc, ctx, A, K, bank, u, q):
    mm, kept, x_hi, x_lo = sems(ctx, nc, "xq", "mm kept x_hi x_lo")
    w = A["w_cq_2"][0].rearrange("(k p) n -> p k n", p=P)
    with ExitStack() as inner:
        wt = Weights(ctx, inner, nc, "xq", KD, mm)
        uh, ul = (buffer(inner, nc, n, [P, KD, SEQ], F32R) for n in ("xq_u_hi", "xq_u_lo"))
        block = inner.enter_context(nc.Block())

        @block.sync
        def _(sp):
            for n in range(XH):
                wt.load(sp, n, n % 2, w[:, :, n * P:(n + 1) * P])

        @block.gpsimd
        def _(pool):
            pool.sem_inc(wt.lo_made, 2)
            for n in range(XH):
                wt.low(pool, n, n % 2)

        @block.tensor
        def _(pe):
            pe.sem_inc(mm, 2)
            for n in range(XH):
                pe.wait_ge(wt.lo_made, ready(n))
                pe.wait_ge(kept, free(n))
                for j, (c, w_) in enumerate(SEQS):
                    m = product(pe, bank[2 * (n % 2) + j][:, 0:w_], wt.pair(n % 2), (uh, ul), c, w_, x_lo if n == 0 else None)
                m.then_inc(mm, 1)

        @block.vector
        def _(dve):
            split_low(dve, u, uh, ul, x_hi, x_lo)

        @block.scalar
        def _(act):
            act.sem_inc(kept, 2)
            split_high(act, u, uh, x_hi, 0, 2)
            wt.high(act, 0, 0, 0)
            split_high(act, u, uh, x_hi, 2)
            wt.high(act, 1, 1, 0)
            for t in range(XH):
                if t + 2 < XH:
                    wt.high(act, t + 2, t % 2, t // 2 + 1)
                act.wait_ge(mm, ready(t))
                for j, (c, n) in enumerate(SEQS):
                    a = act.copy(q[:, t, c:c + n], bank[2 * (t % 2) + j][:, 0:n])
                a.then_inc(kept, 1)


def stage_cross(nc, ctx, A, K, bank, q, mk, mv, out):
    (staged, scored, maxed, negmax, exped, inverted, probs, turned, pt_kept, omm, o_kept) = sems(
        ctx, nc, "x", "staged scored maxed negmax exped inverted probs turned pt_kept omm o_kept")
    ident = K["ident"]
    SC = P ** -0.5
    with ExitStack() as inner:
        qc = buffer(inner, nc, "x_q_block", [P, 2, XH, P])
        pr = buffer(inner, nc, "x_probs", [P, 2, XH, MEM])
        pt = buffer(inner, nc, "x_probs_t", [P, 2 * XH, P])
        mx = buffer(inner, nc, "x_max", [P, 2, XH])
        den = buffer(inner, nc, "x_den", [P, 2, 2, XH])
        block = inner.enter_context(nc.Block())

        @block.gpsimd
        def _(pool):
            with pool.Fori(0, NB // 2) as i:
                for s in range(2):
                    n = 2 * i + s
                    pool.wait_ge(scored, free(n))
                    pool.tensor_copy(qc[:, s, :, :], q[:, :, ds(n * P, P)]).then_inc(staged, 1)

        @block.tensor
        def _(pe):
            pe.sem_inc(scored, 2)

            def scores(n, s):
                pe.wait_ge(staged, n + 1)
                pe.wait_ge(exped, 4 * n + 4)
                for h in range(XH):
                    m = pe.matmul(bank[2 * s + h // 2][:, (h % 2) * MEM:(h % 2 + 1) * MEM], qc[:, s, h, :], mk[:, h, :], start=True, stop=True)
                m.then_inc(scored, 1)

            def output(n, s):
                pe.wait_ge(probs, n + 1)
                for g in range(2):
                    pe.wait_ge(pt_kept, 2 * n + g + 1)
                    for r in range(4):
                        m = pe.transpose(bank[4 + g][:, r * P:(r + 1) * P], pr[:, s, 2 * g + r // 2, (r % 2) * P:(r % 2 + 1) * P], ident[:, :])
                    m.then_inc(turned, 1)
                pe.wait_ge(pt_kept, 2 * n + 4)
                pe.wait_ge(o_kept, n + 1)
                for h in range(XH):
                    for r in range(2):
                        m = pe.matmul(bank[6][:, h * P:(h + 1) * P], mv[:, r, h * P:(h + 1) * P], pt[:, 2 * h + r, :], start=r == 0, stop=r == 1)
                m.then_inc(omm, 1)
            scores(0, 0)
            with pe.Fori(0, NB // 2 - 1) as i:
                for s in range(2):
                    scores(2 * i + s + 1, 1 - s)
                    output(2 * i + s, s)
            scores(NB - 1, 1)
            output(NB - 2, 0)
            output(NB - 1, 1)

        @block.vector
        def _(dve):
            dve.sem_inc(pt_kept, 2)

            def maxima(n, s):
                dve.wait_ge(scored, ready(n))
                for j in range(2):
                    m = dve.tensor_reduce(mx[:, s, 2 * j:2 * j + 2], bank[2 * s + j][:, :].rearrange("p (h t) -> p h t", h=2), AX.X, ALU.max)
                m.then_inc(maxed, 1)
                dve.wait_ge(maxed, n + 1)
                dve.tensor_scalar(mx[:, s, :], mx[:, s, :], -SC, None, ALU.mult).then_inc(negmax, 1)

            def output(n, s):
                dve.wait_ge(exped, 4 * n + 12)
                dve.reciprocal(den[:, s, 1, :], den[:, s, 0, :]).then_inc(inverted, 1)
                dve.wait_ge(inverted, n + 1)
                dve.tensor_tensor(pr[:, s, :, :], pr[:, s, :, :], den[:, s, 1, :].unsqueeze(2).to_broadcast([P, XH, MEM]), ALU.mult).then_inc(probs, 1)
                for g in range(2):
                    dve.wait_ge(turned, 2 * n + g + 1)
                    dve.tensor_copy(pt[:, 4 * g:4 * g + 4, :], bank[4 + g][:, :].rearrange("p (h t) -> p h t", h=4)).then_inc(pt_kept, 1)
            maxima(0, 0)
            with dve.Fori(0, NB // 2 - 1) as i:
                for s in range(2):
                    maxima(2 * i + s + 1, 1 - s)
                    output(2 * i + s, s)
            maxima(NB - 1, 1)
            output(NB - 2, 0)
            output(NB - 1, 1)

        @block.scalar
        def _(act):
            act.sem_inc(o_kept, 1)
            act.sem_inc(exped, 8)

            def exponentials(n, s):
                act.wait_ge(negmax, n + 1)
                for h in range(XH):
                    act.activation(pr[:, s, h, :], bank[2 * s + h // 2][:, (h % 2) * MEM:(h % 2 + 1) * MEM], ACT.Exp, scale=SC,
                                   bias=mx[:, s, h:h + 1], accum_out=den[:, s, 0, h:h + 1]).then_inc(exped, 1)

            def output(n):
                act.wait_ge(omm, n + 1)
                act.copy(out[:, :, ds(n * P, P)], bank[6][:, :].rearrange("p (h t) -> p h t", h=XH)).then_inc(o_kept, 1)
            exponentials(0, 0)
            with act.Fori(0, NB // 2 - 1) as i:
                for s in range(2):
                    exponentials(2 * i + s + 1, 1 - s)
                    output(2 * i + s)
            exponentials(NB - 1, 1)
            output(NB - 2)
            output(NB - 1)


def stage_route(nc, ctx, A, K, bank, h, xt, gates, assigned, token, table, xn_d, list_d):
    (w_in, staged, turned, x_kept, lmm, squared, rstd_made, xn_made, stored_a, stored_b, gw, rmm, cnt, iotas, zeroed, zero_stored, scattered, rows, act_rows, slots_made,
     list_in, list_float, list_turned) = sems(
        ctx, nc, "r", "w_in staged turned x_kept lmm squared rstd_made xn_made stored_a stored_b gw rmm cnt iotas zeroed zero_stored scattered rows act_rows slots_made "
        "list_in list_float list_turned")
    ident, ones, vec, eps, lower = (K[n] for n in ("ident", "ones", "vec", "eps", "lower"))
    stored = (stored_a, stored_b)
    BIG = 64.0
    gn = VEC["norm_ffn2"]
    with ExitStack() as inner:
        hs = buffer(inner, nc, "r_block", [P, 2, KD, P])
        wr = buffer(inner, nc, "r_w", [P, KD, ROUTER])
        br = buffer(inner, nc, "r_bias", [P, ROUTER])
        gain = buffer(inner, nc, "r_gain", [P, D])
        sq = buffer(inner, nc, "r_sq", [P, D])
        xn = buffer(inner, nc, "r_xn", [P, 2, D])
        ss = buffer(inner, nc, "r_ss", [P, 3, NB])
        lg = buffer(inner, nc, "r_logits", [P, NB, ROUTER])
        em = buffer(inner, nc, "r_em", [P, NB, NE])
        em2 = buffer(inner, nc, "r_em2", [P, NB, NE])
        tt = buffer(inner, nc, "r_tmp", [P, NB, NE])
        oh1 = buffer(inner, nc, "r_first", [P, NB, NE])
        oh2 = buffer(inner, nc, "r_second", [P, NB, NE])
        both = buffer(inner, nc, "r_both", [P, NB + 1, NE])
        before = buffer(inner, nc, "r_before", [P, NB, NE])
        rank = buffer(inner, nc, "r_rank", [P, NB, NE])
        g4 = buffer(inner, nc, "r_g4", [P, NB, NG])
        g4b = buffer(inner, nc, "r_g4b", [P, NB, NG])
        sm = buffer(inner, nc, "r_small", [P, 10, NB])
        iota = buffer(inner, nc, "r_iota", [P, NE])
        stepf = buffer(inner, nc, "r_steps", [P, MAXB])
        own = buffer(inner, nc, "r_assignments", [P, 2 * NB], I32)
        empty = buffer(inner, nc, "r_empty", [MAXB, P], I32)
        slots = buffer(inner, nc, "r_slot", [P, 2 * NB], I32)
        lists = buffer(inner, nc, "r_list", [MAXB, P], I32)
        listf = buffer(inner, nc, "r_list_float", [MAXB, P])
        ex = buffer(inner, nc, "r_experts", [P, 5, NE])
        big = buffer(inner, nc, "r_big", [P, MAXB, NE])
        tf = buffer(inner, nc, "r_table", [1, 64])
        sf = buffer(inner, nc, "r_slots", [P, 2, NB])
        block = inner.enter_context(nc.Block())

        @block.sync
        def _(sp):
            sp.dma_start(wr[:, :, 0:NG], A["w_router_group_2"][0].rearrange("(k p) n -> p k n", p=P)).then_inc(w_in, 16)
            sp.dma_start(wr[:, :, NG:ROUTER], A["w_router_expert_2"][0].rearrange("(k p) n -> p k n", p=P)).then_inc(w_in, 16)
            sp.dma_start(br[:, 0:NG], A["b_router_group_2"].to_broadcast([P, NG])).then_inc(w_in, 16)
            sp.dma_start(br[:, NG:ROUTER], A["b_router_expert_2"].to_broadcast([P, NE])).then_inc(w_in, 16)
            sp.dma_start(gain[:, :], A["norm_ffn_2"].to_broadcast([P, D])).then_inc(w_in, 16)
            sp.wait_ge(zeroed, 1)
            sp.dma_start(list_d.rearrange("(b p) o -> b (p o)", p=P), empty[:, :]).then_inc(zero_stored, 16)
            with sp.Fori(0, NB // 2) as i:
                for s in range(2):
                    n = 2 * i + s
                    sp.wait_ge(xn_made, n + 1)
                    sp.dma_start(xn_d[ds(n * P, P), :], xn[:, s, :]).then_inc(stored[s], 16)
            sp.wait_ge(stored[0], 8 * NB)
            sp.wait_ge(stored[1], 8 * NB)
            sp.wait_ge(scattered, 32 * NB)
            sp.dma_start(lists[:, :], list_d.rearrange("(b p) o -> b (p o)", p=P)).then_inc(list_in, 16)

        @block.gpsimd
        def _(pool):
            pool.iota(empty[:, :], [[1, P]], base=2 * SEQ, channel_multiplier=0).then_inc(zeroed, 1)
            pool.iota(iota[:, :], [[1, NE]], base=0, channel_multiplier=0, allow_small_or_imprecise_dtypes=True).then_inc(iotas, 1)
            pool.iota(stepf[:, :], [[1, MAXB]], base=0, channel_multiplier=0, allow_small_or_imprecise_dtypes=True).then_inc(iotas, 1)
            pool.iota(own[:, :], [[P, 2 * NB]], base=0, channel_multiplier=1).then_inc(iotas, 1)
            with pool.Fori(0, NB // 2) as i:
                for s in range(2):
                    pool.wait_ge(lmm, free(2 * i + s))
                    pool.tensor_copy(hs[:, s, :, :], h[:, :, ds((2 * i + s) * P, P)]).then_inc(staged, 1)
            pool.wait_ge(slots_made, 1)
            pool.wait_ge(zero_stored, 16)
            pool.wait_ge(iotas, 3)
            for j in range(2):
                for b in range(NB):
                    pool.indirect_dma_start(out=list_d, out_offset=bass.IndirectOffsetOnAxis(ap=slots[:, j * NB + b:j * NB + b + 1], axis=0),
                                            in_=own[:, j * NB + b:j * NB + b + 1], in_offset=None).then_inc(scattered, 16)
            pool.wait_ge(scattered, 32 * NB)

        @block.tensor
        def _(pe):
            pe.sem_inc(lmm, 2)
            pe.wait_ge(gw, KD)
            with pe.Fori(0, NB // 2) as i:
                for s in range(2):
                    n = 2 * i + s
                    pe.wait_ge(staged, n + 1)
                    pe.wait_ge(x_kept, free(n))
                    for k in range(KD):
                        m = pe.transpose(bank[2 * s + k // 4][:, (k % 4) * P:(k % 4 + 1) * P], hs[:, s, k, :], ident[:, :])
                    m.then_inc(turned, 1)
                    for k in range(KD):
                        m = pe.matmul(bank[4][:, ds(n * ROUTER, ROUTER)], hs[:, s, k, :], wr[:, k, :], start=k == 0, stop=k == KD - 1)
                    m.then_inc(lmm, 1)
            pe.wait_ge(rmm, 1)
            pe.matmul(bank[5][:, 0:NB * NE], lower[:, :], both[:, 0:NB, :], start=True, stop=False)
            pe.matmul(bank[5][:, 0:NB * NE], ones[:, :], before[:, :, :], start=False, stop=True).then_inc(cnt, 1)
            pe.matmul(bank[6][:, 0:NE], ones[:, :], both[:, NB, :], start=True, stop=True).then_inc(cnt, 1)
            pe.wait_ge(list_float, 1)
            pe.transpose(bank[7][:, 0:MAXB], listf[:, :], ident[0:MAXB, 0:MAXB]).then_inc(list_turned, 1)

        @block.scalar
        def _(act):
            act.sem_inc(x_kept, 2)
            with act.Fori(0, NB // 2) as i:
                for s in range(2):
                    n = 2 * i + s
                    act.wait_ge(turned, n + 1)
                    act.copy(xt[:, ds(n, 1), 0:BANK], bank[2 * s][:, :])
                    act.copy(xt[:, ds(n, 1), BANK:D], bank[2 * s + 1][:, :]).then_inc(x_kept, 1)
                    act.wait_ge(x_kept, ready(n))
                    act.wait_ge(squared, n + 1)
                    act.activation(sq[:, :], xt[:, ds(n, 1), :].rearrange("p a d -> p (a d)"), ACT.Square,
                                   accum_out=ss[:, 0, ds(n, 1)]).then_inc(squared, 1)
            act.wait_ge(squared, NB + 1)
            act.activation(ss[:, 1, :], ss[:, 0, :], ACT.Ln, bias=eps[:, 0:1], scale=1.0 / D).then_inc(squared, 1)
            act.wait_ge(squared, NB + 2)
            act.activation(ss[:, 2, :], ss[:, 1, :], ACT.Exp, scale=-0.5).then_inc(rstd_made, 1)
            act.wait_ge(act_rows, 1)
            act.activation(g4b[:, :, :], g4b[:, :, :], ACT.Exp).then_inc(act_rows, 1)
            act.wait_ge(act_rows, 3)
            act.activation(sm[:, 6, :], sm[:, 6, :], ACT.Exp).then_inc(act_rows, 1)

        @block.vector
        def _(dve):
            n = 0

            def then(ins):
                nonlocal n
                n += 1
                ins.then_inc(rows, 1)
                dve.wait_ge(rows, n)

            def over(ap, m):
                return ap.unsqueeze(2).to_broadcast([P, NB, m])

            def along(ap, m):
                return ap.unsqueeze(1).to_broadcast([P, NB, m])
            dve.sem_inc(squared, 1)
            then(dve.memset(tf[:, :], 0.0))
            dve.wait_ge(w_in, 80)
            for k in range(KD):
                dve.tensor_scalar(wr[:, k, :], wr[:, k, :], vec[:, gn + k:gn + k + 1], None, ALU.mult).then_inc(gw, 1)
            dve.wait_ge(rstd_made, 1)
            dve.wait_ge(x_kept, ready(NB - 1))
            dve.wait_ge(lmm, ready(NB - 1))
            then(dve.tensor_tensor(lg[:, :, :], bank[4][:, 0:NB * ROUTER].rearrange("p (b n) -> p b n", n=ROUTER), over(ss[:, 2, :], ROUTER), ALU.mult))
            then(dve.tensor_tensor(lg[:, :, :], lg[:, :, :], along(br[:, :], ROUTER), ALU.add))
            dve.wait_ge(iotas, 3)
            then(dve.tensor_reduce(sm[:, 0, :], lg[:, :, 0:NG], AX.X, ALU.max))
            dve.tensor_tensor(g4b[:, :, :], lg[:, :, 0:NG], over(sm[:, 0, :], NG), ALU.subtract).then_inc(act_rows, 1)
            then(dve.tensor_tensor(g4[:, :, :], lg[:, :, 0:NG], over(sm[:, 0, :], NG), ALU.is_equal))
            then(dve.scalar_tensor_tensor(g4[:, :, :], g4[:, :, :], -BIG, along(iota[:, 0:NG], NG), ALU.mult, ALU.add))
            then(dve.tensor_reduce(sm[:, 1, :], g4[:, :, :], AX.X, ALU.min))
            then(dve.tensor_scalar(sm[:, 1, :], sm[:, 1, :], BIG, None, ALU.add))
            then(dve.tensor_tensor(g4[:, :, :], over(sm[:, 1, :], NG), along(iota[:, 0:NG], NG), ALU.is_equal))
            then(dve.tensor_scalar(g4[:, :, :], g4[:, :, :], -NEG, NEG, ALU.mult, ALU.add))
            for g in range(NG):
                then(dve.tensor_tensor(em[:, :, g * EPG:(g + 1) * EPG], lg[:, :, NG + g * EPG:NG + (g + 1) * EPG],
                                       g4[:, :, g:g + 1].to_broadcast([P, NB, EPG]), ALU.add))
            for j, (src, oh) in enumerate(((em, oh1), (em2, oh2))):
                then(dve.tensor_reduce(sm[:, 2 + j, :], src[:, :, :], AX.X, ALU.max))
                then(dve.tensor_tensor(tt[:, :, :], src[:, :, :], over(sm[:, 2 + j, :], NE), ALU.is_equal))
                then(dve.scalar_tensor_tensor(tt[:, :, :], tt[:, :, :], -BIG, along(iota[:, :], NE), ALU.mult, ALU.add))
                then(dve.tensor_reduce(sm[:, 4, :], tt[:, :, :], AX.X, ALU.min))
                then(dve.tensor_scalar(sm[:, 4, :], sm[:, 4, :], BIG, None, ALU.add))
                then(dve.tensor_tensor(oh[:, :, :], over(sm[:, 4, :], NE), along(iota[:, :], NE), ALU.is_equal))
                if j == 0:
                    then(dve.scalar_tensor_tensor(em2[:, :, :], oh[:, :, :], 2 * NEG, em[:, :, :], ALU.mult, ALU.add))
            dve.wait_ge(act_rows, 2)
            dve.tensor_tensor(sm[:, 6, :], sm[:, 3, :], sm[:, 2, :], ALU.subtract).then_inc(act_rows, 1)
            then(dve.tensor_reduce(sm[:, 5, :], g4b[:, :, :], AX.X, ALU.add))
            dve.wait_ge(act_rows, 4)
            then(dve.tensor_scalar(sm[:, 7, :], sm[:, 6, :], 1.0, None, ALU.add))
            then(dve.tensor_tensor(sm[:, 7, :], sm[:, 7, :], sm[:, 5, :], ALU.mult))
            then(dve.reciprocal(gates[:, 0:NB], sm[:, 7, :]))
            then(dve.tensor_tensor(gates[:, NB:2 * NB], gates[:, 0:NB], sm[:, 6, :], ALU.mult))
            then(dve.tensor_tensor(both[:, 0:NB, :], oh1[:, :, :], oh2[:, :, :], ALU.add))
            then(dve.memset(before[:, 0, :], 0.0))
            for b in range(1, NB):
                then(dve.tensor_tensor(before[:, b, :], before[:, b - 1, :], both[:, b - 1, :], ALU.add))
            dve.tensor_tensor(both[:, NB, :], before[:, NB - 1, :], both[:, NB - 1, :], ALU.add).then_inc(rmm, 1)
            dve.wait_ge(cnt, 2)
            then(dve.tensor_copy(ex[:, 0, :], bank[6][:, 0:NE]))
            then(dve.tensor_scalar(ex[:, 1, :], ex[:, 0, :], 0.0, None, ALU.is_gt))
            for j in range(1, SEQ // P):
                then(dve.scalar_tensor_tensor(ex[:, 1, :], ex[:, 0, :], float(j * P), ex[:, 1, :], ALU.is_gt, ALU.add))
            then(dve.tensor_tensor_scan(ex[:, 2, :], ones[:, 0:NE], ex[:, 1, :], 0.0, ALU.mult, ALU.add))
            then(dve.tensor_tensor(ex[:, 3, :], ex[:, 2, :], ex[:, 1, :], ALU.subtract))
            then(dve.tensor_scalar(ex[:, 4, :], ex[:, 3, :], float(P), None, ALU.mult))
            then(dve.tensor_tensor(rank[:, :, :], bank[5][:, 0:NB * NE].rearrange("p (b n) -> p b n", n=NE), along(ex[:, 4, :], NE), ALU.add))
            for j, oh in enumerate((oh1, oh2)):
                then(dve.tensor_tensor(tt[:, :, :], oh[:, :, :], rank[:, :, :], ALU.mult))
                then(dve.tensor_reduce(sf[:, j, :], tt[:, :, :], AX.X, ALU.add))
            dve.tensor_copy(slots[:, :], sf[:, :, :].rearrange("p j b -> p (j b)")).then_inc(slots_made, 1)
            for b in range(NB):
                if b >= 2:
                    dve.wait_ge(stored[b % 2], 16 * (b // 2))
                dve.scalar_tensor_tensor(xn[:, b % 2, :], xt[:, b, :], ss[:, 2, b:b + 1], gain[:, :], ALU.mult, ALU.mult).then_inc(xn_made, 1)
            then(dve.tensor_tensor(big[0:1, :, :], stepf[0:1, :].unsqueeze(2).to_broadcast([1, MAXB, NE]), ex[0:1, 2, :].unsqueeze(1).to_broadcast([1, MAXB, NE]), ALU.is_ge))
            then(dve.tensor_reduce(tf[:, 0:MAXB], big[0:1, :, :], AX.X, ALU.add))
            then(dve.tensor_scalar(tf[:, 0:MAXB], tf[:, 0:MAXB], float(NE - 1), None, ALU.min))
            then(dve.tensor_scalar(big[0:1, 0:MAXB // 2, 0], stepf[0:1, 0:MAXB // 2], 2.0, None, ALU.mult))
            then(dve.tensor_scalar(big[0:1, 0:MAXB // 2, 1], big[0:1, 0:MAXB // 2, 0], ex[0:1, 2, NE - 1:NE], None, ALU.is_lt))
            then(dve.tensor_reduce(tf[:, PAIRS:PAIRS + 1], big[0:1, 0:MAXB // 2, 1], AX.X, ALU.add))
            dve.tensor_copy(table[:, :], tf[:, :])
            then(dve.memset(assigned[:, MAXB:MAXB + 2], 0))
            dve.wait_ge(list_in, 16)
            dve.tensor_copy(listf[:, :], lists[:, :]).then_inc(list_float, 1)
            dve.wait_ge(list_turned, 1)
            then(dve.tensor_copy(assigned[:, 0:MAXB], bank[7][:, 0:MAXB]))
            then(dve.tensor_scalar(token[:, :], assigned[:, :], SEQ - 1, None, ALU.bitwise_and))


def stage_experts(nc, ctx, A, K, bank, assigned, token, table, xn_d, y_d):
    (g0, g1, turned, x_hi, x_lo, used, hi_made, lo_made, silu_made, hb_made, hturned, h_hi, h_lo,
     y_kept_a, y_kept_b, s0, s1, index_made, waited, ended, y_stored) = sems(
        ctx, nc, "k", "g0 g1 turned x_hi x_lo used hi_made lo_made silu_made hb_made hturned h_hi h_lo "
        "y_kept_a y_kept_b s0 s1 index_made waited ended y_stored")
    PIECES, RAW, SPLIT = 6, 6, 3
    pieces_in = sems(ctx, nc, "k", " ".join(f"piece_in{r}" for r in range(RAW)))
    gathered, stored = (g0, g1), (s0, s1)
    ident = K["ident"]
    w_gate = A["w_e_gate_2"][0].rearrange("e (k p) n -> e p k n", p=P)
    w_up = A["w_e_up_2"][0].rearrange("e (k p) n -> e p k n", p=P)
    w_down = A["w_e_down_2"][0].rearrange("e (k p) n -> e p k n", p=P)
    with ExitStack() as inner:
        raw = buffer(inner, nc, "k_raw", [P, RAW, KE, BANK])
        wh = buffer(inner, nc, "k_w_hi", [P, SPLIT, KE, BANK], F32R)
        wl = buffer(inner, nc, "k_w_lo", [P, SPLIT, KE, BANK], F32R)
        from_ = buffer(inner, nc, "k_from", [P, 2], I32)
        to = buffer(inner, nc, "k_to", [P, 2], I32)
        xg = buffer(inner, nc, "k_rows", [P, 2, D])
        xh = buffer(inner, nc, "k_x_hi", [P, KD, P], F32R)
        xl = buffer(inner, nc, "k_x_lo", [P, KD, P], F32R)
        sg = buffer(inner, nc, "k_silu", [P, BANK])
        hb = buffer(inner, nc, "k_h", [P, BANK])
        hh = buffer(inner, nc, "k_h_hi", [P, KE, P], F32R)
        hl = buffer(inner, nc, "k_h_lo", [P, KE, P], F32R)
        y = buffer(inner, nc, "k_y", [P, 2, D])
        block = inner.enter_context(nc.Block())

        def tiles(ap):
            return ap.rearrange("p (k t) -> p k t", t=P)

        def source(e, j):
            if j < 4:
                w, k, c = (w_gate, w_up)[j // 2], KE * (j % 2), 0
            else:
                w, k, c = w_down, 0, BANK * (j - 4)
            return w[ds(e, 1), :, k:k + KE, c:c + BANK].rearrange("a p k n -> (a p) k n")

        @block.sync
        def _(sp):
            pairs = sp.value_load(table[0:1, PAIRS:PAIRS + 1], min_val=1, max_val=MAXB // 2)

            def load(n, r, e, j):
                sp.wait_ge(lo_made, n + 1)
                sp.dma_start(raw[:, r, :, :], source(e, j)).then_inc(pieces_in[r], 16)
            with sp.Fori(0, pairs) as i:
                for s in range(2):
                    e = sp.value_load(table[0:1, ds(2 * i + s, 1)], min_val=0, max_val=NE - 1)
                    for j in range(PIECES):
                        load(2 * PIECES * i + PIECES * s + j, (PIECES * s + j) % RAW, e, j)
            for j in range(2):
                load(2 * PIECES * pairs + j, j, 0, j)

        @block.gpsimd
        def _(pool):
            pool.sem_inc(y_stored, 2)
            pairs = pool.value_load(table[0:1, PAIRS:PAIRS + 1], min_val=1, max_val=MAXB // 2)

            def gather(g, b, s):
                pool.wait_ge(turned, b + 1)
                pool.tensor_copy(from_[:, s:s + 1], token[:, ds(b, 1)]).then_inc(index_made, 1)
                pool.wait_ge(index_made, g)
                pool.sem_inc(waited, 1)
                pool.wait_ge(waited, 1)
                pool.indirect_dma_start(out=xg[:, s, :], out_offset=None, in_=xn_d,
                                        in_offset=bass.IndirectOffsetOnAxis(ap=from_[:, s:s + 1], axis=0)).then_inc(gathered[s], 16)

            def scatter(g, b, s):
                pool.tensor_copy(to[:, s:s + 1], assigned[:, ds(b, 1)]).then_inc(index_made, 1)
                pool.wait_ge(index_made, g)
                pool.wait_ge(y_kept_a, b + 2)
                pool.wait_ge(y_kept_b, b + 2)
                pool.sem_inc(waited, 1)
                pool.wait_ge(waited, 1)
                pool.indirect_dma_start(out=y_d, out_offset=bass.IndirectOffsetOnAxis(ap=to[:, s:s + 1], axis=0),
                                        in_=y[:, s, :], in_offset=None).then_inc(stored[s], 16)

            def end(i, s):
                pool.wait_ge(stored[s], 16 * i + 16)
                pool.sem_inc(y_stored, 1)
            gather(1, 0, 0)
            gather(2, 1, 1)
            with pool.Fori(0, pairs) as i:
                for s in range(2):
                    gather(4 * i + 2 * s + 3, 2 * i + s + 2, s)
                    scatter(4 * i + 2 * s + 4, 2 * i + s, s)
                    end(i, s)
            pool.wait_ge(gathered[0], 16 * pairs + 16)
            pool.sem_inc(ended, 1)
            pool.wait_ge(gathered[1], 16 * pairs + 16)
            pool.sem_inc(ended, 1)
            pool.wait_ge(ended, 2)

        @block.tensor
        def _(pe):
            pe.sem_inc(turned, 2)
            pe.sem_inc(used, SPLIT)
            pairs = pe.value_load(table[0:1, PAIRS:PAIRS + 1], min_val=1, max_val=MAXB // 2)

            def rows(n_in, s):
                pe.wait_ge(gathered[s], 16 * n_in)
                for k in range(KD):
                    m = pe.transpose(bank[k // 4][:, (k % 4) * P:(k % 4 + 1) * P], xg[:, s, k * P:(k + 1) * P], ident[:, :])
                m.then_inc(turned, 1)

            def piece(n, r, x, out, first, last):
                pe.wait_ge(lo_made, n + RAW + 1)
                hi, lo = x
                for k in range(KE):
                    pe.matmul(out, hi[:, k, :], wh[:, r, k, :], start=first and k == 0, stop=False)
                    pe.matmul(out, hi[:, k, :], wl[:, r, k, :], start=False, stop=False)
                    m = pe.matmul(out, lo[:, k, :], wh[:, r, k, :], start=False, stop=last and k == KE - 1)
                m.then_inc(used, 1)
            rows(1, 0)
            with pe.Fori(0, pairs) as i:
                for s in range(2):
                    b, n = 2 * i + s, 2 * PIECES * i + PIECES * s
                    pe.wait_ge(x_lo, 2 * b + 2)
                    for j in range(4):
                        half = j % 2
                        x = (xh[:, KE * half:KE * half + KE, :], xl[:, KE * half:KE * half + KE, :])
                        piece(n + j, (PIECES * s + j) % SPLIT, x, bank[2 + j // 2][:, :], half == 0, half == 1)
                    rows(i + 1 + s, 1 - s)
                    pe.wait_ge(hb_made, b + 1)
                    for k in range(KE):
                        m = pe.transpose(bank[4][:, k * P:(k + 1) * P], hb[:, k * P:(k + 1) * P], ident[:, :])
                    m.then_inc(hturned, 1)
                    pe.wait_ge(h_lo, b + 1)
                    pe.wait_ge(y_kept_a, b + 1)
                    piece(n + 4, (PIECES * s + 4) % SPLIT, (hh, hl), bank[5][:, :], True, True)
                    pe.wait_ge(y_kept_b, b + 1)
                    piece(n + 5, (PIECES * s + 5) % SPLIT, (hh, hl), bank[6][:, :], True, True)

        @block.scalar
        def _(act):
            act.sem_inc(y_kept_a, 1)
            pairs = act.value_load(table[0:1, PAIRS:PAIRS + 1], min_val=1, max_val=MAXB // 2)

            def high(n, r, q, n_in):
                act.wait_ge(pieces_in[r], 16 * n_in)
                act.wait_ge(used, n + 1)
                act.copy(wh[:, q, :, :], raw[:, r, :, :]).then_inc(hi_made, 1)

            def rows_high(b):
                act.wait_ge(turned, b + 3)
                for h in range(2):
                    act.copy(xh[:, KE * h:KE * h + KE, :], tiles(bank[h][:, :])).then_inc(x_hi, 1)
            high(0, 0, 0, 1)
            high(1, 1, 1, 1)
            rows_high(0)
            with act.Fori(0, pairs) as i:
                for s in range(2):
                    b, n = 2 * i + s, 2 * PIECES * i + PIECES * s

                    def piece(j):
                        high(n + j, j % RAW, j % SPLIT, 2 * i + s + 1 + j // RAW)
                    piece(2)
                    piece(3)
                    act.wait_ge(used, n + 5)
                    act.activation(sg[:, :], bank[2][:, :], ACT.Silu).then_inc(silu_made, 1)
                    piece(4)
                    piece(5)
                    rows_high(b + 1)
                    act.wait_ge(hturned, b + 1)
                    act.copy(hh[:, :, :], tiles(bank[4][:, :])).then_inc(h_hi, 1)
                    piece(6)
                    piece(7)
                    act.wait_ge(y_stored, b + 1)
                    act.wait_ge(used, n + 8)
                    act.copy(y[:, s, 0:BANK], bank[5][:, :]).then_inc(y_kept_a, 1)

        @block.vector
        def _(dve):
            dve.sem_inc(y_kept_b, 1)
            dve.sem_inc(lo_made, RAW)
            pairs = dve.value_load(table[0:1, PAIRS:PAIRS + 1], min_val=1, max_val=MAXB // 2)

            def low(n, r, q):
                dve.wait_ge(hi_made, n + 1)
                dve.tensor_tensor(wl[:, q, :, :], raw[:, r, :, :], wh[:, q, :, :], ALU.subtract).then_inc(lo_made, 1)

            def rows_low(b):
                for h in range(2):
                    dve.wait_ge(x_hi, 2 * b + h + 1)
                    half = slice(KE * h, KE * h + KE)
                    dve.tensor_tensor(xl[:, half, :], tiles(bank[h][:, :]), xh[:, half, :], ALU.subtract).then_inc(x_lo, 1)
            low(0, 0, 0)
            low(1, 1, 1)
            rows_low(0)
            with dve.Fori(0, pairs) as i:
                for s in range(2):
                    b, n = 2 * i + s, 2 * PIECES * i + PIECES * s

                    def piece(j):
                        low(n + j, j % RAW, j % SPLIT)
                    piece(2)
                    piece(3)
                    piece(4)
                    dve.wait_ge(silu_made, b + 1)
                    dve.wait_ge(used, n + 7)
                    dve.tensor_tensor(hb[:, :], sg[:, :], bank[3][:, :], ALU.mult).then_inc(hb_made, 1)
                    rows_low(b + 1)
                    dve.wait_ge(h_hi, b + 1)
                    dve.tensor_tensor(hl[:, :, :], tiles(bank[4][:, :]), hh[:, :, :], ALU.subtract).then_inc(h_lo, 1)
                    piece(5)
                    piece(6)
                    piece(7)
                    dve.wait_ge(y_stored, b + 1)
                    dve.wait_ge(used, n + 9)
                    dve.tensor_copy(y[:, s, BANK:D], bank[6][:, :]).then_inc(y_kept_b, 1)


def stage_finish(nc, ctx, A, K, bank, xt, gates, y_d, out):
    a0, a1, b0, b1, gain_in, first, mixed, squared, normed, stored = sems(ctx, nc, "o2", "a0 a1 b0 b1 gain_in first mixed squared normed stored")
    ga, gb = (a0, a1), (b0, b1)
    eps = K["eps"]
    with ExitStack() as inner:
        ya = buffer(inner, nc, "ya", [P, 2, D])
        yb = buffer(inner, nc, "yb", [P, 2, D])
        sq = buffer(inner, nc, "y_sq", [P, D])
        gain = buffer(inner, nc, "y_gain", [P, D])
        ss = buffer(inner, nc, "y_ss", [P, 3, NB])
        block = inner.enter_context(nc.Block())

        @block.sync
        def _(sp):
            sp.dma_start(gain[:, :], A["norm_final_2"].rearrange("(a d) -> a d", a=1).to_broadcast([P, D])).then_inc(gain_in, 16)
            for b in range(NB + 2):
                if b < NB:
                    if b >= 2:
                        sp.wait_ge(mixed, b - 1)
                    for j, (buf, sem) in enumerate(((ya, ga), (yb, gb))):
                        sp.dma_start(buf[:, b % 2, :], y_d[j * SEQ + b * P:j * SEQ + (b + 1) * P, :]).then_inc(sem[b % 2], 16)
                if b >= 2:
                    sp.wait_ge(normed, b - 1)
                    sp.dma_start(out[0, (b - 2) * P:(b - 1) * P, :], xt[:, b - 2, :]).then_inc(stored, 16)
            sp.wait_ge(stored, 16 * NB)

        @block.vector
        def _(dve):
            def norm(b):
                dve.wait_ge(squared, 3 * b + 3)
                if b == 0:
                    dve.wait_ge(gain_in, 16)
                dve.scalar_tensor_tensor(xt[:, b, :], xt[:, b, :], ss[:, 2, b:b + 1], gain[:, :], ALU.mult, ALU.mult).then_inc(normed, 1)
            for b in range(NB):
                dve.wait_ge(ga[b % 2], 16 * (b // 2 + 1))
                dve.scalar_tensor_tensor(xt[:, b, :], ya[:, b % 2, :], gates[:, b:b + 1], xt[:, b, :], ALU.mult, ALU.add).then_inc(first, 1)
                dve.wait_ge(gb[b % 2], 16 * (b // 2 + 1))
                dve.wait_ge(first, b + 1)
                dve.scalar_tensor_tensor(xt[:, b, :], yb[:, b % 2, :], gates[:, NB + b:NB + b + 1], xt[:, b, :], ALU.mult, ALU.add).then_inc(mixed, 1)
                if b:
                    norm(b - 1)
            norm(NB - 1)

        @block.scalar
        def _(act):
            for b in range(NB):
                act.wait_ge(mixed, b + 1)
                if b:
                    act.wait_ge(squared, 3 * b)
                act.activation(sq[:, :], xt[:, b, :], ACT.Square, accum_out=ss[:, 0, b:b + 1]).then_inc(squared, 1)
                act.wait_ge(squared, 3 * b + 1)
                act.activation(ss[:, 1, b:b + 1], ss[:, 0, b:b + 1], ACT.Ln, bias=eps[:, 0:1], scale=1.0 / D).then_inc(squared, 1)
                act.wait_ge(squared, 3 * b + 2)
                act.activation(ss[:, 2, b:b + 1], ss[:, 1, b:b + 1], ACT.Exp, scale=-0.5).then_inc(squared, 1)




def end_part(nc, before):
    nc.clear_and_free_semaphores(nc.allocated_since(before))
    nc.all_engine_barrier()


def program(nc, A, out):
    h0_d = nc.dram_tensor("h0_scratch", [P, KD, WIDE], F32).ap()
    h1_d = nc.dram_tensor("h1_scratch", [P, KD, LIVE], F32).ap()
    h2_d = nc.dram_tensor("h2_scratch", [P, KD, SEQ], F32).ap()
    xn_d = nc.dram_tensor("xn_scratch", [SEQ, D], F32).ap()
    list_d = nc.dram_tensor("slot_assignments", [MAXB * P, 1], I32).ap()
    y_d = nc.dram_tensor("y_scratch", [2 * SEQ + P, D], F32).ap()
    with ExitStack() as ctx:
        K = constants(ctx, nc)
        bank = [ctx.enter_context(nc.psum_tensor(f"bank{j}", [P, BANK], F32)) for j in range(8)]
        before = nc.snapshot_sems()
        stage_constants(nc, ctx, A, K, bank)
        with ExitStack() as first:
            z_flat = buffer(first, nc, "z", [P, KD * LIVE], side="right")
            z = z_flat[:, :].rearrange("p (k t) -> p k t", k=KD)
            v = z_flat[:, 0:CHUNKS * BANK].rearrange("p (c n) -> p c n", c=CHUNKS)
            with ExitStack() as mixers:
                o = buffer(mixers, nc, "o", [P, HALF, WIDE])
                with ExitStack() as inputs:
                    u = buffer(inputs, nc, "u", [P, KD, WIDE], side="right")
                    with ExitStack() as tokens:
                        h0 = buffer(tokens, nc, "h0", [P, KD, WIDE])
                        stage_load(nc, ctx, A, K, bank, h0, u, h0_d)
                    with ExitStack() as recurrence:
                        q = buffer(recurrence, nc, "q", [P, HALF, WIDE])
                        k = buffer(recurrence, nc, "k", [P, HALF, WIDE])
                        lf = buffer(recurrence, nc, "lf", [P, HALF, WIDE])
                        stage_hgrn_in(nc, ctx, A, K, bank, u, q, k, lf, v)
                        stage_hgrn(nc, ctx, A, K, bank, q, k, lf, v, o, z_flat[:, CHUNKS * BANK:])
                    p = buffer(mixers, nc, "p", [P, HALF, LIVE])
                    stage_branches(nc, ctx, A, K, bank, u, o, p)
                    u_pair = tuple(buffer(mixers, nc, n, [P, KD, LIVE], F32R) for n in ("u_gates_hi", "u_gates_lo"))
                    stage_split(nc, ctx, "us", u[:, :, FIRST:], u_pair)
                stage_mix(nc, ctx, A, K, bank, u_pair, o, p, z)
            post = ExitStack()
            y = buffer(post, nc, "mixed", [P, KD, LIVE])
            h1 = buffer(post, nc, "h1", [P, KD, LIVE])
            acc = buffer(post, nc, "mixed_squares", [P, LIVE])
            stage_project(nc, ctx, A, K, bank, "wo1", A["w_out"][0], KD, z, y, acc, LIVES, h1, h0_d[:, :, FIRST:])
        pair = ExitStack()
        u_pair = tuple(buffer(pair, nc, n, [P, KD, LIVE], F32R, side="right") for n in ("u_ffn_hi", "u_ffn_lo"))
        with post:
            stage_add_norm(nc, ctx, A, K, bank, "n1", y, acc, h1, "mix_post", LIVES, h1_d, u_pair, "ffn_pre")
        post = ExitStack()
        with ExitStack() as ffn:
            hidden = buffer(ffn, nc, "hidden", [P, KF, SEQ])
            with pair:
                stage_ffn(nc, ctx, A, K, bank, u_pair, hidden)
            y = buffer(post, nc, "ffn_out", [P, KD, SEQ], side="right")
            h2 = buffer(post, nc, "h2", [P, KD, SEQ], side="right")
            acc = buffer(post, nc, "ffn_squares", [P, SEQ], side="right")
            stage_down(nc, ctx, A, K, bank, hidden, y, acc, h2, h1_d[:, :, TAPS - 1:])
        pair = ExitStack()
        u_pair = tuple(buffer(pair, nc, n, [P, KD, SEQ], F32R) for n in ("u_mix_hi", "u_mix_lo"))
        with post:
            stage_add_norm(nc, ctx, A, K, bank, "n2", y, acc, h2, "ffn_post", SEQS, h2_d, u_pair, "norm_mix2")
        end_part(nc, before)
        with ExitStack() as mixers:
            qk = buffer(mixers, nc, "qk", [P, KD, SEQ], side="right")
            vm = buffer(mixers, nc, "vm", [P, NB, BANK], side="right")
            og = buffer(mixers, nc, "og", [P, 4, SEQ], side="right")
            gi = buffer(mixers, nc, "gi", [ML_H, SEQ], side="right")
            gf = buffer(mixers, nc, "gf", [ML_H, SEQ], side="right")
            with ExitStack() as attention:
                qa = buffer(attention, nc, "qa", [P, 4, SEQ], side="right")
                ka = buffer(attention, nc, "ka", [P, WIDE], side="right")
                va = buffer(attention, nc, "va", [P, CHUNKS, P], side="right")
                with pair:
                    stage_in2(nc, ctx, A, K, bank, u_pair, qa, ka, va, qk, vm, og, gi, gf)
                state = buffer(ctx, nc, "state", [P, KD, SEQ])
                stage_attention(nc, ctx, A, K, bank, qa, ka, va, state, state[:, KD // 2:, :].rearrange("p k t -> p (k t)"))
            stage_mlstm(nc, ctx, A, K, bank, qk, vm, og, gi, gf, state)
        h = buffer(ctx, nc, "stream", [P, KD, SEQ], side="right")
        stage_residual(nc, ctx, A, K, bank, "wo2", A["w_out_2"][0], KD, state, h, state, "norm_cross", h_load=h2_d)
        with ExitStack() as cross:
            mk = buffer(cross, nc, "mk", [P, 4, MEM])
            mv = buffer(cross, nc, "mv", [P, MEM // P, BANK])
            co = buffer(cross, nc, "co", [P, 4, SEQ])
            stage_memory(nc, ctx, A, K, bank, mk, mv)
            with ExitStack() as attention:
                xq = buffer(attention, nc, "xq", [P, XH, SEQ])
                stage_cross_q(nc, ctx, A, K, bank, state, xq)
                stage_cross(nc, ctx, A, K, bank, xq, mk, mv, co)
            stage_residual(nc, ctx, A, K, bank, "wc", A["w_co_2"][0], 4, co, h)
        end_part(nc, before)
        gates = buffer(ctx, nc, "gates", [P, 2 * NB])
        assigned = buffer(ctx, nc, "assigned", [P, MAXB + 2], I32)
        token = buffer(ctx, nc, "token", [P, MAXB + 2], I32)
        table = buffer(ctx, nc, "table", [1, 64], I32)
        stage_route(nc, ctx, A, K, bank, h, state, gates, assigned, token, table, xn_d, list_d)
        stage_experts(nc, ctx, A, K, bank, assigned, token, table, xn_d, y_d)
        stage_finish(nc, ctx, A, K, bank, state, gates, y_d, out)


_INS = ["x", "meta_tokens", "mix_norm_pre", "mix_norm_post", "w_in", "hgrn_lower_bounds", "hgrn_out_norm", "w_branch_hgrn",
        "pool_proj", "pool_scale", "w_branch_pool", "w_out", "ffn_norm_pre", "ffn_norm_post", "ffn_w_gate", "ffn_w_up",
        "ffn_conv_w", "ffn_conv_b", "ffn_w_down", "mem_2", "norm_mix_2", "w_in_2", "b_gates_2", "conv_w_2", "conv_b_2",
        "att_sinks_2", "norm_att_out_2", "norm_ml_out_2", "w_out_2", "norm_cross_2", "norm_mem_2", "w_cq_2", "w_ckv_2",
        "w_co_2", "norm_ffn_2", "w_router_group_2", "b_router_group_2", "w_router_expert_2", "b_router_expert_2",
        "w_e_gate_2", "w_e_up_2", "w_e_down_2", "norm_final_2"]


def kernel(**inputs):
    import numpy as _np
    import concourse.bacc as _bacc
    from concourse import mybir as _mybir
    from concourse.bass_utils import run_bass_kernel_spmd as _run

    nc = _bacc.Bacc("TRN2", target_bir_lowering=False, num_devices=1)
    arrays, args = {}, {}
    for name in _INS:
        a = _np.ascontiguousarray(inputs[name])
        arrays[f"in_{name}_dram"] = a
        args[name] = nc.dram_tensor(f"in_{name}_dram", a.shape, _mybir.dt.from_np(a.dtype), kind="ExternalInput").ap()
    out = nc.dram_tensor("out_0_dram", (1, SEQ, D), F32, kind="ExternalOutput").ap()
    program(nc, args, out)
    r = _run(nc, [arrays], core_ids=[0])
    return r.results[0]["out_0_dram"]
```
